# Optimizing a Trainium2 kernel written in Bass

```python
import math
import jax, jax.numpy as jnp
from jax import lax
import numpy as np

D_MODEL = 1024
BATCH = 1
SEQ = 128
DEPTH = 2
DEC_BATCH = 1
DEC_SEQ = 512
PAST_LEN = 128

GRID_W = 64
N_BRANCH = 3
BR_W = 512
HY_W = 512
HY_ORDER = 2
HY_SHORT = 3
HY_BANDS = 16
HY_POS_DIM = 1 + 2 * HY_BANDS
HY_FFN = 64
DA_HEADS = 4
DA_HEAD_DIM = 64
DA_V_DIM = 2 * DA_HEAD_DIM
MLA_HEADS = 8
MLA_NOPE = 64
MLA_ROPE = 32
MLA_V = 64
MLA_Q_LORA = 384
MLA_KV_LORA = 256
ROPE_BASE = 10000.0
Q_BLOCK = 128
ALPHA = (2 * DEPTH) ** 0.25
BETA = (8 * DEPTH) ** -0.25
LN_EPS = 1e-5
RMS_EPS = 1e-6

IN_SIZES = (3 * HY_W,
            2 * DA_HEADS * DA_HEAD_DIM,
            2 * DA_HEADS * DA_HEAD_DIM,
            DA_HEADS * DA_V_DIM,
            MLA_Q_LORA,
            MLA_KV_LORA,
            MLA_ROPE,
            N_BRANCH * BR_W,
            N_BRANCH * D_MODEL)
IN_SPLITS = tuple(int(v) for v in np.cumsum(IN_SIZES)[:-1])
D_IN = int(sum(IN_SIZES))

kernel_name = 'hybrid_hyena_diffattn_mla_dit_step'

def layer_norm(x, g, b):
    xf = x.astype(jnp.float32)
    mu = jnp.mean(xf, axis=-1, keepdims=True)
    var = jnp.mean(jnp.square(xf - mu), axis=-1, keepdims=True)
    y = (xf - mu) * lax.rsqrt(var + LN_EPS) * g.astype(jnp.float32) + b.astype(jnp.float32)
    return y.astype(x.dtype)

def rms_norm(x, g):
    xf = x.astype(jnp.float32)
    y = xf * lax.rsqrt(jnp.mean(jnp.square(xf), axis=-1, keepdims=True) + RMS_EPS)
    return (y * g.astype(jnp.float32)).astype(x.dtype)

def grid_positions(n_tok):
    rows = n_tok // GRID_W
    row = jnp.repeat(jnp.arange(rows), GRID_W)
    col = jnp.tile(jnp.arange(GRID_W), rows)
    return row, col

def rope_1d(x, pos, n_mid):
    half = x.shape[-1] // 2
    freqs = 1.0 / (ROPE_BASE ** (jnp.arange(half, dtype=jnp.float32) / half))
    ang = pos.astype(jnp.float32)[:, None] * freqs
    ang = ang.reshape((ang.shape[0],) + (1,) * n_mid + (half,))
    cos = jnp.cos(ang).astype(x.dtype)
    sin = jnp.sin(ang).astype(x.dtype)
    x1, x2 = x[..., :half], x[..., half:]
    return jnp.concatenate([x1 * cos - x2 * sin, x1 * sin + x2 * cos], axis=-1)

def axial_rope(x, row, col, n_mid):
    d = x.shape[-1]
    return jnp.concatenate([rope_1d(x[..., :d // 2], row, n_mid),
                            rope_1d(x[..., d // 2:], col, n_mid)], axis=-1)

def short_conv(u, w, b):
    up = jnp.pad(u, ((0, 0), (1, 1), (0, 0)))
    return up[:, :-2] * w[0] + up[:, 1:-1] * w[1] + up[:, 2:] * w[2] + b

def hyena_filters(n_tok, w1, b1, w2, b2, w3, sin_freq, log_decay):
    t = jnp.arange(n_tok, dtype=jnp.float32)
    t_lin = t / (n_tok - 1)
    bands = jnp.arange(1, HY_BANDS + 1, dtype=jnp.float32)
    ang = (2.0 * math.pi / n_tok) * t[:, None] * bands
    feats = jnp.concatenate([t_lin[:, None], jnp.cos(ang), -jnp.sin(ang)], axis=-1)
    f32 = lambda a: a.astype(jnp.float32)
    sf = f32(sin_freq)
    hid = jnp.sin(sf[0] * (feats @ f32(w1) + f32(b1)))
    hid = jnp.sin(sf[1] * (hid @ f32(w2) + f32(b2)))
    h = hid @ f32(w3)
    h = h * jnp.exp(-t_lin[:, None] * jnp.exp(f32(log_decay)))
    return h.reshape(n_tok, 2, HY_ORDER, HY_W)

def bidir_long_conv(z, h_fwd, h_bwd, skip):
    n_tok, ch = z.shape[1], z.shape[2]
    circ = jnp.concatenate([h_fwd, jnp.zeros((1, ch), jnp.float32),
                            jnp.flip(h_bwd[1:], axis=0)], axis=0)
    zf = jnp.fft.rfft(z.astype(jnp.float32), n=2 * n_tok, axis=1)
    cf = jnp.fft.rfft(circ, axis=0)
    y = jnp.fft.irfft(zf * cf[None], n=2 * n_tok, axis=1)[:, :n_tok]
    return (y + z.astype(jnp.float32) * skip.astype(jnp.float32)).astype(z.dtype)

def hyena(u, conv_w, conv_b, filt, skip):
    u = short_conv(u, conv_w, conv_b)
    v, x1, x2 = jnp.split(u, 3, axis=-1)
    z = v
    for n, gate in enumerate((x1, x2)):
        z = gate * bidir_long_conv(z, filt[:, 0, n], filt[:, 1, n], skip[n])
    return z

def _to_blocks(a):
    b, nb = a.shape[0], a.shape[1] // Q_BLOCK
    return jnp.moveaxis(a.reshape((b, nb, Q_BLOCK) + a.shape[2:]), 1, 0)

def _from_blocks(o):
    nb, b = o.shape[0], o.shape[1]
    return jnp.moveaxis(o, 0, 1).reshape((b, nb * o.shape[2]) + o.shape[3:])

def diff_attention(q, k, v, lam):
    scale = DA_HEAD_DIM ** -0.5

    def block(qb):
        s = jnp.einsum('bqjhd,bkjhd->bjhqk', qb, k, preferred_element_type=jnp.float32) * scale
        pr = jax.nn.softmax(s, axis=-1)
        pr = pr[:, 0] - lam * pr[:, 1]
        return jnp.einsum('bhqk,bkhe->bqhe', pr.astype(v.dtype), v)

    return _from_blocks(lax.map(block, _to_blocks(q)))

def mla_attention(q_nope, q_rope, k_nope, k_rope, v):
    scale = (MLA_NOPE + MLA_ROPE) ** -0.5

    def block(qs):
        qn, qr = qs
        s = (jnp.einsum('bqhd,bkhd->bhqk', qn, k_nope, preferred_element_type=jnp.float32)
             + jnp.einsum('bqhr,bkr->bhqk', qr, k_rope, preferred_element_type=jnp.float32)) * scale
        pr = jax.nn.softmax(s, axis=-1)
        return jnp.einsum('bhqk,bkhe->bqhe', pr.astype(v.dtype), v)

    return _from_blocks(lax.map(block, (_to_blocks(q_nope), _to_blocks(q_rope))))

def trunk_layer(x, mod, l, p, pos=None, ctx=None):
    b, n, _ = x.shape
    shift, scale, gate = jnp.split(mod, 3, axis=-1)
    h = x * (1 + scale) + shift
    proj = h @ p['w_in'][l]
    hy_in, da_q, da_k, da_v, mla_dq, mla_dkv, mla_kr, paths, merge = jnp.split(proj, IN_SPLITS, axis=-1)

    filt = hyena_filters(n, p['hy_ffn_w1'][l], p['hy_ffn_b1'][l], p['hy_ffn_w2'][l],
                         p['hy_ffn_b2'][l], p['hy_ffn_w3'][l], p['hy_sin_freq'][l],
                         p['hy_log_decay'][l])
    y_hy = hyena(hy_in, p['hy_conv_w'][l], p['hy_conv_b'][l], filt, p['hy_skip'][l])

    q = da_q.reshape(b, n, 2, DA_HEADS, DA_HEAD_DIM)
    k = da_k.reshape(b, n, 2, DA_HEADS, DA_HEAD_DIM)
    v = da_v.reshape(b, n, DA_HEADS, DA_V_DIM)
    c_q = rms_norm(mla_dq, p['mla_q_norm'][l])
    qm = (c_q @ p['mla_w_uq'][l]).reshape(b, n, MLA_HEADS, MLA_NOPE + MLA_ROPE)
    q_nope, q_rope = qm[..., :MLA_NOPE], qm[..., MLA_NOPE:]
    c_kv = rms_norm(mla_dkv, p['mla_kv_norm'][l])

    if ctx is None:
        new_ctx = (k, v, c_kv, mla_kr)
        k_all, v_all, ckv_all, kr_all = k, v, c_kv, mla_kr
    else:
        row, col = pos
        q = axial_rope(q, row, col, 2)
        q_rope = axial_rope(q_rope, row, col, 1)
        ctx_k, ctx_v, ctx_ckv, ctx_kr = ctx
        k_all = jnp.concatenate([ctx_k, axial_rope(k, row, col, 2)], axis=1)
        v_all = jnp.concatenate([ctx_v, v], axis=1)
        ckv_all = jnp.concatenate([ctx_ckv, c_kv], axis=1)
        kr_all = jnp.concatenate([ctx_kr, axial_rope(mla_kr, row, col, 0)], axis=1)
        new_ctx = None

    lam_init = 0.8 - 0.6 * math.exp(-0.3 * l)
    lp = p['da_lambda'][l].astype(jnp.float32)
    lam = jnp.exp(jnp.sum(lp[0] * lp[1])) - jnp.exp(jnp.sum(lp[2] * lp[3])) + lam_init
    o = diff_attention(q, k_all, v_all, lam)
    y_da = (rms_norm(o, p['da_subln'][l]) * (1 - lam_init)).reshape(b, n, DA_HEADS * DA_V_DIM)

    kv = (ckv_all @ p['mla_w_ukv'][l]).reshape(b, -1, MLA_HEADS, MLA_NOPE + MLA_V)
    y_mla = mla_attention(q_nope, q_rope, kv[..., :MLA_NOPE], kr_all,
                          kv[..., MLA_NOPE:]).reshape(b, n, MLA_HEADS * MLA_V)

    br = jnp.stack([y_hy, y_da, y_mla], axis=2) * jax.nn.silu(paths.reshape(b, n, N_BRANCH, BR_W))
    y_br = jnp.einsum('blni,nid->blnd', br, p['w_branch'][l])
    merged = jnp.sum(jax.nn.sigmoid(merge.reshape(b, n, N_BRANCH, D_MODEL)) * y_br, axis=2)
    out = merged @ p['w_out'][l]
    x = layer_norm(ALPHA * x + gate * out, p['ln_g'][l], p['ln_b'][l])
    return x, new_ctx

def setup_inputs(seed: int = 0) -> dict:
    key = jax.random.key(seed)
    ks = jax.random.split(key, 40)
    f32 = jnp.float32
    nrm = lambda k, shape, s: jax.random.normal(k, shape, f32) * s
    decay0 = jnp.log(jnp.linspace(3.07, 15.35, 2 * HY_ORDER * HY_W, dtype=f32))
    return {
        'x_prompt': nrm(ks[0], (BATCH, SEQ, D_MODEL), 1.0),
        'x_sample': nrm(ks[1], (DEC_BATCH, DEC_SEQ, D_MODEL), 1.0),
        'c': nrm(ks[2], (DEC_BATCH, D_MODEL), 1.0),
        'cache_diff_k': nrm(ks[3], (DEC_BATCH, DEPTH, PAST_LEN, 2, DA_HEADS, DA_HEAD_DIM), 1.0),
        'cache_diff_v': nrm(ks[4], (DEC_BATCH, DEPTH, PAST_LEN, DA_HEADS, DA_V_DIM), 1.0),
        'cache_mla_ckv': nrm(ks[5], (DEC_BATCH, DEPTH, PAST_LEN, MLA_KV_LORA), 1.0),
        'cache_mla_krope': nrm(ks[6], (DEC_BATCH, DEPTH, PAST_LEN, MLA_ROPE), 1.0),
        'c_ctx': nrm(ks[7], (D_MODEL,), 1.0),
        'w_mod': nrm(ks[8], (DEPTH, D_MODEL, 3 * D_MODEL), D_MODEL ** -0.5),
        'b_mod': nrm(ks[9], (DEPTH, 3 * D_MODEL), 0.02),
        'w_in': nrm(ks[10], (DEPTH, D_MODEL, D_IN), D_MODEL ** -0.5),
        'hy_conv_w': nrm(ks[11], (DEPTH, HY_SHORT, 3 * HY_W), HY_SHORT ** -0.5),
        'hy_conv_b': nrm(ks[12], (DEPTH, 3 * HY_W), 0.02),
        'hy_ffn_w1': nrm(ks[13], (DEPTH, HY_POS_DIM, HY_FFN), HY_POS_DIM ** -0.5),
        'hy_ffn_b1': nrm(ks[14], (DEPTH, HY_FFN), 0.1),
        'hy_ffn_w2': nrm(ks[15], (DEPTH, HY_FFN, HY_FFN), HY_FFN ** -0.5),
        'hy_ffn_b2': nrm(ks[16], (DEPTH, HY_FFN), 0.1),
        'hy_ffn_w3': nrm(ks[17], (DEPTH, HY_FFN, 2 * HY_ORDER * HY_W), 0.1 * HY_FFN ** -0.5),
        'hy_sin_freq': 1.0 + nrm(ks[18], (DEPTH, 2, HY_FFN), 0.05),
        'hy_log_decay': decay0[None, :] + nrm(ks[19], (DEPTH, 2 * HY_ORDER * HY_W), 0.05),
        'hy_skip': nrm(ks[20], (DEPTH, HY_ORDER, HY_W), 1.0),
        'da_lambda': nrm(ks[21], (DEPTH, 4, DA_HEAD_DIM), 0.1),
        'da_subln': 1.0 + nrm(ks[22], (DEPTH, DA_V_DIM), 0.02),
        'mla_q_norm': 1.0 + nrm(ks[23], (DEPTH, MLA_Q_LORA), 0.02),
        'mla_w_uq': nrm(ks[24], (DEPTH, MLA_Q_LORA, MLA_HEADS * (MLA_NOPE + MLA_ROPE)), MLA_Q_LORA ** -0.5),
        'mla_kv_norm': 1.0 + nrm(ks[25], (DEPTH, MLA_KV_LORA), 0.02),
        'mla_w_ukv': nrm(ks[26], (DEPTH, MLA_KV_LORA, MLA_HEADS * (MLA_NOPE + MLA_V)), MLA_KV_LORA ** -0.5),
        'w_branch': nrm(ks[27], (DEPTH, N_BRANCH, BR_W, D_MODEL), BETA * BR_W ** -0.5),
        'w_out': nrm(ks[28], (DEPTH, D_MODEL, D_MODEL), BETA * D_MODEL ** -0.5),
        'ln_g': 1.0 + nrm(ks[29], (DEPTH, D_MODEL), 0.02),
        'ln_b': nrm(ks[30], (DEPTH, D_MODEL), 0.02),
    }

def reference(x_prompt, x_sample, c, cache_diff_k, cache_diff_v, cache_mla_ckv, cache_mla_krope,
              c_ctx, w_mod, b_mod, w_in, hy_conv_w, hy_conv_b, hy_ffn_w1, hy_ffn_b1, hy_ffn_w2,
              hy_ffn_b2, hy_ffn_w3, hy_sin_freq, hy_log_decay, hy_skip, da_lambda, da_subln,
              mla_q_norm, mla_w_uq, mla_kv_norm, mla_w_ukv, w_branch, w_out, ln_g, ln_b):
    p = {'w_in': w_in, 'hy_conv_w': hy_conv_w, 'hy_conv_b': hy_conv_b,
         'hy_ffn_w1': hy_ffn_w1, 'hy_ffn_b1': hy_ffn_b1, 'hy_ffn_w2': hy_ffn_w2,
         'hy_ffn_b2': hy_ffn_b2, 'hy_ffn_w3': hy_ffn_w3, 'hy_sin_freq': hy_sin_freq,
         'hy_log_decay': hy_log_decay, 'hy_skip': hy_skip, 'da_lambda': da_lambda,
         'da_subln': da_subln, 'mla_q_norm': mla_q_norm, 'mla_w_uq': mla_w_uq,
         'mla_kv_norm': mla_kv_norm, 'mla_w_ukv': mla_w_ukv, 'w_branch': w_branch,
         'w_out': w_out, 'ln_g': ln_g, 'ln_b': ln_b}

    xp = x_prompt
    ks_l, vs_l, ckv_l, kr_l = [], [], [], []
    for l in range(DEPTH):
        mod = (jax.nn.silu(c_ctx) @ w_mod[l] + b_mod[l])[None, None, :]
        xp, (k_c, v_c, ckv_c, kr_c) = trunk_layer(xp, mod, l, p)
        ks_l.append(k_c)
        vs_l.append(v_c)
        ckv_l.append(ckv_c)
        kr_l.append(kr_c)
    state_diff_k = jnp.stack(ks_l, axis=1)
    state_diff_v = jnp.stack(vs_l, axis=1)
    state_mla_ckv = jnp.stack(ckv_l, axis=1)
    state_mla_krope = jnp.stack(kr_l, axis=1)

    pos = grid_positions(x_sample.shape[1])
    xs = x_sample
    for l in range(DEPTH):
        mod = (jax.nn.silu(c) @ w_mod[l] + b_mod[l])[:, None, :]
        ctx = (cache_diff_k[:, l], cache_diff_v[:, l], cache_mla_ckv[:, l], cache_mla_krope[:, l])
        xs, _ = trunk_layer(xs, mod, l, p, pos=pos, ctx=ctx)

    return (xp, xs, state_diff_k, state_diff_v, state_mla_ckv, state_mla_krope)


_drawn_inputs = setup_inputs


def setup_inputs(seed=0):
    import zlib

    import numpy as np

    out = dict(_drawn_inputs(seed))
    spreads = {}
    factors = {'cache_diff_k': 6.327,
     'cache_diff_v': 6.122,
     'cache_mla_ckv': 8.0,
     'cache_mla_krope': 8.0,
     'hy_conv_b': 7.087,
     'hy_sin_freq': 4.204,
     'da_lambda': 8.0,
     'da_subln': 8.0,
     'mla_q_norm': 8.0,
     'mla_w_uq': 7.983,
     'mla_kv_norm': 2.818}
    for name, (base, spread) in spreads.items():
        noise = np.random.default_rng([zlib.crc32(name.encode()), seed]).standard_normal(out[name].shape)
        drawn = base * np.exp(spread * noise) if base else spread * noise
        out[name] = __import__('jax').numpy.asarray(drawn.astype(out[name].dtype))
    for name, factor in factors.items():
        out[name] = (out[name] * factor).astype(out[name].dtype)
    return out
```

```python
import math
from contextlib import ExitStack

import numpy as np

import concourse.bass as bass
from concourse import mybir

DEPTH, D, LAT, CTX, PAST = 2, 1024, 512, 128, 128
NTOK = LAT + CTX
HALF = NTOK // 2
KD = D // 128
NT = NTOK // 128
HY, HY_FFN, POS = 512, 64, 33
CT = HY // 128
GRID_W = 64
DAH, DHD, DAV = 4, 64, 128
MH, MN, MR, MV = 8, 64, 32, 64
QL, KVL = 384, 256
NKEY = PAST + NTOK
LKEY = PAST + LAT
ALPHA = (2 * DEPTH) ** 0.25
LN_EPS, RMS_EPS = 1e-5, 1e-6
DA_SCALE = DHD ** -0.5
MLA_SCALE = (MN + MR) ** -0.5
T_HY, T_Q, T_K, T_V, T_DQ, T_DKV, T_KR, T_PATH, T_MERGE = 0, 12, 16, 20, 24, 27, 29, 30, 42
C_KR = 3 * HY + 3 * 512 + QL + KVL
C_PATH = C_KR + MR
D_IN = C_PATH + 3 * 512 + 3 * D
TWO_PI = 2 * math.pi
MAGIC = 1.5 * 2 ** 23
PI_HI, PI_MID = 6.28125, 0.0019350051879882812
PI_LO = TWO_PI - PI_HI - PI_MID
SLOTS = 4


VECS = [("b_mod", 3 * KD), ("hy_conv_w", 36), ("hy_conv_b", 12), ("hy_skip", 8), ("hy_ffn", 4), ("da_subln", 1),
        ("mla_q_norm", 3), ("mla_kv_norm", 2)]
NVEC = sum(n for _, n in VECS)


def vec(vecs, name):
    at = [n for n, _ in VECS].index(name)
    start = sum(n for _, n in VECS[:at])
    return vecs[:, start:start + VECS[at][1]]


def attention_steps(tag, heads, before=None):
    steps, units = [], [(h, t) for h in range(heads) for t in range(NT)]
    for u, (h, t) in enumerate(units):
        if before and t == 2 and h + 1 < heads:
            steps += before(h + 1)
        steps.append((tag + "_score", u))
        if u >= 2 and (u - 2) % NT == NT - 1:
            steps.append((tag + "_pv", (u - 2) // NT))
        if u >= 1:
            steps.append((tag + "_ptrans", u - 1))
    steps.append((tag + "_ptrans", len(units) - 1))
    steps.append((tag + "_pv", heads - 1))
    return steps


def path_steps(n):
    return [("path", 4 * n + c) for c in range(CT)] + [("merge", KD * n + d) for d in range(KD)]


def layer_steps():
    s = [("mod", 0)] + [("ht", f) for f in range(KD)]
    s += [("conv", c) for c in range(4)] + [("ffn", 0), ("ffn", 1)]
    for o in range(2):
        s += [("filt", NT * o + t) for t in range(NT)]
        s += [("fdft", 5 * o + i) for i in range(5)]
        s += [("zt", 3 * o + i) for i in range(3)]
        s += [("zdft", 5 * o + i) for i in range(5)]
        s += [("conv", 4 + 4 * o + c) for c in range(4)]
        s += [("inv", 4 * o + c) for c in range(4)]
    s += path_steps(0)
    s += [("qk", c) for c in range(8)] + [("kc", 0), ("sk", 0)]
    for c in range(4):
        s += [("v", c)]
        if c:
            s += [("vt", c - 1)]
    s += [("vt", 3)]
    s += attention_steps("da", DAH)
    s += [("dams", h) for h in range(DAH)]
    s += path_steps(1)
    s += [("dqkv", i) for i in range(5)] + [("kr", 0), ("cc", 0), ("mms", 0), ("mms", 1), ("sc", 0)]
    s += [("mv", i) for i in range(3)]
    head = lambda h: [("mq", h), ("mk", h)]
    s += head(0) + attention_steps("ml", MH, head)
    s += path_steps(2)
    for d in range(KD):
        s += [("wo", d)]
        if d:
            s += [("xt", d - 1)]
    s += [("xt", KD - 1), ("ln", 0)]
    return s


STEPS = layer_steps()

JOBS = {
    "mod": lambda i: [("mod_ready", 1)],
    "ht": lambda i: [("h_ready", i + 1)],
    "conv": lambda i: [("up_ready", i + 1)],
    "ffn": lambda i: [("farg_ready", i + 1)],
    "filt": lambda i: [("fab_ready", i + 1)],
    "fdft": lambda i: [("spec_ready", i % 5 + 1 + 10 * (i // 5))],
    "zdft": lambda i: [("spec_ready", i % 5 + 6 + 10 * (i // 5))],
    "zt": lambda i: [("zt_ready", i + 1)],
    "inv": lambda i: [("z_ready", i + 1)],
    "path": lambda i: [("gate_used", 12 * (i // 4) + i % 4 + 1)],
    "merge": lambda i: [("th_ready", 12 * (i // 8) + i % 8 + 5), ("gate_used", 12 * (i // 8) + i % 8 + 5)],
    "qk": lambda i: [("raw_ready", i + 1)],
    "kc": lambda i: [("kc_ready", 1)],
    "sk": lambda i: [("sk_ready", 1)],
    "v": lambda i: [("raw_ready", 9 + i)],
    "vt": lambda i: [("v_ready", i + 1)],
    "da_score": lambda u: [("da_exp", 2 * u + 1), ("da_exp", 2 * u + 2)],
    "da_ptrans": lambda u: [("da_pt", u + 1)],
    "da_pv": lambda h: [("da_o", h + 1)],
    "dams": lambda h: [("da_ms", h + 1)],
    "dqkv": lambda i: [("c_raw", i + 1)],
    "kr": lambda i: [("kr_raw", 1)],
    "cc": lambda i: [("cc_ready", 2)],
    "mms": lambda i: [("m_ms", i + 1)],
    "sc": lambda i: [("sc_ready", 1)],
    "mv": lambda i: [("mv_ready", i + 1)],
    "mq": lambda h: [("mq_raw", h + 1)],
    "mk": lambda h: [("mk_ready", h + 1)],
    "ml_score": lambda u: [("ml_exp", u + 1)],
    "ml_ptrans": lambda u: [("ml_pt", u + 1)],
    "ml_pv": lambda h: [("ml_o", h + 1)],
    "wo": lambda d: [("r_ready", d + 1)],
    "xt": lambda d: [("x_part", d + 1)],
    "ln": lambda d: [],
}
PER = dict(mod_ready=1, h_ready=8, up_ready=12, conv_ready=12, farg_ready=2, hid_ready=2, decay_ready=10,
           fab_ready=10, odd_ready=20, spec_ready=20, zt_ready=6, y_ready=2, z_ready=8, th_ready=36, gate_used=36,
           raw_ready=12, qk_ready=8, kc_ready=1, sk_ready=1, v_ready=4, da_max=40, da_exp=40, da_p=20, da_pt=20,
           da_o=4, da_sq=4, da_ms=4, da_rt=1, c_raw=5, c_sq=5, kr_raw=1, cc_ready=2, kr_ready=1, m_ms=2, m_rt=1,
           pad_ready=1, lam_sum=1, lam_exp=1, c_ready=2, sc_ready=1, mv_ready=3, mq_raw=8, mq_ready=8, mk_ready=8, ml_max=40, ml_exp=40, ml_p=40,
           ml_pt=40, ml_o=8, r_ready=8, x_part=8, ln_var=1, ln_rt=1, x_ready=5)


def slot_table():
    table, at, uses, last = {}, 0, [0] * SLOTS, [None] * SLOTS
    for kind, i in STEPS:
        for j, freed in enumerate(JOBS[kind](i)):
            s = at % SLOTS
            table[kind, i, j] = (s, uses[s], last[s])
            last[s] = freed
            uses[s] += 1
            at += 1
    return table, uses


SLOT, USES = slot_table()


def weight_stream():
    w = []
    for kind, i in STEPS:
        if kind == "mod":
            w += [("mod", m) for m in range(3 * KD)]
        elif kind == "conv":
            w.append(("in", T_HY + i))
        elif kind == "path":
            w.append(("in", T_PATH + i))
        elif kind == "merge":
            w += [("in", T_MERGE + i), ("br", i)]
        elif kind == "qk":
            w.append(("in", T_Q + i))
        elif kind == "v":
            w.append(("in", T_V + i))
        elif kind == "dqkv":
            w.append(("in", T_DQ + i))
        elif kind == "kr":
            w.append(("in", T_KR))
        elif kind == "wo":
            w.append(("out", i))
    return w


STREAM = weight_stream()
WORDER = {key: n for n, key in enumerate(STREAM)}
NW = 4
assert len(STREAM) % NW == 2
NSTREAM = len(STREAM)


def constants():
    f = np.float32
    pos_row = np.repeat(np.arange(LAT // GRID_W), GRID_W).astype(f)
    pos_col = np.tile(np.arange(GRID_W), LAT // GRID_W).astype(f)

    def rope(dim, reps):
        q = dim // 4
        freqs = (1.0 / (np.float32(10000.0) ** (np.arange(q, dtype=f) / q))).astype(f)
        cos, sin = [], []
        for pos in (pos_row, pos_col):
            ang = (pos[None, :] * freqs[:, None]).astype(f)
            cos += [np.cos(ang), np.cos(ang)]
            sin += [-np.sin(ang), np.sin(ang)]
        one = np.stack([np.concatenate(cos), np.concatenate(sin)], 1).astype(f)
        return np.tile(one, (reps, 1, 1))

    def feats(n):
        t = np.arange(n, dtype=f)
        ang = (f(TWO_PI / n) * t[:, None] * np.arange(1, 17, dtype=f)).astype(f)
        lin = t / f(n - 1)
        return np.concatenate([lin[:, None], np.cos(ang), -np.sin(ang)], -1).T.astype(f), lin

    f_lat, lin_lat = feats(LAT)
    f_ctx, lin_ctx = feats(CTX)
    u = np.arange(128)
    tok = [2 * (128 * half + u) + par for par in range(2) for half in range(2)]
    negt = np.stack([-lin_lat[t] for t in tok] + [-lin_ctx], 1).astype(f)
    mask = np.ones((128, NT), f)
    mask[0, 0] = mask[0, 4] = 0.0
    k = np.arange(256)
    ang = lambda t: np.pi * np.outer(t, 2 * k + 1) / 1024
    fwd = np.stack([np.stack([np.cos(ang(t)), np.sin(ang(t))], 1) for t in tok], 1).astype(f)
    angc = np.pi * np.outer(u, 2 * u + 1) / 256
    fwdc = np.stack([np.cos(angc), np.sin(angc)], 1).astype(f)
    inv = np.zeros((128, 2, 2, 512), f)
    for m in range(2):
        for q, fn in enumerate((np.cos, np.sin)):
            for par in range(2):
                t = 2 * np.arange(256) + par
                inv[:, m, q, 256 * par:256 * par + 256] = fn(
                    np.pi * np.outer(2 * (128 * m + u) + 1, t) / 1024) / 512
    invc = np.stack([fn(np.pi * np.outer(2 * u + 1, u) / 256) / 128 for fn in (np.cos, np.sin)], 1).astype(f)
    lam = np.stack([[0.8 - 0.6 * math.exp(-0.3 * l), 0.2 + 0.6 * math.exp(-0.3 * l)] for l in range(DEPTH)])
    return {
        "ident": np.eye(128, dtype=f), "ones": np.ones((128, 128), f),
        "rope_da": rope(DHD, 2), "rope_m": rope(MR, 1),
        "feats": np.concatenate([f_lat, f_ctx], 1), "negt": negt, "hmask": mask,
        "fwd": fwd, "fwdc": fwdc, "inv": inv, "invc": invc, "lam_init": lam.astype(f),
    }


def build(nc, A, O):
    f32 = mybir.dt.float32
    ALU = mybir.AluOpType
    ACT = mybir.ActivationFunctionType
    AX = mybir.AxisListType.X
    o_prompt, o_sample, o_k, o_v, o_ckv, o_kr = O

    ctx = ExitStack()
    with ctx:
        def sb(name, shape):
            return ctx.enter_context(nc.sbuf_tensor(name, shape, f32))

        X = sb("X", [128, NT, D])
        H = sb("H", [128, KD, NTOK])
        W = sb("W", [128, NW, KD, 128])
        MG = sb("MG", [128, KD * NTOK])
        BR = sb("BR", [128, CT * NTOK])
        raw = sb("raw", [128, 2, 644])
        th = sb("th", [128, 2, NTOK])
        ident = sb("ident", [128, 128])
        ones = sb("ones", [128, 128])
        rope_da = sb("rope_da", [128, 2, LAT])
        rope_m = sb("rope_m", [96, 2, LAT])
        negt = sb("negt", [128, NT])
        hmask = sb("hmask", [128, NT])
        ccol = sb("ccol", [128, KD, 2])
        csig = sb("csig", [128, KD, 2])
        modc = sb("modc", [128, 3 * KD, 2])
        vecs = sb("vecs", [128, NVEC])
        bmod = vec(vecs, "b_mod")
        convw = vec(vecs, "hy_conv_w").rearrange("p (a b) -> p a b", a=3)
        convb = vec(vecs, "hy_conv_b")
        skip = vec(vecs, "hy_skip").rearrange("p (a b) -> p a b", a=2)
        fvec = vec(vecs, "hy_ffn")[0:HY_FFN]
        subln = vec(vecs, "da_subln")
        qn = vec(vecs, "mla_q_norm")
        kvn = vec(vecs, "mla_kv_norm")
        fw1 = sb("fw1", [POS, HY_FFN])
        fw2 = sb("fw2", [HY_FFN, HY_FFN])
        lp = sb("lp", [128, 4, DHD])
        lpj = sb("lpj", [128, 2, DHD])
        lamc = sb("lamc", [128, 8])
        st = sb("st", [128, 2, 8])
        lnst = sb("lnst", [128, NT, 2, 6])
        lnmv = sb("lnmv", [128, NT, 2])
        lnr = sb("lnr", [128, NT])
        WORK = 25300
        work = sb("work", [128, WORK])

        def area(base, off, *dims):
            n = int(np.prod(dims))
            ap = base[:, off:off + n]
            if len(dims) == 1:
                return ap
            names = "abcd"[:len(dims)]
            return ap.rearrange(f"p ({' '.join(names)}) -> p {' '.join(names)}",
                                **{c: d for c, d in zip(names, dims)})

        ZP = LAT + 2
        V4 = area(work, 0, CT, 642)
        G4 = area(work, 2568, CT, 642)
        zT = area(work, 5136, NT, HY)
        tB, tC = area(work, 5136, 1024), area(work, 6160, 1024)
        PM = area(work, 7696, 2, 2, 1024)
        PMc = area(work, 11792, 2, HY)
        fab = area(work, 7696, 2, NT, HY)
        HS = area(work, 12816, 2, 2, 1024)
        HSc = area(work, 16912, 2, HY)
        decay = area(work, 17936, 2, HY)
        oddb = area(work, 18960, 2, HY)
        fwdc = area(work, 19984, 2, 128)
        invc = area(work, 20240, 2, 128)
        w3 = area(work, 20496, 2, 2, HY)[0:HY_FFN]
        expld = area(work, 22544, 2, 2, HY)
        fwd = area(MG, 0, 4, 2, 256)
        inv = area(MG, 2048, 2, 2, 512)
        tconv = area(MG, 4096, 642)
        feats = area(BR, 0, NTOK)[0:POS]
        hid = area(BR, 640, NTOK)[0:HY_FFN]
        rr = area(BR, 1280, 2, NTOK)[0:HY_FFN]
        qT = area(work, 0, 4, NTOK)
        kT = area(work, 2560, 4, NKEY)
        V = area(work, 5632, 6, 512)
        E = area(work, 8704, 2, 2, NTOK)
        PT = area(work, 11264, 2, NT, LAT)
        PTc = area(work, 16384, 2, 128)
        OT = area(work, 16640, 4, NTOK)
        MS = area(work, 19200, 4, NTOK)
        ckc = area(work, 21760, 512)
        stk = area(work, 22272, 512)
        swp = area(work, 22784, LAT)
        Y = area(work, 0, 4, NTOK)
        cq = area(work, 2560, 3, NTOK)
        ckv = area(work, 4480, 2, NKEY)
        Vm = area(work, 6016, 6, 512)
        mqT = area(work, 9088, 2, NTOK)
        mkT = area(work, 10368, 2, NKEY)
        Em = area(work, 11904, 2, NTOK)
        PTm = area(work, 13184, 1, NT, LAT)
        PTmc = area(work, 15744, 2, 128)
        wuq = area(work, 16000, 3, 768)
        wukv = area(work, 18304, 2, 1024)
        sqm = area(work, 20352, 3, NTOK)
        MSm = area(work, 22272, 2, NTOK)
        cc = area(work, 23552, KVL)
        ckr = area(work, 23808, MR)
        stc = area(work, 23840, KVL + MR)
        krs = area(work, 24128, NTOK)[0:MR]
        swm = area(work, 24768, LAT)
        lng = area(work, 0, D)
        lnb = area(work, 1024, D)
        rT = raw

        PS = [ctx.enter_context(nc.psum_tensor(f"PS{i}", [128, 1024], f32)) for i in range(SLOTS)]

        sems = {}

        def sem(name):
            sems[name] = ctx.enter_context(nc.semaphore(name))
            return sems[name]

        for name in PER:
            sem(name)
        full = [sem(f"psum_full{i}") for i in range(SLOTS)]
        w_here = [sem(f"weights_here{i}") for i in range(NW)]
        w_used = sem("weights_used")
        consts_here = sem("consts_here")
        x_here = sem("x_here")
        small_here = sem("small_here")
        hy_here = sem("hyena_tables_here")
        da_here = sem("da_cache_here")
        ml_here = sem("mla_weights_here")
        ln_here = sem("ln_weights_here")
        c_sig = sem("c_sig")
        c_silu = sem("c_silu")
        store_k = sem("store_k")
        store_c = sem("store_c")
        store_y = sem("store_y")
        act_chain = sem("act_chain")
        dve_chain = sem("dve_chain")
        chain = {"act": 0, "dve": 0}

        def after(name, l, count):
            return sems[name], l * PER[name] + count

        def filled(l, kind, i, j=0):
            s, u, _ = SLOT[kind, i, j]
            return full[s], l * USES[s] + u + 1

        def full_of(kind, i, j=0):
            return full[SLOT[kind, i, j][0]]

        def freed(l, kind, i, j=0):
            before = SLOT[kind, i, j][2]
            if before:
                return after(before[0], l, before[1])
            return after("x_ready", l - 1, 5) if l else (consts_here, 16 * 8)

        def slot(kind, i, j=0):
            return PS[SLOT[kind, i, j][0]]

        def halves(ap):
            return ap.rearrange("p (a b) -> p a b", a=2)

        def two(ps, n=HALF, p=128):
            return ps[0:p, :].rearrange("p (a b) -> p a b", a=2)[:, :, 0:n]

        block = ctx.enter_context(nc.Block())

        N_SMALL, N_HY, N_DA, N_ML, N_LN = 5, 7, 2, 4, 2

        @block.sync
        def _(sp):
            def weight(l, n):
                kind, i = STREAM[n]
                g = l * NSTREAM + n
                if g >= NW:
                    sp.wait_ge(w_used, g - NW + 1)
                b = g % NW
                if kind == "in":
                    src = A["w_in_kr"][l] if i == T_KR else A["w_in"][l, i - (i > T_KR)]
                else:
                    src = A[{"mod": "w_mod", "br": "w_branch", "out": "w_out"}[kind]][l, i]
                sp.dma_start(W[:, b, 0:src.shape[1], 0:src.shape[2]], src).then_inc(w_here[b], 16)

            sp.dma_start(csig[:], A["cvec"]).then_inc(consts_here, 16)
            for t, s in ((ident, "ident"), (ones, "ones"), (rope_da, "rope_da"), (negt, "negt"), (hmask, "hmask")):
                sp.dma_start(t[:], A[s]).then_inc(consts_here, 16)
            sp.dma_start(rope_m[0:MR], A["rope_m"]).then_inc(consts_here, 16)
            sp.dma_start(rope_m[64:96], A["rope_m"]).then_inc(consts_here, 16)
            sp.dma_start(X[:, 0:4, :], A["x_sample"][0].rearrange("(t p) d -> p t d", p=128)).then_inc(x_here, 16)
            sp.dma_start(X[:, 4, :], A["x_prompt"][0]).then_inc(x_here, 16)

            for l in range(DEPTH):
                if l:
                    sp.wait_ge(*after("x_ready", l - 1, 5))
                small = [(vecs[:], A["vecs"][l]), (fw1[:], A["hy_ffn_w1"][l]), (fw2[:], A["hy_ffn_w2"][l]),
                         (lp[:].rearrange("p a b -> p (a b)"),
                          A["da_lambda"][l].rearrange("a b -> (a b)").partition_broadcast(128)),
                         (lamc[:, 0:2], A["lam_init"][l].partition_broadcast(128))]
                assert len(small) == N_SMALL
                for dst, src in small:
                    sp.dma_start(dst, src).then_inc(small_here, 16)
                for dst, src in ((fwd, A["fwd"]), (inv, A["inv"]), (fwdc, A["fwdc"]), (invc, A["invc"]),
                                 (feats, A["feats"]),
                                 (w3.rearrange("p a b c -> p (a b c)"), A["hy_ffn_w3"][l]),
                                 (expld.rearrange("p a b c -> p (a b c)"),
                                  A["hy_log_decay"][l].partition_broadcast(128))):
                    sp.dma_start(dst, src).then_inc(hy_here, 16)
                n = 0
                for kind, i in STEPS:
                    if (kind, i) == ("qk", 0):
                        sp.wait_ge(*after("gate_used", l, 4))
                        sp.dma_start(ckc, A["cache_diff_k"][0, l].rearrange("t a h d -> t (a h d)"))\
                          .then_inc(da_here, 16)
                        sp.dma_start(V[:, 0, :], A["cache_diff_v"][0, l].rearrange("t h d -> t (h d)"))\
                          .then_inc(da_here, 16)
                    if (kind, i) == ("dqkv", 0):
                        sp.wait_ge(*after("sk_ready", l, 1))
                        sp.wait_ge(*after("v_ready", l, 4))
                        sp.dma_start(o_k[0, l].rearrange("t a h d -> t (a h d)"), stk).then_inc(store_k, 16)
                        sp.dma_start(o_v[0, l].rearrange("t h d -> t (h d)"), V[:, 5, :]).then_inc(store_k, 16)
                        sp.wait_ge(*after("gate_used", l, 16))
                        sp.wait_ge(store_k, 32 * (l + 1))
                        for dst, src in ((wuq, A["mla_w_uq"][l].rearrange("(k p) n -> p k n", p=128)),
                                         (wukv, A["mla_w_ukv"][l].rearrange("(k p) n -> p k n", p=128)),
                                         (cc, A["cache_mla_ckv"][0, l]), (ckr, A["cache_mla_krope"][0, l])):
                            sp.dma_start(dst, src).then_inc(ml_here, 16)
                    if (kind, i) == ("wo", 0):
                        sp.wait_ge(*after("sc_ready", l, 1))
                        sp.dma_start(o_ckv[0, l], stc[:, 0:KVL]).then_inc(store_c, 16)
                        sp.dma_start(o_kr[0, l], stc[:, KVL:KVL + MR]).then_inc(store_c, 16)
                        sp.wait_ge(*after("gate_used", l, 28))
                        sp.dma_start(lng, A["ln_g"][l].partition_broadcast(128)).then_inc(ln_here, 16)
                        sp.dma_start(lnb, A["ln_b"][l].partition_broadcast(128)).then_inc(ln_here, 16)
                        sp.wait_ge(store_c, 32 * (l + 1))
                    while n < NSTREAM and STREAM[n] in owned(kind, i):
                        weight(l, n)
                        n += 1
                assert n == NSTREAM
            sp.wait_ge(*after("x_ready", DEPTH - 1, 5))
            sp.dma_start(o_sample[0].rearrange("(t p) d -> p t d", p=128), X[:, 0:4, :]).then_inc(store_y, 16)
            sp.dma_start(o_prompt[0], X[:, 4, :]).then_inc(store_y, 16)
            sp.wait_ge(store_y, 32)

        @block.tensor
        def _(pe):
            def take(l, key):
                g = l * NSTREAM + WORDER[key]
                pe.wait_ge(w_here[g % NW], 16 * (g // NW + 1))
                return W[:, g % NW]

            def project(l, key, ps, src, k, m=128):
                w = take(l, key)
                for a in range(2):
                    for kk in range(k):
                        last = pe.matmul(ps[0:m, 512 * a:512 * a + HALF], w[:, kk, 0:m],
                                         src[:, kk, HALF * a:HALF * a + HALF], start=kk == 0, stop=kk == k - 1)
                return last

            def projected(l, kind, i, key, src, k, m=128, j=0):
                pe.wait_ge(*freed(l, kind, i, j))
                ps = slot(kind, i, j)
                last = project(l, key, ps, src, k, m)
                last.then_inc(full_of(kind, i, j), 1)
                pe.wait_ge(*filled(l, kind, i, j))
                pe.sem_inc(w_used, 1)

            def transpose(out, in_, p=128):
                return pe.transpose(out, in_, ident[0:p, 0:p])

            def dft(l, kind, i, srcs):
                pe.wait_ge(*freed(l, kind, i))
                ps = slot(kind, i)
                if i % 5 < 4:
                    q, m = divmod(i % 5, 2)
                    for par in range(2):
                        for half in range(2):
                            t = 2 * par + half
                            last = pe.matmul(ps[:, 512 * par:512 * par + HY], fwd[:, t, q, 128 * m:128 * m + 128],
                                             srcs[q][:, t, :], start=half == 0, stop=half == 1)
                else:
                    for q in range(2):
                        last = pe.matmul(ps[:, 512 * q:512 * q + HY], fwdc[:, q, :], srcs[q][:, 4, :],
                                         start=True, stop=True)
                last.then_inc(full_of(kind, i), 1)

            def keys(t):
                return (0, LKEY) if t < 4 else (LKEY, CTX)

            def scores(ps, q, k, t):
                k0, n = keys(t)
                if t == 4:
                    return pe.matmul(ps[:, 0:n], q[:, 128 * t:128 * t + 128], k[:, k0:k0 + n], start=True, stop=True)
                for a in range(2):
                    last = pe.matmul(ps[:, 512 * a:512 * a + HALF], q[:, 128 * t:128 * t + 128],
                                     k[:, HALF * a:HALF * a + HALF], start=True, stop=True)
                return last

            def ptrans(l, kind, u, P):
                pe.wait_ge(*freed(l, kind, u))
                ps = slot(kind, u)
                for kt in range(NT if u % NT < 4 else 1):
                    last = transpose(ps[:, 128 * kt:128 * kt + 128], P[:, 128 * kt:128 * kt + 128])
                last.then_inc(full_of(kind, u), 1)

            def values(l, kind, h, v, c0, m, pt, ptc):
                pe.wait_ge(*freed(l, kind, h))
                ps = slot(kind, h)
                for kt in range(NT):
                    pe.matmul(ps[0:m, 0:LAT], v[:, kt, c0:c0 + m], pt[:, kt, :], start=kt == 0, stop=kt == NT - 1)
                pe.matmul(ps[0:m, LAT:NTOK], v[:, 5, c0:c0 + m], ptc, start=True, stop=True).then_inc(full_of(kind, h), 1)

            pe.wait_ge(consts_here, 16 * 8)
            pe.wait_ge(c_silu, 1)
            for l in range(DEPTH):
                if l:
                    pe.wait_ge(*after("x_ready", l - 1, 5))
                    pe.wait_ge(store_c, 32 * l)
                for kind, i in STEPS:
                    if kind == "mod":
                        pe.wait_ge(*freed(l, kind, i))
                        ps = slot(kind, i)
                        for m in range(3 * KD):
                            w = take(l, ("mod", m))
                            for k in range(KD):
                                last = pe.matmul(ps[:, 2 * m:2 * m + 2], w[:, k, :], ccol[:, k, :],
                                                 start=k == 0, stop=k == KD - 1)
                            if m < 3 * KD - 1:
                                last.then_inc(w_used, 1)
                        last.then_inc(full_of(kind, i), 1)
                        pe.wait_ge(*filled(l, kind, i))
                        pe.sem_inc(w_used, 1)
                    elif kind == "ht":
                        pe.wait_ge(*freed(l, kind, i))
                        ps = slot(kind, i)
                        if i == 0:
                            pe.wait_ge(x_here, 32)
                        for t in range(NT):
                            last = transpose(ps[:, 128 * t:128 * t + 128], X[:, t, 128 * i:128 * i + 128])
                        last.then_inc(full_of(kind, i), 1)
                    elif kind == "conv":
                        if i == 0:
                            pe.wait_ge(*after("h_ready", l, 8))
                        projected(l, kind, i, ("in", T_HY + i), H, KD)
                    elif kind == "ffn":
                        pe.wait_ge(*freed(l, kind, i))
                        ps = slot(kind, i)
                        if i == 0:
                            pe.wait_ge(small_here, 16 * N_SMALL * (l + 1))
                            pe.wait_ge(hy_here, 16 * N_HY * (l + 1))
                        else:
                            pe.wait_ge(*after("hid_ready", l, 1))
                        for a in range(2):
                            last = pe.matmul(ps[0:HY_FFN, 512 * a:512 * a + HALF], (fw2 if i else fw1)[:],
                                             (hid if i else feats)[:, HALF * a:HALF * a + HALF], start=True, stop=True)
                        last.then_inc(full_of(kind, i), 1)
                    elif kind == "filt":
                        o, t = divmod(i, NT)
                        pe.wait_ge(*freed(l, kind, i))
                        ps = slot(kind, i)
                        if i == 0:
                            pe.wait_ge(*after("hid_ready", l, 2))
                        par, half = divmod(t, 2)
                        hcol = (hid[:, 256 * half + par:256 * half + par + 255:2] if t < 4
                                else hid[:, LAT:NTOK])
                        for d in range(2):
                            last = pe.matmul(ps[:, 512 * d:512 * d + HY], hcol, w3[:, d, o, :], start=True, stop=True)
                        last.then_inc(full_of(kind, i), 1)
                    elif kind == "fdft":
                        if i % 5 == 0:
                            pe.wait_ge(*after("fab_ready", l, 5 * (i // 5) + 5))
                        dft(l, kind, i, (fab[:, 0], fab[:, 1]))
                    elif kind == "zt":
                        o, r = divmod(i, 3)
                        pe.wait_ge(*freed(l, kind, i))
                        ps = slot(kind, i)
                        if i == 0:
                            pe.wait_ge(*after("conv_ready", l, 4))
                        elif r == 0:
                            pe.wait_ge(*after("z_ready", l, 4 * o))
                        for b in range(2 if r < 2 else 1):
                            for c in range(CT):
                                src = (V4[:, c, 256 * b + r:256 * b + r + 255:2] if r < 2
                                       else V4[:, c, ZP:ZP + CTX])
                                last = transpose(ps[:, 512 * b + 128 * c:512 * b + 128 * c + 128], src)
                        last.then_inc(full_of(kind, i), 1)
                    elif kind == "zdft":
                        if i % 5 == 0:
                            pe.wait_ge(*after("zt_ready", l, 3 * (i // 5) + 3))
                        dft(l, kind, i, (zT, zT))
                    elif kind == "inv":
                        o, c = divmod(i, CT)
                        pe.wait_ge(*freed(l, kind, i))
                        ps = slot(kind, i)
                        if c == 0:
                            pe.wait_ge(*after("y_ready", l, o + 1))
                        for par in range(2):
                            for n_ in range(4):
                                q, m = divmod(n_, 2)
                                pe.matmul(ps[:, 256 * par:256 * par + 256],
                                          PM[:, par, q, 512 * m + 128 * c:512 * m + 128 * c + 128],
                                          inv[:, m, q, 256 * par:256 * par + 256], start=n_ == 0, stop=n_ == 3)
                        for q in range(2):
                            last = pe.matmul(ps[:, 512:640], PMc[:, q, 128 * c:128 * c + 128], invc[:, q, :],
                                             start=q == 0, stop=q == 1)
                        last.then_inc(full_of(kind, i), 1)
                    elif kind == "path":
                        projected(l, kind, i, ("in", T_PATH + i), H, KD)
                    elif kind == "merge":
                        n_, d = divmod(i, KD)
                        projected(l, kind, i, ("in", T_MERGE + i), H, KD)
                        if d == 0:
                            pe.wait_ge(*after("gate_used", l, 12 * n_ + 4))
                        projected(l, kind, i, ("br", i), area(BR, 0, CT, NTOK), CT, j=1)
                    elif kind == "qk":
                        projected(l, kind, i, ("in", T_Q + i), H, KD)
                    elif kind == "kc":
                        pe.wait_ge(*freed(l, kind, i))
                        ps = slot(kind, i)
                        pe.wait_ge(da_here, 16 * N_DA * (l + 1))
                        for c in range(4):
                            last = transpose(ps[:, 128 * c:128 * c + 128], ckc[:, 128 * c:128 * c + 128])
                        last.then_inc(full_of(kind, i), 1)
                    elif kind == "sk":
                        pe.wait_ge(*freed(l, kind, i))
                        ps = slot(kind, i)
                        pe.wait_ge(*after("qk_ready", l, 8))
                        for c in range(4):
                            last = transpose(ps[:, 128 * c:128 * c + 128], kT[:, c, LKEY:NKEY])
                        last.then_inc(full_of(kind, i), 1)
                    elif kind == "v":
                        projected(l, kind, i, ("in", T_V + i), H, KD)
                    elif kind == "vt":
                        pe.wait_ge(*freed(l, kind, i))
                        ps = slot(kind, i)
                        pe.wait_ge(*after("raw_ready", l, 9 + i))
                        for t in range(NT):
                            last = transpose(ps[:, 128 * t:128 * t + 128], raw[:, i % 2, 128 * t:128 * t + 128])
                        last.then_inc(full_of(kind, i), 1)
                    elif kind == "da_score":
                        h, t = divmod(i, NT)
                        if i == 0:
                            pe.wait_ge(*after("kc_ready", l, 1))
                        p = 64 * (h % 2)
                        for j in range(2):
                            pe.wait_ge(*freed(l, kind, i, j))
                            ps = slot(kind, i, j)
                            last = scores(ps, qT[p:p + 64, 2 * j + h // 2], kT[p:p + 64, 2 * j + h // 2], t)
                            last.then_inc(full_of(kind, i, j), 1)
                    elif kind == "da_ptrans":
                        pe.wait_ge(*after("da_p", l, i + 1))
                        ptrans(l, kind, i, E[:, i % 2, 0])
                    elif kind == "da_pv":
                        if i == 0:
                            pe.wait_ge(*after("v_ready", l, 4))
                        pe.wait_ge(*after("da_pt", l, NT * (i + 1)))
                        values(l, kind, i, V, 128 * i, 128, PT[:, i % 2], PTc[:, i % 2])
                    elif kind == "dams":
                        pe.wait_ge(*freed(l, kind, i))
                        ps = slot(kind, i)
                        pe.wait_ge(*after("da_sq", l, i + 1))
                        for a in range(2):
                            last = pe.matmul(ps[:, 512 * a:512 * a + HALF], ones[:],
                                             MS[:, i, HALF * a:HALF * a + HALF], start=True, stop=True)
                        last.then_inc(full_of(kind, i), 1)
                    elif kind == "dqkv":
                        projected(l, kind, i, ("in", T_DQ + i), H, KD)
                    elif kind == "kr":
                        projected(l, kind, i, ("in", T_KR), H, KD, MR)
                    elif kind == "cc":
                        pe.wait_ge(*freed(l, kind, i))
                        ps = slot(kind, i)
                        pe.wait_ge(ml_here, 16 * N_ML * (l + 1))
                        for c in range(2):
                            transpose(ps[:, 128 * c:128 * c + 128], cc[:, 128 * c:128 * c + 128])
                        transpose(ps[0:MR, 512:640], ckr).then_inc(full_of(kind, i), 1)
                    elif kind == "mms":
                        pe.wait_ge(*freed(l, kind, i))
                        ps = slot(kind, i)
                        pe.wait_ge(*after("c_sq", l, 3 if i == 0 else 5))
                        k = 3 - i
                        for a in range(2):
                            for kk in range(k):
                                last = pe.matmul(ps[:, 512 * a:512 * a + HALF], ones[:],
                                                 sqm[:, kk, HALF * a:HALF * a + HALF], start=kk == 0, stop=kk == k - 1)
                        last.then_inc(full_of(kind, i), 1)
                    elif kind == "sc":
                        pe.wait_ge(*freed(l, kind, i))
                        ps = slot(kind, i)
                        pe.wait_ge(*after("c_ready", l, 2))
                        for c in range(2):
                            transpose(ps[:, 128 * c:128 * c + 128], ckv[:, c, LKEY:NKEY])
                        transpose(ps[:, 512:512 + MR], krs[:, LAT:NTOK], MR).then_inc(full_of(kind, i), 1)
                    elif kind == "mv":
                        pe.wait_ge(*freed(l, kind, i))
                        ps = slot(kind, i)
                        for b in range(2):
                            t = 2 * i + b
                            for k in range(2):
                                last = pe.matmul(
                                    ps[:, 512 * b:512 * b + 512], ckv[:, k, 128 * t:128 * t + 128],
                                    wukv[:, k, :].rearrange("p (h e) -> p h e", h=MH)[:, :, MN:MN + MV],
                                    start=k == 0, stop=k == 1)
                        last.then_inc(full_of(kind, i), 1)
                    elif kind == "mq":
                        pe.wait_ge(*freed(l, kind, i))
                        ps = slot(kind, i)
                        for a in range(2):
                            for k in range(3):
                                last = pe.matmul(ps[0:96, 512 * a:512 * a + HALF], wuq[:, k, 96 * i:96 * i + 96],
                                                 cq[:, k, HALF * a:HALF * a + HALF], start=k == 0, stop=k == 2)
                        last.then_inc(full_of(kind, i), 1)
                    elif kind == "mk":
                        pe.wait_ge(*freed(l, kind, i))
                        ps = slot(kind, i)
                        n_ = NKEY // 2
                        for a in range(2):
                            for k in range(2):
                                last = pe.matmul(ps[0:MN, 512 * a:512 * a + n_], wukv[:, k, 128 * i:128 * i + MN],
                                                 ckv[:, k, n_ * a:n_ * a + n_], start=k == 0, stop=k == 1)
                        last.then_inc(full_of(kind, i), 1)
                    elif kind == "ml_score":
                        h, t = divmod(i, NT)
                        pe.wait_ge(*freed(l, kind, i))
                        ps = slot(kind, i)
                        if t == 0:
                            pe.wait_ge(*after("mq_ready", l, h + 1))
                            pe.wait_ge(*after("mk_ready", l, h + 1))
                            pe.wait_ge(*after("kr_ready", l, 1))
                        scores(ps, mqT[0:96, h % 2], mkT[0:96, h % 2], t).then_inc(full_of(kind, i), 1)
                    elif kind == "ml_ptrans":
                        pe.wait_ge(*after("ml_p", l, i + 1))
                        ptrans(l, kind, i, Em[:, i % 2])
                    elif kind == "ml_pv":
                        if i == 0:
                            pe.wait_ge(*after("mv_ready", l, 3))
                        pe.wait_ge(*after("ml_pt", l, NT * (i + 1)))
                        values(l, kind, i, Vm, MV * i, MV, PTm[:, 0], PTmc[:, i % 2])
                    elif kind == "wo":
                        if i == 0:
                            pe.wait_ge(*after("gate_used", l, 36))
                        projected(l, kind, i, ("out", i), area(MG, 0, KD, NTOK), KD)
                    elif kind == "xt":
                        pe.wait_ge(*freed(l, kind, i))
                        ps = slot(kind, i)
                        pe.wait_ge(*after("r_ready", l, i + 1))
                        for t in range(NT):
                            last = transpose(ps[:, 128 * t:128 * t + 128], rT[:, i % 2, 128 * t:128 * t + 128])
                        last.then_inc(full_of(kind, i), 1)

        @block.scalar
        def _(act):
            def link(ins):
                chain["act"] += 1
                ins.then_inc(act_chain, 1)
                act.wait_ge(act_chain, chain["act"])

            def copy(out, in_, scale=1.0):
                return act.activation(out, in_, ACT.Copy, scale=scale)

            act.wait_ge(consts_here, 16 * 8)
            act.activation(ccol[:], csig[:], ACT.Sigmoid).then_inc(c_sig, 1)
            for l in range(DEPTH):
                for kind, i in STEPS:
                    if kind == "mod":
                        act.wait_ge(*after("lam_sum", l, 1))
                        act.activation(lamc[:, 4:6], lamc[:, 4:6], ACT.Exp).then_inc(sems["lam_exp"], 1)
                    elif kind == "conv":
                        act.wait_ge(*filled(l, kind, i))
                        ps = slot(kind, i)
                        if i >= 2:
                            act.wait_ge(*after("conv_ready", l, i - 1))
                        elif l:
                            act.wait_ge(*after("x_part", l - 1, 8))
                        if i < 2:
                            act.wait_ge(*after("pad_ready", l, 1))
                        r = raw[:, i % 2, :]
                        copy(r[:, 1:1 + HALF], ps[:, 0:HALF])
                        copy(r[:, 1 + HALF:1 + LAT], ps[:, 512:512 + LAT - HALF])
                        copy(r[:, ZP + 1:ZP + 1 + CTX], ps[:, 512 + LAT - HALF:512 + HALF]).then_inc(sems["up_ready"], 1)
                        if i == 3:
                            act.wait_ge(hy_here, 16 * N_HY * (l + 1))
                            link(act.activation(expld, expld, ACT.Exp))
                    elif kind == "ffn":
                        act.wait_ge(*after("farg_ready", l, i + 1))
                        act.activation(hid, rr[:, 0], ACT.Sin).then_inc(sems["hid_ready"], 1)
                    elif kind == "filt":
                        o, t = divmod(i, NT)
                        if i:
                            act.wait_ge(*after("fab_ready", l, i))
                        act.activation(decay, expld[:, :, o, :], ACT.Exp, scale=negt[:, t:t + 1]).then_inc(sems["decay_ready"], 1)
                    elif kind in ("fdft", "zdft"):
                        n = 10 * (i // 5) + 5 * (kind == "zdft") + i % 5
                        act.wait_ge(*filled(l, kind, i))
                        ps = slot(kind, i)
                        if i % 5 < 4:
                            if n >= 2:
                                act.wait_ge(*after("spec_ready", l, n - 1))
                            copy(oddb[:, n % 2], ps[:, 512:1024]).then_inc(sems["odd_ready"], 1)
                        else:
                            dst = HSc if kind == "fdft" else PMc
                            if n >= 2:
                                act.wait_ge(*after("spec_ready", l, n))
                            copy(dst, halves(ps[:, :])).then_inc(sems["spec_ready"], 1)
                            act.nop().then_inc(sems["odd_ready"], 1)
                    elif kind == "zt":
                        o, r = divmod(i, 3)
                        act.wait_ge(*filled(l, kind, i))
                        ps = slot(kind, i)
                        if o == 1 and r == 0:
                            act.wait_ge(*after("y_ready", l, 1))
                        if r < 2:
                            copy(zT[:, 2 * r:2 * r + 2, :], halves(ps[:, :])).then_inc(sems["zt_ready"], 1)
                        else:
                            copy(zT[:, 4, :], ps[:, 0:HY]).then_inc(sems["zt_ready"], 1)
                    elif kind in ("path", "merge"):
                        n = 12 * (i // 4) + i % 4 if kind == "path" else 12 * (i // 8) + 4 + i % 8
                        act.wait_ge(*filled(l, kind, i))
                        ps = slot(kind, i)
                        if n >= 2:
                            act.wait_ge(*after("gate_used", l, n - 1))
                        act.activation(halves(th[:, n % 2]), two(ps), ACT.Tanh, scale=0.5).then_inc(sems["th_ready"], 1)
                    elif kind in ("qk", "v"):
                        n = i + 8 * (kind == "v")
                        act.wait_ge(*filled(l, kind, i))
                        ps = slot(kind, i)
                        if n >= 10:
                            act.wait_ge(*after("v_ready", l, n - 9))
                        elif n >= 2:
                            act.wait_ge(*after("qk_ready", l, n - 1))
                        copy(halves(raw[:, n % 2, 0:NTOK]), two(ps), DA_SCALE if n < 4 else 1.0).then_inc(sems["raw_ready"], 1)
                    elif kind == "kc":
                        act.wait_ge(*filled(l, kind, i))
                        ps = slot(kind, i)
                        copy(kT[:, :, 0:PAST], ps[:, 0:512].rearrange("p (a b) -> p a b", a=4)).then_inc(sems["kc_ready"], 1)
                    elif kind == "sk":
                        act.wait_ge(*filled(l, kind, i))
                        copy(stk, slot(kind, i)[:, 0:512]).then_inc(sems["sk_ready"], 1)
                    elif kind == "da_score":
                        n = keysn(i)
                        for j in range(2):
                            act.wait_ge(*filled(l, kind, i, j))
                            ps = slot(kind, i, j)
                            act.wait_ge(*after("da_max", l, 2 * i + j + 1))
                            e = E[:, i % 2, j, 0:n]
                            act.activation(two_or_one(e, n), two(ps) if n > CTX else ps[:, 0:n], ACT.Exp,
                                               bias=st[:, i % 2, j:j + 1], accum_out=st[:, i % 2, 2 + j:3 + j]).then_inc(sems["da_exp"], 1)
                    elif kind in ("da_ptrans", "ml_ptrans"):
                        h, t = divmod(i, NT)
                        act.wait_ge(*filled(l, kind, i))
                        ps = slot(kind, i)
                        da = kind[0] == "d"
                        if t < 4:
                            dst = (PT[:, h % 2] if da else PTm[:, 0])[:, :, 128 * t:128 * t + 128]
                            if not da and t == 0 and h:
                                act.wait_ge(*after("ml_o", l, h))
                            ins = copy(dst, ps[:, 0:640].rearrange("p (a b) -> p a b", a=NT))
                        else:
                            ins = copy((PTc if da else PTmc)[:, h % 2], ps[:, 0:CTX])
                        ins.then_inc(sems[kind[:2] + "_pt"], 1)
                    elif kind == "da_pv":
                        act.wait_ge(*filled(l, kind, i))
                        copy(OT[:, i], slot(kind, i)[:, 0:NTOK]).then_inc(sems["da_o"], 1)
                    elif kind == "dams" and i == DAH - 1:
                        act.wait_ge(*after("da_ms", l, 4))
                        act.activation(MS, MS, ACT.Sqrt).then_inc(sems["da_rt"], 1)
                    elif kind == "dqkv":
                        act.wait_ge(*filled(l, kind, i))
                        ps = slot(kind, i)
                        if i == 0:
                            act.wait_ge(*after("gate_used", l, 16))
                        dst = cq[:, i] if i < 3 else ckv[:, i - 3, PAST:NKEY]
                        copy(halves(dst), two(ps)).then_inc(sems["c_raw"], 1)
                    elif kind == "kr":
                        act.wait_ge(*filled(l, kind, i))
                        copy(halves(krs), two(slot(kind, i), p=MR)).then_inc(sems["kr_raw"], 1)
                    elif kind == "cc":
                        act.wait_ge(*filled(l, kind, i))
                        ps = slot(kind, i)
                        copy(ckv[:, :, 0:PAST], ps[:, 0:256].rearrange("p (a b) -> p a b", a=2)).then_inc(sems["cc_ready"], 1)
                        for b in range(2):
                            last = copy(mkT[64:96, b, 0:PAST], ps[0:MR, 512:640])
                        last.then_inc(sems["cc_ready"], 1)
                    elif kind == "mms" and i == 1:
                        act.wait_ge(*after("m_ms", l, 2))
                        act.activation(MSm, MSm, ACT.Sqrt).then_inc(sems["m_rt"], 1)
                    elif kind == "sc":
                        act.wait_ge(*filled(l, kind, i))
                        ps = slot(kind, i)
                        copy(stc[:, 0:KVL], ps[:, 0:KVL])
                        copy(stc[:, KVL:KVL + MR], ps[:, 512:512 + MR]).then_inc(sems["sc_ready"], 1)
                    elif kind == "mv":
                        act.wait_ge(*filled(l, kind, i))
                        copy(Vm[:, 2 * i:2 * i + 2, :], halves(slot(kind, i)[:, :])).then_inc(sems["mv_ready"], 1)
                    elif kind == "mq":
                        act.wait_ge(*filled(l, kind, i))
                        copy(halves(mqT[0:96, i % 2]), two(slot(kind, i), p=96), MLA_SCALE).then_inc(sems["mq_raw"], 1)
                    elif kind == "mk":
                        act.wait_ge(*filled(l, kind, i))
                        copy(halves(mkT[0:MN, i % 2]), two(slot(kind, i), NKEY // 2, MN)).then_inc(sems["mk_ready"], 1)
                    elif kind == "ml_score":
                        n = keysn(i)
                        act.wait_ge(*filled(l, kind, i))
                        ps = slot(kind, i)
                        act.wait_ge(*after("ml_max", l, i + 1))
                        act.activation(two_or_one(Em[:, i % 2, 0:n], n), two(ps) if n > CTX else ps[:, 0:n],
                                           ACT.Exp, bias=st[:, i % 2, 0:1], accum_out=st[:, i % 2, 2:3]).then_inc(sems["ml_exp"], 1)
                    elif kind == "ml_pv":
                        p = 64 * (i % 2)
                        act.wait_ge(*filled(l, kind, i))
                        copy(Y[p:p + 64, i // 2], slot(kind, i)[0:MV, 0:NTOK]).then_inc(sems["ml_o"], 1)
                    elif kind == "wo":
                        act.wait_ge(*filled(l, kind, i))
                        ps = slot(kind, i)
                        if i >= 2:
                            act.wait_ge(*after("x_part", l, i - 1))
                        r, g = rT[:, i % 2, :], modc[:, 2 * KD + i, :]
                        copy_ = lambda o_, i_, s_: act.activation(o_, i_, ACT.Copy, scale=s_)
                        copy_(r[:, 0:HALF], ps[:, 0:HALF], g[:, 0:1])
                        copy_(r[:, HALF:LAT], ps[:, 512:512 + LAT - HALF], g[:, 0:1])
                        copy_(r[:, LAT:NTOK], ps[:, 512 + LAT - HALF:512 + HALF], g[:, 1:2]).then_inc(sems["r_ready"], 1)
                    elif kind == "ln":
                        act.wait_ge(*after("ln_var", l, 1))
                        act.activation(lnr[:], lnr[:], ACT.Sqrt).then_inc(sems["ln_rt"], 1)

        @block.vector
        def _(dve):
            def link(ins):
                chain["dve"] += 1
                ins.then_inc(dve_chain, 1)
                dve.wait_ge(dve_chain, chain["dve"])

            signalled = {}

            def own(name):
                signalled[name] = signalled.get(name, 0) + 1
                return sems[name], signalled[name]

            TT, TS, STT = dve.tensor_tensor, dve.tensor_scalar, dve.scalar_tensor_tensor

            def softmax_max(ps, n, out):
                return dve.tensor_reduce(out, two(ps) if n > CTX else ps[:, 0:n],
                                         mybir.AxisListType.XY if n > CTX else AX, ALU.max, negate=True)

            dve.wait_ge(consts_here, 16 * 8)
            dve.wait_ge(c_sig, 1)
            TT(ccol[:], ccol[:], csig[:], ALU.mult).then_inc(c_silu, 1)
            def clear_pads():
                dve.memset(raw[:, :, 0:1], 0.0)
                dve.memset(raw[:, :, LAT + 1:LAT + 3], 0.0)
                return dve.memset(raw[:, :, 643:644], 0.0)

            for l in range(DEPTH):
                for kind, i in STEPS:
                    if kind == "mod":
                        dve.wait_ge(small_here, 16 * N_SMALL * (l + 1))
                        dve.wait_ge(*filled(l, kind, i))
                        ps = slot(kind, i)
                        clear_pads().then_inc(sems["pad_ready"], 1)
                        dve.wait_ge(*own("pad_ready"))
                        link(TT(modc[:], ps[:, 0:6 * KD].rearrange("p (m c) -> p m c", c=2),
                                bmod[:].rearrange("p (m c) -> p m c", c=1).to_broadcast([128, 3 * KD, 2]), ALU.add))
                        link(TS(modc[:, KD:2 * KD, :], modc[:, KD:2 * KD, :], 1.0, None, ALU.add))
                        TS(modc[:, 2 * KD:, :], modc[:, 2 * KD:, :], 0.5, None, ALU.mult).then_inc(sems["mod_ready"], 1)
                        dve.wait_ge(*own("mod_ready"))
                        dve.wait_ge(*after("mod_ready", l, 1))
                        link(TT(lpj[:], lp[:, 0:4:2, :], lp[:, 1:4:2, :], ALU.mult))
                        link(dve.tensor_reduce(lamc[:, 2:4], lpj[:], AX, ALU.add))
                        TS(lamc[:, 4:6], lamc[:, 2:4], 1.0, None, ALU.mult).then_inc(sems["lam_sum"], 1)
                        dve.wait_ge(*own("lam_sum"))
                    elif kind == "ht":
                        dve.wait_ge(*filled(l, kind, i))
                        ps = slot(kind, i)
                        s = modc[:, KD + i, :]
                        b = modc[:, i, :]
                        TS(H[:, i, 0:LAT], ps[:, 0:LAT], s[:, 0:1], b[:, 0:1], ALU.mult, ALU.add)
                        TS(H[:, i, LAT:NTOK], ps[:, LAT:NTOK], s[:, 1:2], b[:, 1:2], ALU.mult, ALU.add).then_inc(sems["h_ready"], 1)
                        dve.wait_ge(*own("h_ready"))
                    elif kind == "conv":
                        dve.wait_ge(*after("up_ready", l, i + 1))
                        r = raw[:, i % 2, :]
                        dst = V4[:, i] if i < 4 else G4[:, i % 4]
                        w = lambda tap: convw[:, tap, i:i + 1]
                        link(TS(tconv, r[:, 1:643], w(1), convb[:, i:i + 1], ALU.mult, ALU.add))
                        link(STT(tconv, r[:, 0:642], w(0), tconv, ALU.mult, ALU.add))
                        STT(dst, r[:, 2:644], w(2), tconv, ALU.mult, ALU.add).then_inc(sems["conv_ready"], 1)
                        dve.wait_ge(*own("conv_ready"))
                    elif kind == "ffn":
                        dve.wait_ge(*filled(l, kind, i))
                        ps = slot(kind, i)
                        a, k = rr[:, 0], rr[:, 1]
                        if i:
                            dve.wait_ge(*after("hid_ready", l, 1))
                        link(TS(halves(a), two(ps, p=HY_FFN), fvec[:, i:i + 1], fvec[:, 2 + i:3 + i],
                                ALU.add, ALU.mult))
                        link(TS(k, a, 1 / TWO_PI, MAGIC, ALU.mult, ALU.add))
                        link(TS(k, k, MAGIC, None, ALU.subtract))
                        for part in (PI_HI, PI_MID, PI_LO):
                            link(STT(a, k, -part, a, ALU.mult, ALU.add))
                        TS(a, a, math.pi - 1e-6, -(math.pi - 1e-6), ALU.min, ALU.max).then_inc(sems["farg_ready"], 1)
                        dve.wait_ge(*own("farg_ready"))
                    elif kind == "filt":
                        o, t = divmod(i, NT)
                        dve.wait_ge(*filled(l, kind, i))
                        ps = slot(kind, i)
                        dve.wait_ge(*after("decay_ready", l, i + 1))
                        TT(oddb[:, 0], ps[:, 0:HY], decay[:, 0], ALU.mult)
                        link(STT(oddb[:, 1], ps[:, 512:1024], hmask[:, t:t + 1], decay[:, 1], ALU.mult, ALU.mult))
                        TT(fab[:, 0, t], oddb[:, 0], oddb[:, 1], ALU.add)
                        TT(fab[:, 1, t], oddb[:, 0], oddb[:, 1], ALU.subtract).then_inc(sems["fab_ready"], 1)
                        dve.wait_ge(*own("fab_ready"))
                    elif kind in ("fdft", "zdft"):
                        n = 10 * (i // 5) + 5 * (kind == "zdft") + i % 5
                        if i % 5 < 4:
                            q, m = divmod(i % 5, 2)
                            dve.wait_ge(*filled(l, kind, i))
                            ps = slot(kind, i)
                            dve.wait_ge(*after("odd_ready", l, n + 1))
                            dst = HS if kind == "fdft" else PM
                            TT(dst[:, 0, q, 512 * m:512 * m + 512], ps[:, 0:HY], oddb[:, n % 2], ALU.add)
                            TT(dst[:, 1, q, 512 * m:512 * m + 512], ps[:, 0:HY], oddb[:, n % 2], ALU.subtract).then_inc(sems["spec_ready"], 1)
                            dve.wait_ge(*own("spec_ready"))
                        elif kind == "zdft":
                            dve.wait_ge(*after("spec_ready", l, n + 1))
                            for s in range(2):
                                product(dve, link, TT, ALU, PM[:, s], HS[:, s], tB, tC)
                            link(TT(PM[:, 1], PM[:, 0], PM[:, 1], ALU.subtract))
                            link(STT(PM[:, 0], PM[:, 0], 2.0, PM[:, 1], ALU.mult, ALU.subtract))
                            product(dve, link, TT, ALU, PMc, HSc, tB[:, 0:HY], tC[:, 0:HY])
                            dve.nop().then_inc(sems["y_ready"], 1)
                    elif kind == "inv":
                        o, c = divmod(i, CT)
                        dve.wait_ge(*filled(l, kind, i))
                        ps = slot(kind, i)
                        dve.wait_ge(*after("conv_ready", l, 8 + 4 * o))
                        sk = skip[:, o, c:c + 1]
                        t_lat, t_ctx = tconv[:, 0:LAT], tconv[:, ZP:ZP + CTX]
                        pairs = lambda ap: ap.rearrange("p (u a) -> p u a", a=2)
                        STT(pairs(t_lat), pairs(V4[:, c, 0:LAT]), sk,
                            ps[:, 0:LAT].rearrange("p (a u) -> p u a", a=2), ALU.mult, ALU.add)
                        link(STT(t_ctx, V4[:, c, ZP:ZP + CTX], sk, ps[:, 512:640], ALU.mult, ALU.add))
                        TT(V4[:, c, 0:LAT], t_lat, G4[:, c, 0:LAT], ALU.mult)
                        TT(V4[:, c, ZP:ZP + CTX], t_ctx, G4[:, c, ZP:ZP + CTX], ALU.mult).then_inc(sems["z_ready"], 1)
                        dve.wait_ge(*own("z_ready"))
                        if i == 7:
                            dve.wait_ge(*after("z_ready", l, 8))
                    elif kind == "path":
                        n_, c = divmod(i, CT)
                        g = 12 * n_ + c
                        dve.wait_ge(*filled(l, kind, i))
                        ps = slot(kind, i)
                        dve.wait_ge(*after("th_ready", l, g + 1))
                        if n_ == 2 and c == 0:
                            dve.wait_ge(*after("ml_o", l, MH))
                        t_ = th[:, g % 2]
                        link(STT(halves(t_), halves(t_), 1.0, two(ps), ALU.add, ALU.mult))
                        out = BR[:, NTOK * c:NTOK * c + NTOK]
                        if n_ == 0:
                            STT(out[:, 0:LAT], t_[:, 0:LAT], 0.5, V4[:, c, 0:LAT], ALU.mult, ALU.mult)
                            STT(out[:, LAT:NTOK], t_[:, LAT:NTOK], 0.5, V4[:, c, ZP:ZP + CTX],
                                    ALU.mult, ALU.mult).then_inc(sems["gate_used"], 1)
                            dve.wait_ge(*own("gate_used"))
                        else:
                            y = OT[:, c] if n_ == 1 else Y[:, c]
                            STT(out, t_, 0.5, y, ALU.mult, ALU.mult).then_inc(sems["gate_used"], 1)
                            dve.wait_ge(*own("gate_used"))
                    elif kind == "merge":
                        n_, d = divmod(i, KD)
                        g = 12 * n_ + 4 + d
                        dve.wait_ge(*filled(l, kind, i, 1))
                        ps = slot(kind, i, 1)
                        dve.wait_ge(*after("th_ready", l, g + 1))
                        t_ = th[:, g % 2]
                        m = MG[:, NTOK * d:NTOK * d + NTOK]
                        if n_ == 0:
                            STT(halves(m), halves(t_), 1.0, two(ps), ALU.add, ALU.mult).then_inc(sems["gate_used"], 1)
                            dve.wait_ge(*own("gate_used"))
                        else:
                            link(STT(halves(t_), halves(t_), 1.0, two(ps), ALU.add, ALU.mult))
                            TT(m, m, t_, ALU.add).then_inc(sems["gate_used"], 1)
                            dve.wait_ge(*own("gate_used"))
                    elif kind == "qk":
                        dve.wait_ge(*after("raw_ready", l, i + 1))
                        r = raw[:, i % 2, 0:LAT]
                        dst = qT[:, i, :] if i < 4 else kT[:, i - 4, PAST:NKEY]
                        mask = [(p + 16) % 32 for p in range(32)]
                        dve.stream_shuffle(swp, r, mask=mask).then_inc(dve_chain, 1)
                        chain["dve"] += 1
                        link(TT(dst[:, 0:LAT], r, rope_da[:, 0], ALU.mult))
                        link(TT(swp, swp, rope_da[:, 1], ALU.mult))
                        TT(dst[:, 0:LAT], dst[:, 0:LAT], swp, ALU.add)
                        dve.tensor_copy(dst[:, LAT:NTOK], raw[:, i % 2, LAT:NTOK]).then_inc(sems["qk_ready"], 1)
                        dve.wait_ge(*own("qk_ready"))
                    elif kind == "vt":
                        dve.wait_ge(*filled(l, kind, i))
                        ps = slot(kind, i)
                        dve.tensor_copy(V[:, 1:6, 128 * i:128 * i + 128],
                                            ps[:, 0:640].rearrange("p (a b) -> p a b", a=NT)).then_inc(sems["v_ready"], 1)
                        dve.wait_ge(*own("v_ready"))
                    elif kind == "da_score":
                        if i == 0:
                            dve.wait_ge(*after("lam_exp", l, 1))
                            link(TT(lamc[:, 2:3], lamc[:, 4:5], lamc[:, 5:6], ALU.subtract))
                            link(TS(lamc[:, 6:7], lamc[:, 2:3], lamc[:, 0:1], -1.0, ALU.add, ALU.mult))
                            link(TT(lamc[:, 7:8], subln[:], lamc[:, 1:2], ALU.mult))
                        n = keysn(i)
                        for j in range(2):
                            dve.wait_ge(*filled(l, kind, i, j))
                            ps = slot(kind, i, j)
                            softmax_max(ps, n, st[:, i % 2, j:j + 1]).then_inc(sems["da_max"], 1)
                            dve.wait_ge(*own("da_max"))
                    elif kind == "da_ptrans":
                        n = keysn(i)
                        s, e = st[:, i % 2], E[:, i % 2]
                        dve.wait_ge(*after("da_exp", l, 2 * i + 2))
                        link(dve.reciprocal(s[:, 4:6], s[:, 2:4]))
                        link(TT(s[:, 6:7], s[:, 5:6], lamc[:, 6:7], ALU.mult))
                        link(TS(e[:, 0, 0:n], e[:, 0, 0:n], s[:, 4:5], None, ALU.mult))
                        STT(e[:, 0, 0:n], e[:, 1, 0:n], s[:, 6:7], e[:, 0, 0:n], ALU.mult, ALU.add).then_inc(sems["da_p"], 1)
                        dve.wait_ge(*own("da_p"))
                    elif kind == "da_pv":
                        dve.wait_ge(*after("da_o", l, i + 1))
                        TT(MS[:, i], OT[:, i], OT[:, i], ALU.mult).then_inc(sems["da_sq"], 1)
                        dve.wait_ge(*own("da_sq"))
                    elif kind == "dams":
                        dve.wait_ge(*filled(l, kind, i))
                        ps = slot(kind, i)
                        TS(halves(MS[:, i]), two(ps), 1.0 / DAV, RMS_EPS, ALU.mult, ALU.add).then_inc(sems["da_ms"], 1)
                        dve.wait_ge(*own("da_ms"))
                        if i == DAH - 1:
                            dve.wait_ge(*after("da_rt", l, 1))
                            link(dve.reciprocal(MS, MS))
                            link(STT(OT, OT, lamc[:, 7:8], MS, ALU.mult, ALU.mult))
                    elif kind == "dqkv":
                        dve.wait_ge(*after("c_raw", l, i + 1))
                        c = cq[:, i] if i < 3 else ckv[:, i - 3, PAST:NKEY]
                        if i == 3:
                            dve.wait_ge(*after("m_ms", l, 1))
                        TT(sqm[:, i % 3], c, c, ALU.mult).then_inc(sems["c_sq"], 1)
                        dve.wait_ge(*own("c_sq"))
                        if i == 2:
                            dve.wait_ge(*filled(l, "mms", 0))
                            ps = slot("mms", 0)
                            TS(halves(MSm[:, 0]), two(ps), 1.0 / QL, RMS_EPS, ALU.mult, ALU.add).then_inc(sems["m_ms"], 1)
                            dve.wait_ge(*own("m_ms"))
                    elif kind == "kr":
                        dve.wait_ge(*after("kr_raw", l, 1))
                        sw, r = swm[0:MR], krs[:, 0:LAT]
                        dve.stream_shuffle(sw, r, mask=[p ^ 8 for p in range(32)]).then_inc(dve_chain, 1)
                        chain["dve"] += 1
                        link(TT(Em[:, 0][0:MR, 0:LAT], r, rope_m[0:MR, 0], ALU.mult))
                        link(TT(sw, sw, rope_m[0:MR, 1], ALU.mult))
                        for b in range(2):
                            TT(mkT[64:96, b, PAST:LKEY], Em[:, 0][0:MR, 0:LAT], sw, ALU.add)
                            last = dve.tensor_copy(mkT[64:96, b, LKEY:NKEY], krs[:, LAT:NTOK])
                        last.then_inc(sems["kr_ready"], 1)
                        dve.wait_ge(*own("kr_ready"))
                    elif kind == "mms" and i == 1:
                        dve.wait_ge(*filled(l, kind, i))
                        ps = slot(kind, i)
                        TS(halves(MSm[:, 1]), two(ps), 1.0 / KVL, RMS_EPS, ALU.mult, ALU.add).then_inc(sems["m_ms"], 1)
                        dve.wait_ge(*own("m_ms"))
                        dve.wait_ge(*after("m_rt", l, 1))
                        link(dve.reciprocal(MSm, MSm))
                        for k in range(3):
                            last = STT(cq[:, k], cq[:, k], qn[:, k:k + 1], MSm[:, 0], ALU.mult, ALU.mult)
                        last.then_inc(sems["c_ready"], 1)
                        dve.wait_ge(*own("c_ready"))
                        for k in range(2):
                            c = ckv[:, k, PAST:NKEY]
                            last = STT(c, c, kvn[:, k:k + 1], MSm[:, 1], ALU.mult, ALU.mult)
                        last.then_inc(sems["c_ready"], 1)
                        dve.wait_ge(*own("c_ready"))
                    elif kind == "mq":
                        dve.wait_ge(*after("mq_raw", l, i + 1))
                        sw, q = swm[64:96], mqT[64:96, i % 2, 0:LAT]
                        dve.stream_shuffle(sw, q, mask=[p ^ 8 for p in range(32)]).then_inc(dve_chain, 1)
                        chain["dve"] += 1
                        dve.wait_ge(dve_chain, chain["dve"])
                        TT(q, q, rope_m[64:96, 0], ALU.mult)
                        link(TT(sw, sw, rope_m[64:96, 1], ALU.mult))
                        TT(q, q, sw, ALU.add).then_inc(sems["mq_ready"], 1)
                        dve.wait_ge(*own("mq_ready"))
                    elif kind == "ml_score":
                        dve.wait_ge(*filled(l, kind, i))
                        softmax_max(slot(kind, i), keysn(i), st[:, i % 2, 0:1]).then_inc(sems["ml_max"], 1)
                        dve.wait_ge(*own("ml_max"))
                    elif kind == "ml_ptrans":
                        s, e, n = st[:, i % 2], Em[:, i % 2], keysn(i)
                        dve.wait_ge(*after("ml_exp", l, i + 1))
                        link(dve.reciprocal(s[:, 4:5], s[:, 2:3]))
                        TS(e[:, 0:n], e[:, 0:n], s[:, 4:5], None, ALU.mult).then_inc(sems["ml_p"], 1)
                        dve.wait_ge(*own("ml_p"))
                    elif kind == "xt":
                        dve.wait_ge(*filled(l, kind, i))
                        ps = slot(kind, i)
                        x = X[:, :, 128 * i:128 * i + 128]
                        STT(x, x, ALPHA, ps[:, 0:640].rearrange("p (a b) -> p a b", a=NT), ALU.mult, ALU.add).then_inc(sems["x_part"], 1)
                        dve.wait_ge(*own("x_part"))
                    elif kind == "ln":
                        dve.wait_ge(*after("x_part", l, 8))
                        for t in range(NT):
                            for b in range(2):
                                last = dve.bn_stats(lnst[:, t, b, :], X[:, t, 512 * b:512 * b + 512])
                        link(last)
                        for t in range(NT):
                            last = dve.bn_aggr(lnmv[:, t, :], lnst[:, t, :, :].rearrange("p a b -> p (a b)"))
                        link(last)
                        TS(lnr[:], lnmv[:, :, 1], LN_EPS, None, ALU.add).then_inc(sems["ln_var"], 1)
                        dve.wait_ge(*own("ln_var"))
                        dve.wait_ge(*after("ln_rt", l, 1))
                        link(dve.reciprocal(lnr[:], lnr[:]))
                        dve.wait_ge(ln_here, 32 * (l + 1))
                        for t in range(NT):
                            x = X[:, t, :]
                            link(TS(x, x, lnmv[:, t, 0:1], lnr[:, t:t + 1], ALU.subtract, ALU.mult))
                            link(TT(x, x, lng, ALU.mult))
                            TT(x, x, lnb, ALU.add).then_inc(sems["x_ready"], 1)
                            dve.wait_ge(*own("x_ready"))
    return nc


def keysn(u):
    return LKEY if u % NT < 4 else CTX


def two_or_one(e, n):
    return e.rearrange("p (a b) -> p a b", a=2) if n > CTX else e


def product(dve, link, TT, ALU, z, h, tb, tc):
    TT(tb, z[:, 0], h[:, 1], ALU.mult)
    link(TT(tc, z[:, 1], h[:, 1], ALU.mult))
    link(TT(z[:, 0], z[:, 0], h[:, 0], ALU.mult))
    TT(z[:, 0], z[:, 0], tc, ALU.subtract)
    link(TT(z[:, 1], z[:, 1], h[:, 0], ALU.mult))
    link(TT(z[:, 1], z[:, 1], tb, ALU.add))


def owned(kind, i):
    return {"mod": [("mod", m) for m in range(3 * KD)], "conv": [("in", T_HY + i)], "path": [("in", T_PATH + i)],
            "merge": [("in", T_MERGE + i), ("br", i)], "qk": [("in", T_Q + i)], "v": [("in", T_V + i)],
            "dqkv": [("in", T_DQ + i)], "kr": [("in", T_KR)], "wo": [("out", i)]}.get(kind, [])


def tiles(w, m=128):
    l, r, c = w.shape
    return w.reshape(l, r // 128, 128, c // m, m).transpose(0, 3, 2, 1, 4)


def columns(v):
    return v.reshape(DEPTH, -1, 128).transpose(0, 2, 1)


def laid_out(x):
    w_in = x["w_in"]
    ffn = np.stack([x["hy_ffn_b1"], x["hy_ffn_b2"], x["hy_sin_freq"][:, 0], x["hy_sin_freq"][:, 1]], -1)
    ffn = np.concatenate([ffn, np.zeros((DEPTH, 128 - HY_FFN, 4), ffn.dtype)], 1)
    return {
        "cvec": np.stack([x["c"][0], x["c_ctx"]], -1).reshape(KD, 128, 2).transpose(1, 0, 2),
        "w_mod": tiles(x["w_mod"]),
        "w_in": tiles(np.concatenate([w_in[:, :, :C_KR], w_in[:, :, C_PATH:]], -1)),
        "w_in_kr": tiles(w_in[:, :, C_KR:C_PATH], MR)[:, 0],
        "w_branch": np.stack([tiles(x["w_branch"][:, n]) for n in range(3)], 1).reshape(DEPTH, 3 * KD, 128, CT, 128),
        "w_out": tiles(x["w_out"]),
        "vecs": np.concatenate([columns(x["b_mod"]), columns(x["hy_conv_w"]), columns(x["hy_conv_b"]),
                                columns(x["hy_skip"]), ffn, columns(x["da_subln"]), columns(x["mla_q_norm"]),
                                columns(x["mla_kv_norm"])], -1),
    }


INPUTS = ["x_prompt", "x_sample", "cache_diff_k", "cache_diff_v", "cache_mla_ckv", "cache_mla_krope", "hy_ffn_w1",
          "hy_ffn_w2", "hy_ffn_w3", "hy_log_decay", "da_lambda", "mla_w_uq", "mla_w_ukv", "ln_g", "ln_b"]
OUTPUTS = [(1, CTX, D), (1, LAT, D), (1, DEPTH, CTX, 2, DAH, DHD), (1, DEPTH, CTX, DAH, DAV), (1, DEPTH, CTX, KVL),
           (1, DEPTH, CTX, MR)]


def kernel(**inputs):
    import concourse.bacc as bacc
    from concourse.bass_utils import run_bass_kernel_spmd as run

    nc = bacc.Bacc("TRN2", target_bir_lowering=False, num_devices=1)
    f32 = mybir.dt.float32
    arrays, A = {}, {}
    for name, a in [(n, inputs[n]) for n in INPUTS] + list(laid_out(inputs).items()) + list(constants().items()):
        a = np.ascontiguousarray(a)
        arrays[f"in_{name}"] = a
        A[name] = nc.dram_tensor(f"in_{name}", a.shape, mybir.dt.from_np(a.dtype), kind="ExternalInput").ap()
    outs = [nc.dram_tensor(f"out_{i}", s, f32, kind="ExternalOutput").ap() for i, s in enumerate(OUTPUTS)]
    build(nc, A, outs)
    r = run(nc, [arrays], core_ids=[0])
    return tuple(r.results[0][f"out_{i}"] for i in range(len(OUTPUTS)))
```

```python
import math
from contextlib import ExitStack

import numpy as np

import concourse.bass as bass
from concourse import mybir

DEPTH, D, LAT, CTX, PAST = 2, 1024, 512, 128, 128
NTOK = LAT + CTX
HALF = NTOK // 2
KD = D // 128
NT = NTOK // 128
HY, HY_FFN, POS = 512, 64, 33
CT = HY // 128
GRID_W = 64
DAH, DHD, DAV = 4, 64, 128
MH, MN, MR, MV = 8, 64, 32, 64
QL, KVL = 384, 256
NKEY = PAST + NTOK
LKEY = PAST + LAT
ALPHA = (2 * DEPTH) ** 0.25
LN_EPS, RMS_EPS = 1e-5, 1e-6
DA_SCALE = DHD ** -0.5
MLA_SCALE = (MN + MR) ** -0.5
T_HY, T_Q, T_K, T_V, T_DQ, T_DKV, T_KR, T_PATH, T_MERGE = 0, 12, 16, 20, 24, 27, 29, 30, 42
C_KR = 3 * HY + 3 * 512 + QL + KVL
C_PATH = C_KR + MR
D_IN = C_PATH + 3 * 512 + 3 * D
TWO_PI = 2 * math.pi
MAGIC = 1.5 * 2 ** 23
PI_HI, PI_MID = 6.28125, 0.0019350051879882812
PI_LO = TWO_PI - PI_HI - PI_MID
SLOTS = 4

VECS = [("b_mod", 3 * KD), ("hy_conv_w", 36), ("hy_conv_b", 12), ("hy_skip", 8), ("hy_ffn", 4), ("da_subln", 1),
        ("mla_q_norm", 3), ("mla_kv_norm", 2)]
NVEC = sum(n for _, n in VECS)


def vec(vecs, name):
    at = [n for n, _ in VECS].index(name)
    start = sum(n for _, n in VECS[:at])
    return vecs[:, start:start + VECS[at][1]]




def attention_steps(tag, heads, fillers, before=None):
    steps, units, taken = [], [(h, t) for h in range(heads) for t in range(NT)], 0
    for u, (h, t) in enumerate(units):
        if before and t == 2 and h + 1 < heads:
            steps += before(h + 1)
        steps.append((tag + "_score", u))
        if u >= 2 and (u - 2) % NT == NT - 1:
            steps.append((tag + "_pv", (u - 2) // NT))
        upto = len(fillers) * (u + 1) // len(units)
        steps += fillers[taken:upto]
        taken = upto
        if u >= 1:
            steps.append((tag + "_ptrans", u - 1))
    return steps + [(tag + "_ptrans", len(units) - 1), (tag + "_pv", heads - 1)]


def path_steps(n):
    return [("path", CT * n + c) for c in range(CT)]


def merge_steps(n):
    return [(kind, KD * n + d) for d in range(KD) for kind in ("mgate", "mbranch")]


def weave(a, b):
    out, taken = [], 0
    for n, step in enumerate(a):
        out.append(step)
        upto = len(b) * (n + 1) // len(a)
        out += b[taken:upto]
        taken = upto
    return out


def layer_steps():
    s = [("mod", 0)] + [("ht", f) for f in range(KD)]
    s += [("conv", 0), ("conv", 1), ("ffn", 0), ("conv", 2), ("ffn", 1), ("conv", 3)]
    for o in range(2):
        filt = [("filt", NT * o + t) for t in range(NT)]
        convs = [("conv", 4 + 4 * o + c) for c in range(4)]
        s += filt if o == 0 else weave(convs, filt)
        s += [("fdft", 5 * o + i) for i in range(5)]
        s += [("zt", 3 * o + i) for i in range(3)]
        s += [("zdft", 5 * o + i) for i in range(5)]
        s += convs if o == 0 else []
        s += [("inv", 4 * o + c) for c in range(4)]
    s += path_steps(0)
    s += [("qk", c) for c in range(8)] + [("kc", 0), ("sk", 0)]
    for c in range(4):
        s += [("v", c)]
        if c:
            s += [("vt", c - 1)]
    s += [("vt", 3)]
    s += attention_steps("da", DAH, merge_steps(0))
    s += [("dams", h) for h in range(DAH)]
    s += path_steps(1)
    s += [("dqkv", i) for i in range(5)] + [("kr", 0), ("cc", 0), ("mms", 0), ("mms", 1), ("sc", 0)]
    s += [("mv", i) for i in range(3)]
    head = lambda h: [("mq", h), ("mk", h)]
    s += head(0) + attention_steps("ml", MH, merge_steps(1), head)
    s += path_steps(2) + merge_steps(2)
    for d in range(KD):
        s += [("wo", d)]
        if d:
            s += [("xt", d - 1)]
    s += [("xt", KD - 1), ("ln", 0)]
    return s


STEPS = layer_steps()




def owned(kind, i):
    first = {"conv": T_HY, "path": T_PATH, "mgate": T_MERGE, "qk": T_Q, "v": T_V, "dqkv": T_DQ, "kr": T_KR}
    if kind == "mod":
        return [(("mod", m), None) for m in range(3 * KD)]
    if kind in first:
        return [(("in", first[kind] + i), (kind, i))]
    if kind == "mbranch":
        return [(("br", i), (kind, i))]
    return [(("out", i), (kind, i))] if kind == "wo" else []


OWNED = [own for step in STEPS for own in owned(*step)]
STREAM = [key for key, _ in OWNED]
NSTREAM = len(STREAM)
NW = 2
NMOD = 3 * KD
NSPLIT = NSTREAM - NMOD
SPLIT_AT = {key: n - NMOD for n, key in enumerate(STREAM) if n >= NMOD}


JOBS = {
    "mod": lambda i: [("mod_ready", 1)],
    "ht": lambda i: [("h_f32", i + 1)],
    "conv": lambda i: [("up_ready", i + 1)],
    "ffn": lambda i: [("farg_ready", i + 1)],
    "filt": lambda i: [("fab_ready", i + 1)],
    "fdft": lambda i: [("spec_ready", i % 5 + 1 + 10 * (i // 5))],
    "zdft": lambda i: [("spec_ready", i % 5 + 6 + 10 * (i // 5))],
    "zt": lambda i: [("zt_ready", i + 1)],
    "inv": lambda i: [("z_ready", i + 1)],
    "path": lambda i: [("br_f32", i + 1)],
    "mgate": lambda i: [("th_ready", 12 * (i // 8) + i % 8 + 5)],
    "mbranch": lambda i: [("gate_used", 12 * (i // 8) + i % 8 + 5)],
    "qk": lambda i: [("raw_ready", i + 1)],
    "kc": lambda i: [("kc_ready", 1)],
    "sk": lambda i: [("sk_ready", 1)],
    "v": lambda i: [("raw_ready", 9 + i)],
    "vt": lambda i: [("v_ready", i + 1)],
    "da_score": lambda u: [("da_exp", 2 * u + 1), ("da_exp", 2 * u + 2)],
    "da_ptrans": lambda u: [("da_pt", u + 1)],
    "da_pv": lambda h: [("da_o", h + 1)],
    "dams": lambda h: [("da_ms", h + 1)],
    "dqkv": lambda i: [("c_raw", i + 1)],
    "kr": lambda i: [("kr_raw", 1)],
    "cc": lambda i: [("cc_ready", 2)],
    "mms": lambda i: [("m_ms", i + 1)],
    "sc": lambda i: [("sc_ready", 1)],
    "mv": lambda i: [("mv_ready", i + 1)],
    "mq": lambda h: [("mq_raw", h + 1)],
    "mk": lambda h: [("mk_ready", h + 1)],
    "ml_score": lambda u: [("ml_exp", u + 1)],
    "ml_ptrans": lambda u: [("ml_pt", u + 1)],
    "ml_pv": lambda h: [("ml_o", h + 1)],
    "wo": lambda d: [("r_ready", d + 1)],
    "xt": lambda d: [("x_part", d + 1)],
    "ln": lambda d: [],
}
PER = dict(mod_ready=1, h_f32=8, h_hi=8, h_ready=8, br_f32=12, br_hi=12, mg_hi=8, mg_ready=8,
           mod_used=3 * KD - 1, w_hi=NSPLIT, w_lo=NSPLIT, up_ready=12, conv_ready=12, farg_ready=2, hid_ready=2, decay_ready=10,
           fab_ready=10, odd_ready=20, spec_ready=20, zt_ready=6, y_ready=2, z_ready=8, th_ready=36, gate_used=36,
           raw_ready=12, qk_ready=8, kc_ready=1, sk_ready=1, v_ready=4, da_max=40, da_exp=40, da_p=20, da_pt=20,
           da_o=4, da_sq=4, da_ms=4, da_rt=1, c_raw=5, c_sq=5, kr_raw=1, cc_ready=2, kr_ready=1, m_ms=2, m_rt=1,
           pad_ready=1, lam_sum=1, lam_exp=1, c_ready=2, sc_ready=1, mv_ready=3, mq_raw=8, mq_ready=8, mk_ready=8, ml_max=40, ml_exp=40, ml_p=40,
           ml_pt=40, ml_o=8, r_ready=8, x_part=8, ln_var=1, ln_rt=1, x_ready=5)


def slot_table():
    table, at, uses, last = {}, 0, [0] * SLOTS, [None] * SLOTS
    for kind, i in STEPS:
        for j, freed in enumerate(JOBS[kind](i)):
            s = at % SLOTS
            table[kind, i, j] = (s, uses[s], last[s])
            last[s] = freed
            uses[s] += 1
            at += 1
    return table, uses

SLOT, USES = slot_table()


def split_upto(kind, i):
    if kind == "ht":
        return 1
    if kind == "mod" or not owned(kind, i):
        return 0
    return min(NSPLIT, SPLIT_AT[owned(kind, i)[0][0]] + 2)


def constants():
    f = np.float32
    pos_row = np.repeat(np.arange(LAT // GRID_W), GRID_W).astype(f)
    pos_col = np.tile(np.arange(GRID_W), LAT // GRID_W).astype(f)

    def rope(dim, reps):
        q = dim // 4
        freqs = (1.0 / (np.float32(10000.0) ** (np.arange(q, dtype=f) / q))).astype(f)
        cos, sin = [], []
        for pos in (pos_row, pos_col):
            ang = (pos[None, :] * freqs[:, None]).astype(f)
            cos += [np.cos(ang), np.cos(ang)]
            sin += [-np.sin(ang), np.sin(ang)]
        one = np.stack([np.concatenate(cos), np.concatenate(sin)], 1).astype(f)
        return np.tile(one, (reps, 1, 1))

    def feats(n):
        t = np.arange(n, dtype=f)
        ang = (f(TWO_PI / n) * t[:, None] * np.arange(1, 17, dtype=f)).astype(f)
        lin = t / f(n - 1)
        return np.concatenate([lin[:, None], np.cos(ang), -np.sin(ang)], -1).T.astype(f), lin

    f_lat, lin_lat = feats(LAT)
    f_ctx, lin_ctx = feats(CTX)
    u = np.arange(128)
    tok = [2 * (128 * half + u) + par for par in range(2) for half in range(2)]
    negt = np.stack([-lin_lat[t] for t in tok] + [-lin_ctx], 1).astype(f)
    mask = np.ones((128, NT), f)
    mask[0, 0] = mask[0, 4] = 0.0
    k = np.arange(256)
    ang = lambda t: np.pi * np.outer(t, 2 * k + 1) / 1024
    fwd = np.stack([np.stack([np.cos(ang(t)), np.sin(ang(t))], 1) for t in tok], 1).astype(f)
    angc = np.pi * np.outer(u, 2 * u + 1) / 256
    fwdc = np.stack([np.cos(angc), np.sin(angc)], 1).astype(f)
    inv = np.zeros((128, 2, 2, 512), f)
    for m in range(2):
        for q, fn in enumerate((np.cos, np.sin)):
            for par in range(2):
                t = 2 * np.arange(256) + par
                inv[:, m, q, 256 * par:256 * par + 256] = fn(
                    np.pi * np.outer(2 * (128 * m + u) + 1, t) / 1024) / 512
    invc = np.stack([fn(np.pi * np.outer(2 * u + 1, u) / 256) / 128 for fn in (np.cos, np.sin)], 1).astype(f)
    lam = np.stack([[0.8 - 0.6 * math.exp(-0.3 * l), 0.2 + 0.6 * math.exp(-0.3 * l)] for l in range(DEPTH)])
    return {
        "ident": np.eye(128, dtype=f), "ones": np.ones((128, 128), f),
        "rope_da": rope(DHD, 2), "rope_m": rope(MR, 1),
        "feats": np.concatenate([f_lat, f_ctx], 1), "negt": negt, "hmask": mask,
        "fwd": fwd, "fwdc": fwdc, "inv": inv, "invc": invc, "lam_init": lam.astype(f),
    }


def build(nc, A, O):
    f32, f32r = mybir.dt.float32, mybir.dt.float32r
    ALU = mybir.AluOpType
    ACT = mybir.ActivationFunctionType
    AX = mybir.AxisListType.X
    o_prompt, o_sample, o_k, o_v, o_ckv, o_kr = O
    x_mid = nc.dram_tensor("x_mid", (128, NT * D), f32, kind="Internal").ap()

    ctx = ExitStack()
    with ctx:
        at = [(nc.sbuf_base + 31) // 32 * 32]

        def sb(name, shape, dtype=f32, over=None):
            if over is None:
                over = at[0]
                at[0] += -(-int(np.prod(shape[1:])) * 4 // 32) * 32
                assert at[0] <= nc.sbuf_usable_end, name
            return nc.alloc_sbuf_tensor_at(name, shape, dtype, offset=over)

        Hh = sb("Hh", [128, KD, NTOK], f32r)
        Hl = sb("Hl", [128, KD, NTOK], f32r)
        W = sb("W", [128, NW, KD, 128])
        Wh = sb("Wh", [128, 2, KD, 128], f32r)
        Wl = sb("Wl", [128, 2, KD, 128], f32r)
        MG = sb("MG", [128, KD * NTOK])
        br_at = at[0]
        BRh = sb("BRh", [128, CT, NTOK], f32r)
        BRl = sb("BRl", [128, CT, NTOK], f32r)
        BR = sb("BR", [128, 2 * CT * NTOK], over=br_at)
        raw = sb("raw", [128, 2, 644])
        th = sb("th", [128, 2, NTOK])
        ident = sb("ident", [128, 128])
        ones = sb("ones", [128, 128])
        rope_da = sb("rope_da", [128, 2, LAT])
        rope_m = sb("rope_m", [96, 2, LAT])
        negt = sb("negt", [128, NT])
        hmask = sb("hmask", [128, NT])
        ccol = sb("ccol", [128, KD, 2])
        csig = sb("csig", [128, KD, 2])
        modc = sb("modc", [128, 3 * KD, 2])
        vecs = sb("vecs", [128, NVEC])
        bmod = vec(vecs, "b_mod")
        convw = vec(vecs, "hy_conv_w").rearrange("p (a b) -> p a b", a=3)
        convb = vec(vecs, "hy_conv_b")
        skip = vec(vecs, "hy_skip").rearrange("p (a b) -> p a b", a=2)
        fvec = vec(vecs, "hy_ffn")[0:HY_FFN]
        subln = vec(vecs, "da_subln")
        qn = vec(vecs, "mla_q_norm")
        kvn = vec(vecs, "mla_kv_norm")
        fw1 = sb("fw1", [POS, HY_FFN])
        fw2 = sb("fw2", [HY_FFN, HY_FFN])
        lp = sb("lp", [128, 4, DHD])
        lpj = sb("lpj", [128, 2, DHD])
        lamc = sb("lamc", [128, 8])
        st = sb("st", [128, 2, 8])
        lnst = sb("lnst", [128, NT, 2, 6])
        lnmv = sb("lnmv", [128, NT, 2])
        lnr = sb("lnr", [128, NT])
        work_at = at[0]
        WORK = 20640
        work = sb("work", [128, WORK])

        def area(base, off, *dims):
            n = int(np.prod(dims))
            ap = base[:, off:off + n]
            if len(dims) == 1:
                return ap
            names = "abcd"[:len(dims)]
            return ap.rearrange(f"p ({' '.join(names)}) -> p {' '.join(names)}",
                                **{c: d for c, d in zip(names, dims)})

        ZP = LAT + 2
        V4 = area(work, 0, CT, 642)
        G4 = area(work, 2568, CT, 642)
        feats = area(work, 2568, NTOK)[0:POS]
        rr = area(work, 3208, 2, NTOK)[0:HY_FFN]
        zT = area(work, 5136, NT, HY)
        tB, tC = area(work, 5136, 1024), area(work, 6160, 1024)
        PM = area(work, 7696, 2, 2, 1024)
        PMc = area(work, 11792, 2, HY)
        fab = area(work, 7696, 2, NT, HY)
        HS = area(work, 12816, 2, 2, 1024)
        HSc = area(work, 16912, 2, HY)
        decay = area(work, 17936, 2, HY)
        oddb = area(work, 18960, 2, HY)
        fwdc = area(work, 19984, 2, 128)
        invc = area(work, 20240, 2, 128)
        w3 = area(BR, 0, 2, 2, HY)[0:HY_FFN]
        expld = area(BR, 2048, 2, 2, HY)
        hid = area(BR, 4096, NTOK)[0:HY_FFN]
        fwd = area(MG, 0, 4, 2, 256)
        inv = area(MG, 2048, 2, 2, 512)
        tconv = area(MG, 4096, 642)
        qT = area(work, 0, 4, NTOK)
        MS = area(work, 0, 4, NTOK)
        kT = area(work, 2560, 4, NKEY)
        V = area(work, 5632, 6, 512)
        E = area(work, 8704, 2, 2, NTOK)
        sqd = area(work, 8704, 4, NTOK)
        PT = area(work, 11264, NT, LAT)
        PTc = area(work, 13824, 2, 128)
        OT = area(work, 14080, 4, NTOK)
        ckc = area(work, 16640, 512)
        stk = area(work, 17152, 512)
        swp = area(work, 17664, LAT)
        Y = area(work, 0, 4, NTOK)
        cq = area(work, 2560, 3, NTOK)
        ckv = area(work, 4480, 2, NKEY)
        Vm = area(work, 6016, 6, 512)
        mqT = area(work, 9088, 2, NTOK)
        mkT = area(work, 10368, 2, NKEY)
        wuq = area(work, 11904, 3, 768)
        wukv = area(work, 14208, 2, 1024)
        Em = area(work, 16256, 2, NTOK)
        PTm = area(work, 17536, NT, LAT)
        PTmc = area(work, 20096, 2, 128)
        stc = area(work, 20352, KVL + MR)
        sqm = area(work, 16256, 3, NTOK)
        MSm = area(work, 18176, 2, NTOK)
        cc = area(work, 19456, KVL)
        ckr = area(work, 19712, MR)
        krs = raw[0:MR, 0, 0:NTOK]
        swm = raw[:, 1, 0:LAT]
        krt = Vm[0:MR, 0, 0:LAT]
        X = area(work, 0, NT, D)
        lng = area(work, 5120, D)
        lnb = area(work, 6144, D)
        MGh = sb("MGh", [128, KD, NTOK], f32r, over=work_at + 4 * 7168)
        MGl = sb("MGl", [128, KD, NTOK], f32r, over=work_at + 4 * 12288)
        rT = raw

        PS = [ctx.enter_context(nc.psum_tensor(f"PS{i}", [128, 1024], f32)) for i in range(SLOTS)]

        sems = {}

        def sem(name):
            sems[name] = ctx.enter_context(nc.semaphore(name))
            return sems[name]

        for name in PER:
            sem(name)
        full = [sem(f"psum_full{i}") for i in range(SLOTS)]
        w_here = [sem(f"weights_here{i}") for i in range(NW)]
        x_saved = sem("x_saved")
        consts_here = sem("consts_here")
        x_here = sem("x_here")
        small_here = sem("small_here")
        hy_here = sem("hyena_tables_here")
        da_here = sem("da_cache_here")
        ml_here = sem("mla_weights_here")
        ln_here = sem("ln_weights_here")
        c_sig = sem("c_sig")
        c_silu = sem("c_silu")
        store_k = sem("store_k")
        store_c = sem("store_c")
        store_y = sem("store_y")
        act_chain = sem("act_chain")
        dve_chain = sem("dve_chain")
        chain = {"act": 0, "dve": 0}

        def after(name, l, count):
            return sems[name], l * PER[name] + count

        def filled(l, kind, i, j=0):
            s, u, _ = SLOT[kind, i, j]
            return full[s], l * USES[s] + u + 1

        def full_of(kind, i, j=0):
            return full[SLOT[kind, i, j][0]]

        def freed(l, kind, i, j=0):
            before = SLOT[kind, i, j][2]
            if before:
                return after(before[0], l, before[1])
            return after("x_ready", l - 1, 5) if l else (consts_here, 16 * 8)

        def tile_done(l, n):
            l, n = (l, n) if n >= 0 else (l - 1, n + NSPLIT)
            return filled(l, *OWNED[NMOD + n][1])

        def slot(kind, i, j=0):
            return PS[SLOT[kind, i, j][0]]

        def halves(ap):
            return ap.rearrange("p (a b) -> p a b", a=2)

        def two(ps, n=HALF, p=128):
            return ps[0:p, :].rearrange("p (a b) -> p a b", a=2)[:, :, 0:n]

        block = ctx.enter_context(nc.Block())

        N_SMALL, N_HY, N_DA, N_ML, N_LN = 5, 7, 2, 4, 2

        @block.sync
        def _(sp):
            def weight(l, n):
                kind, i = STREAM[n]
                g = l * NSTREAM + n
                if g >= NW:
                    before = (n - NW) % NSTREAM
                    lb = l if n >= NW else l - 1
                    if before >= NMOD:
                        sp.wait_ge(*after("w_lo", lb, before - NMOD + 1))
                    elif before < NMOD - 1:
                        sp.wait_ge(*after("mod_used", lb, before + 1))
                    else:
                        sp.wait_ge(*filled(lb, "mod", 0))
                src = A[{"mod": "w_mod", "in": "w_in", "br": "w_branch", "out": "w_out"}[kind]][l, i]
                sp.dma_start(W[:, g % NW, 0:src.shape[1], :], src).then_inc(w_here[g % NW], 16)

            sp.dma_start(csig[:], A["cvec"]).then_inc(consts_here, 16)
            for t, s in ((ident, "ident"), (ones, "ones"), (rope_da, "rope_da"), (negt, "negt"), (hmask, "hmask")):
                sp.dma_start(t[:], A[s]).then_inc(consts_here, 16)
            sp.dma_start(rope_m[0:MR], A["rope_m"]).then_inc(consts_here, 16)
            sp.dma_start(rope_m[64:96], A["rope_m"]).then_inc(consts_here, 16)
            def load_x(l):
                if l == 0:
                    sp.dma_start(X[:, 0:4, :], A["x_sample"][0].rearrange("(t p) d -> p t d", p=128))\
                      .then_inc(x_here, 16)
                    sp.dma_start(X[:, 4, :], A["x_prompt"][0]).then_inc(x_here, 16)
                else:
                    sp.dma_start(X, x_mid.rearrange("p (t d) -> p t d", t=NT)).then_inc(x_here, 32)

            load_x(0)

            for l in range(DEPTH):
                if l:
                    sp.wait_ge(*after("x_ready", l - 1, 5))
                small = [(vecs[:], A["vecs"][l]), (fw1[:], A["hy_ffn_w1"][l]), (fw2[:], A["hy_ffn_w2"][l]),
                         (lp[:].rearrange("p a b -> p (a b)"),
                          A["da_lambda"][l].rearrange("a b -> (a b)").partition_broadcast(128)),
                         (lamc[:, 0:2], A["lam_init"][l].partition_broadcast(128))]
                assert len(small) == N_SMALL
                for dst, src in small:
                    sp.dma_start(dst, src).then_inc(small_here, 16)
                for dst, src in ((fwd, A["fwd"]), (inv, A["inv"]),
                                 (w3.rearrange("p a b c -> p (a b c)"), A["hy_ffn_w3"][l]),
                                 (expld.rearrange("p a b c -> p (a b c)"),
                                  A["hy_log_decay"][l].partition_broadcast(128))):
                    sp.dma_start(dst, src).then_inc(hy_here, 16)
                if l:
                    sp.dma_start(x_mid.rearrange("p (t d) -> p t d", t=NT), X).then_inc(x_saved, 16)
                n = 0
                for kind, i in STEPS:
                    if (kind, i) == ("ffn", 0):
                        sp.wait_ge(*after("h_f32", l, KD))
                        if l:
                            sp.wait_ge(x_saved, 16)
                        for dst, src in ((fwdc, A["fwdc"]), (invc, A["invc"]), (feats, A["feats"])):
                            sp.dma_start(dst, src).then_inc(hy_here, 16)
                    if (kind, i) == ("qk", 3):
                        sp.wait_ge(*after("gate_used", l, 4))
                        sp.dma_start(ckc, A["cache_diff_k"][0, l].rearrange("t a h d -> t (a h d)"))\
                          .then_inc(da_here, 16)
                        sp.dma_start(V[:, 0, :], A["cache_diff_v"][0, l].rearrange("t h d -> t (h d)"))\
                          .then_inc(da_here, 16)
                    if (kind, i) == ("mbranch", 2):
                        sp.wait_ge(*after("sk_ready", l, 1))
                        sp.wait_ge(*after("v_ready", l, 4))
                        sp.dma_start(o_k[0, l].rearrange("t a h d -> t (a h d)"), stk).then_inc(store_k, 16)
                        sp.dma_start(o_v[0, l].rearrange("t h d -> t (h d)"), V[:, 5, :]).then_inc(store_k, 16)
                    if (kind, i) == ("dqkv", 3):
                        sp.wait_ge(*after("gate_used", l, 16))
                        sp.wait_ge(store_k, 32 * (l + 1))
                        for dst, src in ((wuq, A["mla_w_uq"][l].rearrange("(k p) n -> p k n", p=128)),
                                         (wukv, A["mla_w_ukv"][l].rearrange("(k p) n -> p k n", p=128)),
                                         (cc, A["cache_mla_ckv"][0, l]), (ckr, A["cache_mla_krope"][0, l])):
                            sp.dma_start(dst, src).then_inc(ml_here, 16)
                    if (kind, i) == ("mbranch", KD + 2):
                        sp.wait_ge(*after("sc_ready", l, 1))
                        sp.dma_start(o_ckv[0, l], stc[:, 0:KVL]).then_inc(store_c, 16)
                        sp.dma_start(o_kr[0, l], stc[:, KVL:KVL + MR]).then_inc(store_c, 16)
                    if (kind, i) == ("mgate", 2 * KD + 3):
                        sp.wait_ge(*after("gate_used", l, 28))
                        sp.dma_start(lng, A["ln_g"][l].partition_broadcast(128)).then_inc(ln_here, 16)
                        sp.dma_start(lnb, A["ln_b"][l].partition_broadcast(128)).then_inc(ln_here, 16)
                        load_x(l)
                        sp.wait_ge(store_c, 32 * (l + 1))
                    for _ in owned(kind, i):
                        weight(l, n)
                        n += 1
                assert n == NSTREAM
            sp.wait_ge(*after("x_ready", DEPTH - 1, 5))
            sp.dma_start(o_sample[0].rearrange("(t p) d -> p t d", p=128), X[:, 0:4, :]).then_inc(store_y, 16)
            sp.dma_start(o_prompt[0], X[:, 4, :]).then_inc(store_y, 16)
            sp.wait_ge(store_y, 32)

        @block.tensor
        def _(pe):
            def project(l, kind, i, key, xh, xl, k):
                n = SPLIT_AT[key]
                b = n % 2
                pe.wait_ge(*after("w_lo", l, n + 1))
                pe.wait_ge(*freed(l, kind, i))
                ps = slot(kind, i)
                for a in range(2):
                    t = slice(HALF * a, HALF * a + HALF)
                    for kk in range(k):
                        for part, (w, x) in enumerate(((Wh, xh), (Wh, xl), (Wl, xh))):
                            last = pe.matmul(ps[:, 512 * a:512 * a + HALF], w[:, b, kk, :], x[:, kk, t],
                                             start=kk + part == 0, stop=kk == k - 1 and part == 2)
                last.then_inc(full_of(kind, i), 1)

            def transpose(out, in_, p=128):
                return pe.transpose(out, in_, ident[0:p, 0:p])

            def dft(l, kind, i, srcs):
                pe.wait_ge(*freed(l, kind, i))
                ps = slot(kind, i)
                if i % 5 < 4:
                    q, m = divmod(i % 5, 2)
                    for par in range(2):
                        for half in range(2):
                            t = 2 * par + half
                            last = pe.matmul(ps[:, 512 * par:512 * par + HY], fwd[:, t, q, 128 * m:128 * m + 128],
                                             srcs[q][:, t, :], start=half == 0, stop=half == 1)
                else:
                    for q in range(2):
                        last = pe.matmul(ps[:, 512 * q:512 * q + HY], fwdc[:, q, :], srcs[q][:, 4, :],
                                         start=True, stop=True)
                last.then_inc(full_of(kind, i), 1)

            def keys(t):
                return (0, LKEY) if t < 4 else (LKEY, CTX)

            def scores(ps, q, k, t):
                k0, n = keys(t)
                if t == 4:
                    return pe.matmul(ps[:, 0:n], q[:, 128 * t:128 * t + 128], k[:, k0:k0 + n], start=True, stop=True)
                for a in range(2):
                    last = pe.matmul(ps[:, 512 * a:512 * a + HALF], q[:, 128 * t:128 * t + 128],
                                     k[:, HALF * a:HALF * a + HALF], start=True, stop=True)
                return last

            def ptrans(l, kind, u, P):
                pe.wait_ge(*freed(l, kind, u))
                ps = slot(kind, u)
                for kt in range(NT if u % NT < 4 else 1):
                    last = transpose(ps[:, 128 * kt:128 * kt + 128], P[:, 128 * kt:128 * kt + 128])
                last.then_inc(full_of(kind, u), 1)

            def values(l, kind, h, v, c0, m, pt, ptc):
                pe.wait_ge(*freed(l, kind, h))
                ps = slot(kind, h)
                for kt in range(NT):
                    pe.matmul(ps[0:m, 0:LAT], v[:, kt, c0:c0 + m], pt[:, kt, :], start=kt == 0, stop=kt == NT - 1)
                pe.matmul(ps[0:m, LAT:NTOK], v[:, 5, c0:c0 + m], ptc, start=True, stop=True).then_inc(full_of(kind, h), 1)

            pe.wait_ge(consts_here, 16 * 8)
            pe.wait_ge(c_silu, 1)
            for l in range(DEPTH):
                if l:
                    pe.wait_ge(*after("x_ready", l - 1, 5))
                    pe.wait_ge(store_c, 32 * l)
                for kind, i in STEPS:
                    if kind == "mod":
                        pe.wait_ge(*freed(l, kind, i))
                        ps = slot(kind, i)
                        for m in range(3 * KD):
                            g = l * NSTREAM + m
                            pe.wait_ge(w_here[g % NW], 16 * (g // NW + 1))
                            for k in range(KD):
                                last = pe.matmul(ps[:, 2 * m:2 * m + 2], W[:, g % NW, k, :], ccol[:, k, :],
                                                 start=k == 0, stop=k == KD - 1)
                            if m < NMOD - 1:
                                last.then_inc(sems["mod_used"], 1)
                        last.then_inc(full_of(kind, i), 1)
                    elif kind == "ht":
                        pe.wait_ge(*freed(l, kind, i))
                        ps = slot(kind, i)
                        if l == 0 and i == 0:
                            pe.wait_ge(x_here, 32)
                        for t in range(NT):
                            last = transpose(ps[:, 128 * t:128 * t + 128], X[:, t, 128 * i:128 * i + 128])
                        last.then_inc(full_of(kind, i), 1)
                    elif kind == "conv":
                        if i == 0:
                            pe.wait_ge(*after("h_ready", l, 8))
                        project(l, kind, i, ("in", T_HY + i), Hh, Hl, KD)
                    elif kind == "ffn":
                        pe.wait_ge(*freed(l, kind, i))
                        ps = slot(kind, i)
                        if i == 0:
                            pe.wait_ge(small_here, 16 * N_SMALL * (l + 1))
                            pe.wait_ge(hy_here, 16 * N_HY * (l + 1))
                        else:
                            pe.wait_ge(*after("hid_ready", l, 1))
                        for a in range(2):
                            last = pe.matmul(ps[0:HY_FFN, 512 * a:512 * a + HALF], (fw2 if i else fw1)[:],
                                             (hid if i else feats)[:, HALF * a:HALF * a + HALF], start=True, stop=True)
                        last.then_inc(full_of(kind, i), 1)
                    elif kind == "filt":
                        o, t = divmod(i, NT)
                        pe.wait_ge(*freed(l, kind, i))
                        ps = slot(kind, i)
                        if i == 0:
                            pe.wait_ge(*after("hid_ready", l, 2))
                        par, half = divmod(t, 2)
                        hcol = (hid[:, 256 * half + par:256 * half + par + 255:2] if t < 4
                                else hid[:, LAT:NTOK])
                        for d in range(2):
                            last = pe.matmul(ps[:, 512 * d:512 * d + HY], hcol, w3[:, d, o, :], start=True, stop=True)
                        last.then_inc(full_of(kind, i), 1)
                    elif kind == "fdft":
                        if i % 5 == 0:
                            pe.wait_ge(*after("fab_ready", l, 5 * (i // 5) + 5))
                        dft(l, kind, i, (fab[:, 0], fab[:, 1]))
                    elif kind == "zt":
                        o, r = divmod(i, 3)
                        pe.wait_ge(*freed(l, kind, i))
                        ps = slot(kind, i)
                        if i == 0:
                            pe.wait_ge(*after("conv_ready", l, 4))
                        elif r == 0:
                            pe.wait_ge(*after("z_ready", l, 4 * o))
                        for b in range(2 if r < 2 else 1):
                            for c in range(CT):
                                src = (V4[:, c, 256 * b + r:256 * b + r + 255:2] if r < 2
                                       else V4[:, c, ZP:ZP + CTX])
                                last = transpose(ps[:, 512 * b + 128 * c:512 * b + 128 * c + 128], src)
                        last.then_inc(full_of(kind, i), 1)
                    elif kind == "zdft":
                        if i % 5 == 0:
                            pe.wait_ge(*after("zt_ready", l, 3 * (i // 5) + 3))
                        dft(l, kind, i, (zT, zT))
                    elif kind == "inv":
                        o, c = divmod(i, CT)
                        pe.wait_ge(*freed(l, kind, i))
                        ps = slot(kind, i)
                        if c == 0:
                            pe.wait_ge(*after("y_ready", l, o + 1))
                        for par in range(2):
                            for n_ in range(4):
                                q, m = divmod(n_, 2)
                                pe.matmul(ps[:, 256 * par:256 * par + 256],
                                          PM[:, par, q, 512 * m + 128 * c:512 * m + 128 * c + 128],
                                          inv[:, m, q, 256 * par:256 * par + 256], start=n_ == 0, stop=n_ == 3)
                        for q in range(2):
                            last = pe.matmul(ps[:, 512:640], PMc[:, q, 128 * c:128 * c + 128], invc[:, q, :],
                                             start=q == 0, stop=q == 1)
                        last.then_inc(full_of(kind, i), 1)
                    elif kind == "path":
                        project(l, kind, i, ("in", T_PATH + i), Hh, Hl, KD)
                    elif kind == "mgate":
                        project(l, kind, i, ("in", T_MERGE + i), Hh, Hl, KD)
                    elif kind == "mbranch":
                        if i % KD == 0:
                            pe.wait_ge(*after("gate_used", l, 12 * (i // KD) + 4))
                        project(l, kind, i, ("br", i), BRh, BRl, CT)
                    elif kind == "qk":
                        project(l, kind, i, ("in", T_Q + i), Hh, Hl, KD)
                    elif kind == "kc":
                        pe.wait_ge(*freed(l, kind, i))
                        ps = slot(kind, i)
                        pe.wait_ge(da_here, 16 * N_DA * (l + 1))
                        for c in range(4):
                            last = transpose(ps[:, 128 * c:128 * c + 128], ckc[:, 128 * c:128 * c + 128])
                        last.then_inc(full_of(kind, i), 1)
                    elif kind == "sk":
                        pe.wait_ge(*freed(l, kind, i))
                        ps = slot(kind, i)
                        pe.wait_ge(*after("qk_ready", l, 8))
                        for c in range(4):
                            last = transpose(ps[:, 128 * c:128 * c + 128], kT[:, c, LKEY:NKEY])
                        last.then_inc(full_of(kind, i), 1)
                    elif kind == "v":
                        project(l, kind, i, ("in", T_V + i), Hh, Hl, KD)
                    elif kind == "vt":
                        pe.wait_ge(*freed(l, kind, i))
                        ps = slot(kind, i)
                        pe.wait_ge(*after("raw_ready", l, 9 + i))
                        for t in range(NT):
                            last = transpose(ps[:, 128 * t:128 * t + 128], raw[:, i % 2, 128 * t:128 * t + 128])
                        last.then_inc(full_of(kind, i), 1)
                    elif kind == "da_score":
                        h, t = divmod(i, NT)
                        if i == 0:
                            pe.wait_ge(*after("kc_ready", l, 1))
                        p = 64 * (h % 2)
                        for j in range(2):
                            pe.wait_ge(*freed(l, kind, i, j))
                            ps = slot(kind, i, j)
                            last = scores(ps, qT[p:p + 64, 2 * j + h // 2], kT[p:p + 64, 2 * j + h // 2], t)
                            last.then_inc(full_of(kind, i, j), 1)
                    elif kind == "da_ptrans":
                        pe.wait_ge(*after("da_p", l, i + 1))
                        ptrans(l, kind, i, E[:, i % 2, 0])
                    elif kind == "da_pv":
                        if i == 0:
                            pe.wait_ge(*after("v_ready", l, 4))
                        pe.wait_ge(*after("da_pt", l, NT * (i + 1)))
                        values(l, kind, i, V, 128 * i, 128, PT, PTc[:, i % 2])
                    elif kind == "dams":
                        pe.wait_ge(*freed(l, kind, i))
                        ps = slot(kind, i)
                        pe.wait_ge(*after("da_sq", l, i + 1))
                        for a in range(2):
                            last = pe.matmul(ps[:, 512 * a:512 * a + HALF], ones[:],
                                             sqd[:, i, HALF * a:HALF * a + HALF], start=True, stop=True)
                        last.then_inc(full_of(kind, i), 1)
                    elif kind == "dqkv":
                        project(l, kind, i, ("in", T_DQ + i), Hh, Hl, KD)
                    elif kind == "kr":
                        project(l, kind, i, ("in", T_KR), Hh, Hl, KD)
                    elif kind == "cc":
                        pe.wait_ge(*freed(l, kind, i))
                        ps = slot(kind, i)
                        pe.wait_ge(ml_here, 16 * N_ML * (l + 1))
                        for c in range(2):
                            transpose(ps[:, 128 * c:128 * c + 128], cc[:, 128 * c:128 * c + 128])
                        transpose(ps[0:MR, 512:640], ckr).then_inc(full_of(kind, i), 1)
                    elif kind == "mms":
                        pe.wait_ge(*freed(l, kind, i))
                        ps = slot(kind, i)
                        pe.wait_ge(*after("c_sq", l, 3 if i == 0 else 5))
                        k = 3 - i
                        for a in range(2):
                            for kk in range(k):
                                last = pe.matmul(ps[:, 512 * a:512 * a + HALF], ones[:],
                                                 sqm[:, kk, HALF * a:HALF * a + HALF], start=kk == 0, stop=kk == k - 1)
                        last.then_inc(full_of(kind, i), 1)
                    elif kind == "sc":
                        pe.wait_ge(*freed(l, kind, i))
                        ps = slot(kind, i)
                        pe.wait_ge(*after("c_ready", l, 2))
                        for c in range(2):
                            transpose(ps[:, 128 * c:128 * c + 128], ckv[:, c, LKEY:NKEY])
                        transpose(ps[:, 512:512 + MR], krs[:, LAT:NTOK], MR).then_inc(full_of(kind, i), 1)
                    elif kind == "mv":
                        pe.wait_ge(*freed(l, kind, i))
                        ps = slot(kind, i)
                        for b in range(2):
                            t = 2 * i + b
                            for k in range(2):
                                last = pe.matmul(
                                    ps[:, 512 * b:512 * b + 512], ckv[:, k, 128 * t:128 * t + 128],
                                    wukv[:, k, :].rearrange("p (h e) -> p h e", h=MH)[:, :, MN:MN + MV],
                                    start=k == 0, stop=k == 1)
                        last.then_inc(full_of(kind, i), 1)
                    elif kind == "mq":
                        pe.wait_ge(*freed(l, kind, i))
                        ps = slot(kind, i)
                        for a in range(2):
                            for k in range(3):
                                last = pe.matmul(ps[0:96, 512 * a:512 * a + HALF], wuq[:, k, 96 * i:96 * i + 96],
                                                 cq[:, k, HALF * a:HALF * a + HALF], start=k == 0, stop=k == 2)
                        last.then_inc(full_of(kind, i), 1)
                    elif kind == "mk":
                        pe.wait_ge(*freed(l, kind, i))
                        ps = slot(kind, i)
                        n_ = NKEY // 2
                        for a in range(2):
                            for k in range(2):
                                last = pe.matmul(ps[0:MN, 512 * a:512 * a + n_], wukv[:, k, 128 * i:128 * i + MN],
                                                 ckv[:, k, n_ * a:n_ * a + n_], start=k == 0, stop=k == 1)
                        last.then_inc(full_of(kind, i), 1)
                    elif kind == "ml_score":
                        h, t = divmod(i, NT)
                        pe.wait_ge(*freed(l, kind, i))
                        ps = slot(kind, i)
                        if t == 0:
                            pe.wait_ge(*after("mq_ready", l, h + 1))
                            pe.wait_ge(*after("mk_ready", l, h + 1))
                            pe.wait_ge(*after("kr_ready", l, 1))
                        scores(ps, mqT[0:96, h % 2], mkT[0:96, h % 2], t).then_inc(full_of(kind, i), 1)
                    elif kind == "ml_ptrans":
                        pe.wait_ge(*after("ml_p", l, i + 1))
                        ptrans(l, kind, i, Em[:, i % 2])
                    elif kind == "ml_pv":
                        if i == 0:
                            pe.wait_ge(*after("mv_ready", l, 3))
                        pe.wait_ge(*after("ml_pt", l, NT * (i + 1)))
                        values(l, kind, i, Vm, MV * i, MV, PTm, PTmc[:, i % 2])
                    elif kind == "wo":
                        if i == 0:
                            pe.wait_ge(*after("mg_ready", l, KD))
                        project(l, kind, i, ("out", i), MGh, MGl, KD)
                    elif kind == "xt":
                        pe.wait_ge(*freed(l, kind, i))
                        ps = slot(kind, i)
                        pe.wait_ge(*after("r_ready", l, i + 1))
                        for t in range(NT):
                            last = transpose(ps[:, 128 * t:128 * t + 128], rT[:, i % 2, 128 * t:128 * t + 128])
                        last.then_inc(full_of(kind, i), 1)

        @block.scalar
        def _(act):
            def link(ins):
                chain["act"] += 1
                ins.then_inc(act_chain, 1)
                act.wait_ge(act_chain, chain["act"])

            def copy(out, in_, scale=1.0):
                return act.activation(out, in_, ACT.Copy, scale=scale)

            act.wait_ge(consts_here, 16 * 8)
            act.activation(ccol[:], csig[:], ACT.Sigmoid).then_inc(c_sig, 1)

            def high_part(l, n):
                g = l * NSTREAM + NMOD + n
                act.wait_ge(w_here[g % NW], 16 * (g // NW + 1))
                if l or n >= 2:
                    act.wait_ge(*tile_done(l, n - 2))
                k = CT if STREAM[NMOD + n][0] == "br" else KD
                copy(Wh[:, n % 2, 0:k, :], W[:, g % NW, 0:k, :]).then_inc(sems["w_hi"], 1)

            for l in range(DEPTH):
                split = 0
                for kind, i in STEPS:
                    while split < split_upto(kind, i):
                        high_part(l, split)
                        split += 1
                    if kind == "mod":
                        act.wait_ge(*after("lam_sum", l, 1))
                        act.activation(lamc[:, 4:6], lamc[:, 4:6], ACT.Exp).then_inc(sems["lam_exp"], 1)
                    elif kind == "ht":
                        act.wait_ge(*after("h_f32", l, i + 1))
                        copy(Hh[:, i, :], th[:, i % 2]).then_inc(sems["h_hi"], 1)
                    elif kind == "conv":
                        act.wait_ge(*filled(l, kind, i))
                        ps = slot(kind, i)
                        if i >= 2:
                            act.wait_ge(*after("conv_ready", l, i - 1))
                        elif l:
                            act.wait_ge(*after("x_part", l - 1, 8))
                        if i < 2:
                            act.wait_ge(*after("pad_ready", l, 1))
                        r = raw[:, i % 2, :]
                        copy(r[:, 1:1 + HALF], ps[:, 0:HALF])
                        copy(r[:, 1 + HALF:1 + LAT], ps[:, 512:512 + LAT - HALF])
                        copy(r[:, ZP + 1:ZP + 1 + CTX], ps[:, 512 + LAT - HALF:512 + HALF]).then_inc(sems["up_ready"], 1)
                        if i == 3:
                            act.wait_ge(hy_here, 16 * N_HY * (l + 1))
                            link(act.activation(expld, expld, ACT.Exp))
                    elif kind == "ffn":
                        act.wait_ge(*after("farg_ready", l, i + 1))
                        act.activation(hid, rr[:, 0], ACT.Sin).then_inc(sems["hid_ready"], 1)
                    elif kind == "filt":
                        o, t = divmod(i, NT)
                        if i:
                            act.wait_ge(*after("fab_ready", l, i))
                        act.activation(decay, expld[:, :, o, :], ACT.Exp, scale=negt[:, t:t + 1]).then_inc(sems["decay_ready"], 1)
                    elif kind in ("fdft", "zdft"):
                        n = 10 * (i // 5) + 5 * (kind == "zdft") + i % 5
                        act.wait_ge(*filled(l, kind, i))
                        ps = slot(kind, i)
                        if i % 5 < 4:
                            if n >= 2:
                                act.wait_ge(*after("spec_ready", l, n - 1))
                            copy(oddb[:, n % 2], ps[:, 512:1024]).then_inc(sems["odd_ready"], 1)
                        else:
                            dst = HSc if kind == "fdft" else PMc
                            if n >= 2:
                                act.wait_ge(*after("spec_ready", l, n))
                            copy(dst, halves(ps[:, :])).then_inc(sems["spec_ready"], 1)
                            act.nop().then_inc(sems["odd_ready"], 1)
                    elif kind == "zt":
                        o, r = divmod(i, 3)
                        act.wait_ge(*filled(l, kind, i))
                        ps = slot(kind, i)
                        if o == 1 and r == 0:
                            act.wait_ge(*after("y_ready", l, 1))
                        if r < 2:
                            copy(zT[:, 2 * r:2 * r + 2, :], halves(ps[:, :])).then_inc(sems["zt_ready"], 1)
                        else:
                            copy(zT[:, 4, :], ps[:, 0:HY]).then_inc(sems["zt_ready"], 1)
                    elif kind in ("path", "mgate"):
                        n = 12 * (i // 4) + i % 4 if kind == "path" else 12 * (i // 8) + 4 + i % 8
                        act.wait_ge(*filled(l, kind, i))
                        ps = slot(kind, i)
                        if n >= 2:
                            act.wait_ge(*after("gate_used", l, n - 1))
                        act.activation(halves(th[:, n % 2]), two(ps), ACT.Tanh, scale=0.5)\
                           .then_inc(sems["th_ready"], 1)
                    elif kind in ("qk", "v"):
                        n = i + 8 * (kind == "v")
                        act.wait_ge(*filled(l, kind, i))
                        ps = slot(kind, i)
                        if n >= 10:
                            act.wait_ge(*after("v_ready", l, n - 9))
                        elif n >= 2:
                            act.wait_ge(*after("qk_ready", l, n - 1))
                        copy(halves(raw[:, n % 2, 0:NTOK]), two(ps), DA_SCALE if n < 4 else 1.0).then_inc(sems["raw_ready"], 1)
                    elif kind == "kc":
                        act.wait_ge(*filled(l, kind, i))
                        ps = slot(kind, i)
                        copy(kT[:, :, 0:PAST], ps[:, 0:512].rearrange("p (a b) -> p a b", a=4)).then_inc(sems["kc_ready"], 1)
                    elif kind == "sk":
                        act.wait_ge(*filled(l, kind, i))
                        copy(stk, slot(kind, i)[:, 0:512]).then_inc(sems["sk_ready"], 1)
                    elif kind == "da_score":
                        n = keysn(i)
                        for j in range(2):
                            act.wait_ge(*filled(l, kind, i, j))
                            ps = slot(kind, i, j)
                            act.wait_ge(*after("da_max", l, 2 * i + j + 1))
                            e = E[:, i % 2, j, 0:n]
                            act.activation(two_or_one(e, n), two(ps) if n > CTX else ps[:, 0:n], ACT.Exp,
                                               bias=st[:, i % 2, j:j + 1], accum_out=st[:, i % 2, 2 + j:3 + j]).then_inc(sems["da_exp"], 1)
                    elif kind in ("da_ptrans", "ml_ptrans"):
                        h, t = divmod(i, NT)
                        act.wait_ge(*filled(l, kind, i))
                        ps = slot(kind, i)
                        da = kind[0] == "d"
                        if t < 4:
                            dst = (PT if da else PTm)[:, :, 128 * t:128 * t + 128]
                            if t == 0 and h:
                                act.wait_ge(*after("da_o" if da else "ml_o", l, h))
                            ins = copy(dst, ps[:, 0:640].rearrange("p (a b) -> p a b", a=NT))
                        else:
                            ins = copy((PTc if da else PTmc)[:, h % 2], ps[:, 0:CTX])
                        ins.then_inc(sems[kind[:2] + "_pt"], 1)
                    elif kind == "da_pv":
                        act.wait_ge(*filled(l, kind, i))
                        copy(OT[:, i], slot(kind, i)[:, 0:NTOK]).then_inc(sems["da_o"], 1)
                    elif kind == "dams" and i == DAH - 1:
                        act.wait_ge(*after("da_ms", l, 4))
                        act.activation(MS, MS, ACT.Sqrt).then_inc(sems["da_rt"], 1)
                    elif kind == "dqkv":
                        act.wait_ge(*filled(l, kind, i))
                        ps = slot(kind, i)
                        if i == 0:
                            act.wait_ge(*after("gate_used", l, 16))
                            act.wait_ge(store_k, 32 * (l + 1))
                        dst = cq[:, i] if i < 3 else ckv[:, i - 3, PAST:NKEY]
                        copy(halves(dst), two(ps)).then_inc(sems["c_raw"], 1)
                    elif kind == "kr":
                        act.wait_ge(*filled(l, kind, i))
                        copy(halves(krs), two(slot(kind, i), p=MR)).then_inc(sems["kr_raw"], 1)
                    elif kind == "cc":
                        act.wait_ge(*filled(l, kind, i))
                        ps = slot(kind, i)
                        copy(ckv[:, :, 0:PAST], ps[:, 0:256].rearrange("p (a b) -> p a b", a=2)).then_inc(sems["cc_ready"], 1)
                        for b in range(2):
                            last = copy(mkT[64:96, b, 0:PAST], ps[0:MR, 512:640])
                        last.then_inc(sems["cc_ready"], 1)
                    elif kind == "mms" and i == 1:
                        act.wait_ge(*after("m_ms", l, 2))
                        act.activation(MSm, MSm, ACT.Sqrt).then_inc(sems["m_rt"], 1)
                    elif kind == "sc":
                        act.wait_ge(*filled(l, kind, i))
                        ps = slot(kind, i)
                        copy(stc[:, 0:KVL], ps[:, 0:KVL])
                        copy(stc[:, KVL:KVL + MR], ps[:, 512:512 + MR]).then_inc(sems["sc_ready"], 1)
                    elif kind == "mv":
                        act.wait_ge(*filled(l, kind, i))
                        copy(Vm[:, 2 * i:2 * i + 2, :], halves(slot(kind, i)[:, :])).then_inc(sems["mv_ready"], 1)
                    elif kind == "mq":
                        act.wait_ge(*filled(l, kind, i))
                        copy(halves(mqT[0:96, i % 2]), two(slot(kind, i), p=96), MLA_SCALE).then_inc(sems["mq_raw"], 1)
                    elif kind == "mk":
                        act.wait_ge(*filled(l, kind, i))
                        copy(halves(mkT[0:MN, i % 2]), two(slot(kind, i), NKEY // 2, MN)).then_inc(sems["mk_ready"], 1)
                    elif kind == "ml_score":
                        n = keysn(i)
                        act.wait_ge(*filled(l, kind, i))
                        ps = slot(kind, i)
                        act.wait_ge(*after("ml_max", l, i + 1))
                        act.activation(two_or_one(Em[:, i % 2, 0:n], n), two(ps) if n > CTX else ps[:, 0:n],
                                           ACT.Exp, bias=st[:, i % 2, 0:1], accum_out=st[:, i % 2, 2:3]).then_inc(sems["ml_exp"], 1)
                    elif kind == "ml_pv":
                        p = 64 * (i % 2)
                        act.wait_ge(*filled(l, kind, i))
                        copy(Y[p:p + 64, i // 2], slot(kind, i)[0:MV, 0:NTOK]).then_inc(sems["ml_o"], 1)
                    elif kind == "wo":
                        act.wait_ge(*filled(l, kind, i))
                        ps = slot(kind, i)
                        if i >= 2:
                            act.wait_ge(*after("x_part", l, i - 1))
                        r, g = rT[:, i % 2, :], modc[:, 2 * KD + i, :]
                        copy_ = lambda o_, i_, s_: act.activation(o_, i_, ACT.Copy, scale=s_)
                        copy_(r[:, 0:HALF], ps[:, 0:HALF], g[:, 0:1])
                        copy_(r[:, HALF:LAT], ps[:, 512:512 + LAT - HALF], g[:, 0:1])
                        copy_(r[:, LAT:NTOK], ps[:, 512 + LAT - HALF:512 + HALF], g[:, 1:2]).then_inc(sems["r_ready"], 1)
                    elif kind == "ln":
                        act.wait_ge(*after("ln_var", l, 1))
                        act.activation(lnr[:], lnr[:], ACT.Sqrt).then_inc(sems["ln_rt"], 1)

        @block.vector
        def _(dve):
            def link(ins):
                chain["dve"] += 1
                ins.then_inc(dve_chain, 1)
                dve.wait_ge(dve_chain, chain["dve"])

            signalled = {}

            def own(name):
                signalled[name] = signalled.get(name, 0) + 1
                return sems[name], signalled[name]

            TT, TS, STT = dve.tensor_tensor, dve.tensor_scalar, dve.scalar_tensor_tensor

            def softmax_max(ps, n, out):
                return dve.tensor_reduce(out, two(ps) if n > CTX else ps[:, 0:n],
                                         mybir.AxisListType.XY if n > CTX else AX, ALU.max, negate=True)

            dve.wait_ge(consts_here, 16 * 8)
            dve.wait_ge(c_sig, 1)
            TT(ccol[:], ccol[:], csig[:], ALU.mult).then_inc(c_silu, 1)
            def clear_pads():
                dve.memset(raw[:, :, 0:1], 0.0)
                dve.memset(raw[:, :, LAT + 1:LAT + 3], 0.0)
                return dve.memset(raw[:, :, 643:644], 0.0)

            for l in range(DEPTH):
                for kind, i in STEPS:
                    if kind == "mod":
                        dve.wait_ge(small_here, 16 * N_SMALL * (l + 1))
                        dve.wait_ge(*filled(l, kind, i))
                        ps = slot(kind, i)
                        clear_pads().then_inc(sems["pad_ready"], 1)
                        dve.wait_ge(*own("pad_ready"))
                        link(TT(modc[:], ps[:, 0:6 * KD].rearrange("p (m c) -> p m c", c=2),
                                bmod[:].rearrange("p (m c) -> p m c", c=1).to_broadcast([128, 3 * KD, 2]), ALU.add))
                        link(TS(modc[:, KD:2 * KD, :], modc[:, KD:2 * KD, :], 1.0, None, ALU.add))
                        TS(modc[:, 2 * KD:, :], modc[:, 2 * KD:, :], 0.5, None, ALU.mult).then_inc(sems["mod_ready"], 1)
                        dve.wait_ge(*own("mod_ready"))
                        dve.wait_ge(*after("mod_ready", l, 1))
                        link(TT(lpj[:], lp[:, 0:4:2, :], lp[:, 1:4:2, :], ALU.mult))
                        link(dve.tensor_reduce(lamc[:, 2:4], lpj[:], AX, ALU.add))
                        TS(lamc[:, 4:6], lamc[:, 2:4], 1.0, None, ALU.mult).then_inc(sems["lam_sum"], 1)
                        dve.wait_ge(*own("lam_sum"))
                    elif kind == "ht":
                        dve.wait_ge(*filled(l, kind, i))
                        ps = slot(kind, i)
                        s = modc[:, KD + i, :]
                        b = modc[:, i, :]
                        if i >= 2:
                            dve.wait_ge(*after("h_ready", l, i - 1))
                        h = th[:, i % 2]
                        TS(h[:, 0:LAT], ps[:, 0:LAT], s[:, 0:1], b[:, 0:1], ALU.mult, ALU.add)
                        TS(h[:, LAT:NTOK], ps[:, LAT:NTOK], s[:, 1:2], b[:, 1:2], ALU.mult, ALU.add)\
                            .then_inc(sems["h_f32"], 1)
                        dve.wait_ge(*own("h_f32"))
                    elif kind == "conv":
                        dve.wait_ge(*after("up_ready", l, i + 1))
                        r = raw[:, i % 2, :]
                        dst = V4[:, i] if i < 4 else G4[:, i % 4]
                        w = lambda tap: convw[:, tap, i:i + 1]
                        if l and i == 0:
                            dve.wait_ge(x_saved, 16)
                        link(TS(tconv, r[:, 1:643], w(1), convb[:, i:i + 1], ALU.mult, ALU.add))
                        link(STT(tconv, r[:, 0:642], w(0), tconv, ALU.mult, ALU.add))
                        STT(dst, r[:, 2:644], w(2), tconv, ALU.mult, ALU.add).then_inc(sems["conv_ready"], 1)
                        dve.wait_ge(*own("conv_ready"))
                    elif kind == "ffn":
                        dve.wait_ge(*filled(l, kind, i))
                        ps = slot(kind, i)
                        a, k = rr[:, 0], rr[:, 1]
                        if i:
                            dve.wait_ge(*after("hid_ready", l, 1))
                        link(TS(halves(a), two(ps, p=HY_FFN), fvec[:, i:i + 1], fvec[:, 2 + i:3 + i],
                                ALU.add, ALU.mult))
                        link(TS(k, a, 1 / TWO_PI, MAGIC, ALU.mult, ALU.add))
                        link(TS(k, k, MAGIC, None, ALU.subtract))
                        for part in (PI_HI, PI_MID, PI_LO):
                            link(STT(a, k, -part, a, ALU.mult, ALU.add))
                        TS(a, a, math.pi - 1e-6, -(math.pi - 1e-6), ALU.min, ALU.max).then_inc(sems["farg_ready"], 1)
                        dve.wait_ge(*own("farg_ready"))
                    elif kind == "filt":
                        o, t = divmod(i, NT)
                        dve.wait_ge(*filled(l, kind, i))
                        ps = slot(kind, i)
                        dve.wait_ge(*after("decay_ready", l, i + 1))
                        TT(oddb[:, 0], ps[:, 0:HY], decay[:, 0], ALU.mult)
                        link(STT(oddb[:, 1], ps[:, 512:1024], hmask[:, t:t + 1], decay[:, 1], ALU.mult, ALU.mult))
                        TT(fab[:, 0, t], oddb[:, 0], oddb[:, 1], ALU.add)
                        TT(fab[:, 1, t], oddb[:, 0], oddb[:, 1], ALU.subtract).then_inc(sems["fab_ready"], 1)
                        dve.wait_ge(*own("fab_ready"))
                    elif kind in ("fdft", "zdft"):
                        n = 10 * (i // 5) + 5 * (kind == "zdft") + i % 5
                        if i % 5 < 4:
                            q, m = divmod(i % 5, 2)
                            dve.wait_ge(*filled(l, kind, i))
                            ps = slot(kind, i)
                            dve.wait_ge(*after("odd_ready", l, n + 1))
                            dst = HS if kind == "fdft" else PM
                            TT(dst[:, 0, q, 512 * m:512 * m + 512], ps[:, 0:HY], oddb[:, n % 2], ALU.add)
                            TT(dst[:, 1, q, 512 * m:512 * m + 512], ps[:, 0:HY], oddb[:, n % 2], ALU.subtract).then_inc(sems["spec_ready"], 1)
                            dve.wait_ge(*own("spec_ready"))
                        elif kind == "zdft":
                            dve.wait_ge(*after("spec_ready", l, n + 1))
                            for s in range(2):
                                product(dve, link, TT, ALU, PM[:, s], HS[:, s], tB, tC)
                            link(TT(PM[:, 1], PM[:, 0], PM[:, 1], ALU.subtract))
                            link(STT(PM[:, 0], PM[:, 0], 2.0, PM[:, 1], ALU.mult, ALU.subtract))
                            product(dve, link, TT, ALU, PMc, HSc, tB[:, 0:HY], tC[:, 0:HY])
                            dve.nop().then_inc(sems["y_ready"], 1)
                    elif kind == "inv":
                        o, c = divmod(i, CT)
                        dve.wait_ge(*filled(l, kind, i))
                        ps = slot(kind, i)
                        dve.wait_ge(*after("conv_ready", l, 8 + 4 * o))
                        sk = skip[:, o, c:c + 1]
                        t_lat, t_ctx = tconv[:, 0:LAT], tconv[:, ZP:ZP + CTX]
                        pairs = lambda ap: ap.rearrange("p (u a) -> p u a", a=2)
                        STT(pairs(t_lat), pairs(V4[:, c, 0:LAT]), sk,
                            ps[:, 0:LAT].rearrange("p (a u) -> p u a", a=2), ALU.mult, ALU.add)
                        link(STT(t_ctx, V4[:, c, ZP:ZP + CTX], sk, ps[:, 512:640], ALU.mult, ALU.add))
                        TT(V4[:, c, 0:LAT], t_lat, G4[:, c, 0:LAT], ALU.mult)
                        TT(V4[:, c, ZP:ZP + CTX], t_ctx, G4[:, c, ZP:ZP + CTX], ALU.mult).then_inc(sems["z_ready"], 1)
                        dve.wait_ge(*own("z_ready"))
                        if i == 7:
                            dve.wait_ge(*after("z_ready", l, 8))
                    elif kind == "path":
                        n_, c = divmod(i, CT)
                        dve.wait_ge(*filled(l, kind, i))
                        ps = slot(kind, i)
                        dve.wait_ge(*after("th_ready", l, 12 * n_ + c + 1))
                        if n_ == 2 and c == 0:
                            dve.wait_ge(*after("ml_o", l, MH))
                        t_ = th[:, c % 2]
                        link(STT(halves(t_), halves(t_), 1.0, two(ps), ALU.add, ALU.mult))
                        if n_ == 0:
                            STT(t_[:, 0:LAT], t_[:, 0:LAT], 0.5, V4[:, c, 0:LAT], ALU.mult, ALU.mult)
                            STT(t_[:, LAT:NTOK], t_[:, LAT:NTOK], 0.5, V4[:, c, ZP:ZP + CTX],
                                ALU.mult, ALU.mult).then_inc(sems["br_f32"], 1)
                        else:
                            y = OT[:, c] if n_ == 1 else Y[:, c]
                            STT(t_, t_, 0.5, y, ALU.mult, ALU.mult).then_inc(sems["br_f32"], 1)
                        dve.wait_ge(*own("br_f32"))
                    elif kind == "mbranch":
                        n_, d = divmod(i, KD)
                        g = 12 * n_ + 4 + d
                        dve.wait_ge(*filled(l, kind, i))
                        ps = slot(kind, i)
                        dve.wait_ge(*after("th_ready", l, g + 1))
                        t_ = th[:, g % 2]
                        m = MG[:, NTOK * d:NTOK * d + NTOK]
                        if n_ == 0:
                            STT(halves(m), halves(t_), 1.0, two(ps), ALU.add, ALU.mult)\
                                .then_inc(sems["gate_used"], 1)
                        else:
                            link(STT(halves(t_), halves(t_), 1.0, two(ps), ALU.add, ALU.mult))
                            TT(m, m, t_, ALU.add).then_inc(sems["gate_used"], 1)
                        dve.wait_ge(*after("gate_used", l, g + 1))
                    elif kind == "qk":
                        dve.wait_ge(*after("raw_ready", l, i + 1))
                        r = raw[:, i % 2, 0:LAT]
                        dst = qT[:, i, :] if i < 4 else kT[:, i - 4, PAST:NKEY]
                        mask = [(p + 16) % 32 for p in range(32)]
                        dve.stream_shuffle(swp, r, mask=mask).then_inc(dve_chain, 1)
                        chain["dve"] += 1
                        link(TT(dst[:, 0:LAT], r, rope_da[:, 0], ALU.mult))
                        link(TT(swp, swp, rope_da[:, 1], ALU.mult))
                        TT(dst[:, 0:LAT], dst[:, 0:LAT], swp, ALU.add)
                        dve.tensor_copy(dst[:, LAT:NTOK], raw[:, i % 2, LAT:NTOK]).then_inc(sems["qk_ready"], 1)
                        dve.wait_ge(*own("qk_ready"))
                    elif kind == "vt":
                        dve.wait_ge(*filled(l, kind, i))
                        ps = slot(kind, i)
                        dve.tensor_copy(V[:, 1:6, 128 * i:128 * i + 128],
                                            ps[:, 0:640].rearrange("p (a b) -> p a b", a=NT)).then_inc(sems["v_ready"], 1)
                        dve.wait_ge(*own("v_ready"))
                    elif kind == "da_score":
                        if i == 0:
                            dve.wait_ge(*after("lam_exp", l, 1))
                            link(TT(lamc[:, 2:3], lamc[:, 4:5], lamc[:, 5:6], ALU.subtract))
                            link(TS(lamc[:, 6:7], lamc[:, 2:3], lamc[:, 0:1], -1.0, ALU.add, ALU.mult))
                            link(TT(lamc[:, 7:8], subln[:], lamc[:, 1:2], ALU.mult))
                        n = keysn(i)
                        for j in range(2):
                            dve.wait_ge(*filled(l, kind, i, j))
                            ps = slot(kind, i, j)
                            softmax_max(ps, n, st[:, i % 2, j:j + 1]).then_inc(sems["da_max"], 1)
                            dve.wait_ge(*own("da_max"))
                    elif kind == "da_ptrans":
                        n = keysn(i)
                        s, e = st[:, i % 2], E[:, i % 2]
                        dve.wait_ge(*after("da_exp", l, 2 * i + 2))
                        link(dve.reciprocal(s[:, 4:6], s[:, 2:4]))
                        link(TT(s[:, 6:7], s[:, 5:6], lamc[:, 6:7], ALU.mult))
                        link(TS(e[:, 0, 0:n], e[:, 0, 0:n], s[:, 4:5], None, ALU.mult))
                        STT(e[:, 0, 0:n], e[:, 1, 0:n], s[:, 6:7], e[:, 0, 0:n], ALU.mult, ALU.add).then_inc(sems["da_p"], 1)
                        dve.wait_ge(*own("da_p"))
                    elif kind == "da_pv":
                        dve.wait_ge(*after("da_o", l, i + 1))
                        if i == DAH - 1:
                            for h in range(DAH):
                                TT(sqd[:, h], OT[:, h], OT[:, h], ALU.mult).then_inc(sems["da_sq"], 1)
                                dve.wait_ge(*own("da_sq"))
                    elif kind == "dams":
                        dve.wait_ge(*filled(l, kind, i))
                        ps = slot(kind, i)
                        TS(halves(MS[:, i]), two(ps), 1.0 / DAV, RMS_EPS, ALU.mult, ALU.add).then_inc(sems["da_ms"], 1)
                        dve.wait_ge(*own("da_ms"))
                        if i == DAH - 1:
                            dve.wait_ge(*after("da_rt", l, 1))
                            link(dve.reciprocal(MS, MS))
                            link(STT(OT, OT, lamc[:, 7:8], MS, ALU.mult, ALU.mult))
                    elif kind == "dqkv":
                        dve.wait_ge(*after("c_raw", l, i + 1))
                        c = cq[:, i] if i < 3 else ckv[:, i - 3, PAST:NKEY]
                        if i == 0:
                            dve.wait_ge(store_k, 32 * (l + 1))
                        if i == 3:
                            dve.wait_ge(*after("m_ms", l, 1))
                        TT(sqm[:, i % 3], c, c, ALU.mult).then_inc(sems["c_sq"], 1)
                        dve.wait_ge(*own("c_sq"))
                        if i == 2:
                            dve.wait_ge(*filled(l, "mms", 0))
                            ps = slot("mms", 0)
                            TS(halves(MSm[:, 0]), two(ps), 1.0 / QL, RMS_EPS, ALU.mult, ALU.add).then_inc(sems["m_ms"], 1)
                            dve.wait_ge(*own("m_ms"))
                    elif kind == "kr":
                        dve.wait_ge(*after("kr_raw", l, 1))
                        sw, r = swm[0:MR], krs[:, 0:LAT]
                        dve.stream_shuffle(sw, r, mask=[p ^ 8 for p in range(32)]).then_inc(dve_chain, 1)
                        chain["dve"] += 1
                        link(TT(krt, r, rope_m[0:MR, 0], ALU.mult))
                        link(TT(sw, sw, rope_m[0:MR, 1], ALU.mult))
                        for b in range(2):
                            TT(mkT[64:96, b, PAST:LKEY], krt, sw, ALU.add)
                            last = dve.tensor_copy(mkT[64:96, b, LKEY:NKEY], krs[:, LAT:NTOK])
                        last.then_inc(sems["kr_ready"], 1)
                        dve.wait_ge(*own("kr_ready"))
                    elif kind == "mms" and i == 1:
                        dve.wait_ge(*filled(l, kind, i))
                        ps = slot(kind, i)
                        TS(halves(MSm[:, 1]), two(ps), 1.0 / KVL, RMS_EPS, ALU.mult, ALU.add).then_inc(sems["m_ms"], 1)
                        dve.wait_ge(*own("m_ms"))
                        dve.wait_ge(*after("m_rt", l, 1))
                        link(dve.reciprocal(MSm, MSm))
                        for k in range(3):
                            last = STT(cq[:, k], cq[:, k], qn[:, k:k + 1], MSm[:, 0], ALU.mult, ALU.mult)
                        last.then_inc(sems["c_ready"], 1)
                        dve.wait_ge(*own("c_ready"))
                        for k in range(2):
                            c = ckv[:, k, PAST:NKEY]
                            last = STT(c, c, kvn[:, k:k + 1], MSm[:, 1], ALU.mult, ALU.mult)
                        last.then_inc(sems["c_ready"], 1)
                        dve.wait_ge(*own("c_ready"))
                    elif kind == "mq":
                        dve.wait_ge(*after("mq_raw", l, i + 1))
                        sw, q = swm[64:96], mqT[64:96, i % 2, 0:LAT]
                        dve.stream_shuffle(sw, q, mask=[p ^ 8 for p in range(32)]).then_inc(dve_chain, 1)
                        chain["dve"] += 1
                        dve.wait_ge(dve_chain, chain["dve"])
                        TT(q, q, rope_m[64:96, 0], ALU.mult)
                        link(TT(sw, sw, rope_m[64:96, 1], ALU.mult))
                        TT(q, q, sw, ALU.add).then_inc(sems["mq_ready"], 1)
                        dve.wait_ge(*own("mq_ready"))
                    elif kind == "ml_score":
                        dve.wait_ge(*filled(l, kind, i))
                        softmax_max(slot(kind, i), keysn(i), st[:, i % 2, 0:1]).then_inc(sems["ml_max"], 1)
                        dve.wait_ge(*own("ml_max"))
                    elif kind == "ml_ptrans":
                        s, e, n = st[:, i % 2], Em[:, i % 2], keysn(i)
                        dve.wait_ge(*after("ml_exp", l, i + 1))
                        link(dve.reciprocal(s[:, 4:5], s[:, 2:3]))
                        TS(e[:, 0:n], e[:, 0:n], s[:, 4:5], None, ALU.mult).then_inc(sems["ml_p"], 1)
                        dve.wait_ge(*own("ml_p"))
                    elif kind == "xt":
                        dve.wait_ge(*filled(l, kind, i))
                        ps = slot(kind, i)
                        x = X[:, :, 128 * i:128 * i + 128]
                        if i == 0:
                            dve.wait_ge(x_here, 32 * (l + 2))
                        STT(x, x, ALPHA, ps[:, 0:640].rearrange("p (a b) -> p a b", a=NT), ALU.mult, ALU.add).then_inc(sems["x_part"], 1)
                        dve.wait_ge(*own("x_part"))
                    elif kind == "ln":
                        dve.wait_ge(*after("x_part", l, 8))
                        for t in range(NT):
                            for b in range(2):
                                last = dve.bn_stats(lnst[:, t, b, :], X[:, t, 512 * b:512 * b + 512])
                        link(last)
                        for t in range(NT):
                            last = dve.bn_aggr(lnmv[:, t, :], lnst[:, t, :, :].rearrange("p a b -> p (a b)"))
                        link(last)
                        TS(lnr[:], lnmv[:, :, 1], LN_EPS, None, ALU.add).then_inc(sems["ln_var"], 1)
                        dve.wait_ge(*own("ln_var"))
                        dve.wait_ge(*after("ln_rt", l, 1))
                        link(dve.reciprocal(lnr[:], lnr[:]))
                        dve.wait_ge(ln_here, 32 * (l + 1))
                        for t in range(NT):
                            x = X[:, t, :]
                            link(TS(x, x, lnmv[:, t, 0:1], lnr[:, t:t + 1], ALU.subtract, ALU.mult))
                            link(TT(x, x, lng, ALU.mult))
                            TT(x, x, lnb, ALU.add).then_inc(sems["x_ready"], 1)
                            dve.wait_ge(*own("x_ready"))

        @block.gpsimd
        def _(pool):
            def minus(out, in_, high):
                return pool.tensor_tensor(out, in_, high.bitcast(f32), ALU.subtract)

            def low_part(l, n):
                g = l * NSTREAM + NMOD + n
                pool.wait_ge(*after("w_hi", l, n + 1))
                if l or n >= 2:
                    pool.wait_ge(*tile_done(l, n - 2))
                k = CT if STREAM[NMOD + n][0] == "br" else KD
                minus(Wl[:, n % 2, 0:k, :], W[:, g % NW, 0:k, :], Wh[:, n % 2, 0:k, :])\
                    .then_inc(sems["w_lo"], 1)

            for l in range(DEPTH):
                split = 0
                for kind, i in STEPS:
                    while split < split_upto(kind, i):
                        low_part(l, split)
                        split += 1
                    if kind == "ht":
                        pool.wait_ge(*after("h_hi", l, i + 1))
                        minus(Hl[:, i, :], th[:, i % 2], Hh[:, i, :]).then_inc(sems["h_ready"], 1)
                    elif kind == "path":
                        c = i % CT
                        pool.wait_ge(*after("br_f32", l, i + 1))
                        pool.tensor_copy(BRh[:, c, :], th[:, c % 2]).then_inc(sems["br_hi"], 1)
                        pool.wait_ge(*after("br_hi", l, i + 1))
                        minus(BRl[:, c, :], th[:, c % 2], BRh[:, c, :]).then_inc(sems["gate_used"], 1)
                    elif kind == "mbranch" and i >= 2 * KD:
                        d = i - 2 * KD
                        m = MG[:, NTOK * d:NTOK * d + NTOK]
                        pool.wait_ge(*after("gate_used", l, 28 + d + 1))
                        pool.tensor_copy(MGh[:, d, :], m).then_inc(sems["mg_hi"], 1)
                        pool.wait_ge(*after("mg_hi", l, d + 1))
                        minus(MGl[:, d, :], m, MGh[:, d, :]).then_inc(sems["mg_ready"], 1)
    return nc


def keysn(u):
    return LKEY if u % NT < 4 else CTX


def two_or_one(e, n):
    return e.rearrange("p (a b) -> p a b", a=2) if n > CTX else e


def product(dve, link, TT, ALU, z, h, tb, tc):
    TT(tb, z[:, 0], h[:, 1], ALU.mult)
    link(TT(tc, z[:, 1], h[:, 1], ALU.mult))
    link(TT(z[:, 0], z[:, 0], h[:, 0], ALU.mult))
    TT(z[:, 0], z[:, 0], tc, ALU.subtract)
    link(TT(z[:, 1], z[:, 1], h[:, 0], ALU.mult))
    link(TT(z[:, 1], z[:, 1], tb, ALU.add))


def tiles(w, m=128):
    l, r, c = w.shape
    return w.reshape(l, r // 128, 128, c // m, m).transpose(0, 3, 2, 1, 4)


def columns(v):
    return v.reshape(DEPTH, -1, 128).transpose(0, 2, 1)


def laid_out(x):
    w_in = x["w_in"]
    ffn = np.stack([x["hy_ffn_b1"], x["hy_ffn_b2"], x["hy_sin_freq"][:, 0], x["hy_sin_freq"][:, 1]], -1)
    ffn = np.concatenate([ffn, np.zeros((DEPTH, 128 - HY_FFN, 4), ffn.dtype)], 1)
    return {
        "cvec": np.stack([x["c"][0], x["c_ctx"]], -1).reshape(KD, 128, 2).transpose(1, 0, 2),
        "w_mod": tiles(x["w_mod"]),
        "w_in": tiles(np.concatenate([w_in[:, :, :C_KR + 128], w_in[:, :, C_PATH:]], -1)),
        "w_branch": np.stack([tiles(x["w_branch"][:, n]) for n in range(3)], 1).reshape(DEPTH, 3 * KD, 128, CT, 128),
        "w_out": tiles(x["w_out"]),
        "vecs": np.concatenate([columns(x["b_mod"]), columns(x["hy_conv_w"]), columns(x["hy_conv_b"]),
                                columns(x["hy_skip"]), ffn, columns(x["da_subln"]), columns(x["mla_q_norm"]),
                                columns(x["mla_kv_norm"])], -1),
    }

INPUTS = ["x_prompt", "x_sample", "cache_diff_k", "cache_diff_v", "cache_mla_ckv", "cache_mla_krope", "hy_ffn_w1",
          "hy_ffn_w2", "hy_ffn_w3", "hy_log_decay", "da_lambda", "mla_w_uq", "mla_w_ukv", "ln_g", "ln_b"]
OUTPUTS = [(1, CTX, D), (1, LAT, D), (1, DEPTH, CTX, 2, DAH, DHD), (1, DEPTH, CTX, DAH, DAV), (1, DEPTH, CTX, KVL),
           (1, DEPTH, CTX, MR)]


def kernel(**inputs):
    import concourse.bacc as bacc
    from concourse.bass_utils import run_bass_kernel_spmd as run

    nc = bacc.Bacc("TRN2", target_bir_lowering=False, num_devices=1)
    f32 = mybir.dt.float32
    arrays, A = {}, {}
    for name, a in [(n, inputs[n]) for n in INPUTS] + list(laid_out(inputs).items()) + list(constants().items()):
        a = np.ascontiguousarray(a)
        arrays[f"in_{name}"] = a
        A[name] = nc.dram_tensor(f"in_{name}", a.shape, mybir.dt.from_np(a.dtype), kind="ExternalInput").ap()
    outs = [nc.dram_tensor(f"out_{i}", s, f32, kind="ExternalOutput").ap() for i, s in enumerate(OUTPUTS)]
    build(nc, A, outs)
    r = run(nc, [arrays], core_ids=[0])
    return tuple(r.results[0][f"out_{i}"] for i in range(len(OUTPUTS)))
```

```python
import math
from contextlib import ExitStack

import numpy as np

import concourse.bass as bass
from concourse import mybir

DEPTH, D, LAT, CTX, PAST = 2, 1024, 512, 128, 128
NTOK = LAT + CTX
HALF = NTOK // 2
KD = D // 128
NT = NTOK // 128
HY, HY_FFN, POS = 512, 64, 33
CT = HY // 128
GRID_W = 64
DAH, DHD, DAV = 4, 64, 128
MH, MN, MR, MV = 8, 64, 32, 64
QL, KVL = 384, 256
NKEY = PAST + NTOK
LKEY = PAST + LAT
ALPHA = (2 * DEPTH) ** 0.25
LN_EPS, RMS_EPS = 1e-5, 1e-6
DA_SCALE = DHD ** -0.5
MLA_SCALE = (MN + MR) ** -0.5
T_HY, T_Q, T_K, T_V, T_DQ, T_DKV, T_KR, T_PATH, T_MERGE = 0, 12, 16, 20, 24, 27, 29, 30, 42
C_KR = 3 * HY + 3 * 512 + QL + KVL
C_PATH = C_KR + MR
TWO_PI = 2 * math.pi
MAGIC = 1.5 * 2 ** 23
PI_HI, PI_MID = 6.28125, 0.0019350051879882812
PI_LO = TWO_PI - PI_HI - PI_MID
SLOTS = 4

VECS = [("ln_g", KD), ("ln_b", KD), ("hy_conv_w", 36), ("hy_conv_b", 12), ("hy_skip", 8), ("hy_ffn", 4),
        ("da_subln", 1), ("mla_q_norm", 3), ("mla_kv_norm", 2)]
NVEC = sum(n for _, n in VECS)


def vec(vecs, name):
    at = [n for n, _ in VECS].index(name)
    start = sum(n for _, n in VECS[:at])
    return vecs[:, start:start + VECS[at][1]]


LAG = 2


def attention_steps(tag, heads, fillers, before=None, behind=None):
    steps, units, taken = [], [(h, t) for h in range(heads) for t in range(NT)], 0
    for u, (h, t) in enumerate(units):
        if before and h + 1 < heads:
            steps += before(h + 1, t)
        steps.append((tag + "_score", u))
        if u > LAG and (u - LAG - 1) % NT == NT - 1:
            steps.append((tag + "_pv", (u - LAG - 1) // NT))
        if behind and u > LAG + 1 and (u - LAG - 2) % NT == NT - 1:
            steps += behind((u - LAG - 2) // NT)[:1]
        if behind and u > LAG + 2 and (u - LAG - 3) % NT == NT - 1:
            steps += behind((u - LAG - 3) // NT)[1:]
        upto = len(fillers) * (u + 1) // len(units)
        steps += fillers[taken:upto]
        taken = upto
        if u >= LAG:
            steps.append((tag + "_ptrans", u - LAG))
    return steps + [(tag + "_ptrans", len(units) - LAG + n) for n in range(LAG)] + [(tag + "_pv", heads - 1)]


def path_steps(n):
    return [("path", CT * n + c) for c in range(CT)]


def merge_steps(n):
    return [(kind, KD * n + d) for d in range(KD) for kind in ("mgate", "mbranch")]


def weave(a, b):
    out, taken = [], 0
    for n, step in enumerate(a):
        out.append(step)
        upto = len(b) * (n + 1) // len(a)
        out += b[taken:upto]
        taken = upto
    return out


def layer_steps(l):
    if l == 0:
        p = [("pmod", g) for g in range(KD)]
        f = [("ffn", 0), ("ffn", 1)] + [("filt", t) for t in range(NT)] + [("fdft", i) for i in range(5)]
        rows = [("pmrow", g) for g in range(KD)]
        s = [("lam", 0)] + rows[:1] + f[:1] + rows[1:3] + p[:2] + f[1:2] + rows[3:5] + p[2:4] + f[2:3]
        s += rows[5:6] + p[4:5] + f[3:4] + rows[6:7] + p[5:6] + f[4:5] + rows[7:] + p[6:7] + f[5:6] + p[7:] + f[6:9]
        s += [("ht", c) for c in range(KD)]
        s += [("conv", 0), ("conv", 1), ("fdft", 2), ("conv", 2), ("conv", 3), ("fdft", 3), ("fdft", 4)]
    else:
        f = [("filt", t) for t in range(NT)]
        s = [("lam", 0)] + [("ht", c) for c in range(KD)]
        s += [("conv", 0)] + f[:1] + [("conv", 1)] + f[1:3] + [("conv", 2)] + f[3:] + [("conv", 3)]
        s += [("fdft", i) for i in range(5)]
    for o in range(2):
        convs = [("conv", 4 + 4 * o + c) for c in range(4)]
        if o:
            f = [("filt", NT + t) for t in range(NT)]
            s += f[:1] + convs[:1] + f[1:3] + convs[1:2] + f[3:4] + convs[2:3] + f[4:5] + convs[3:]
            s += [("fdft", 5 + i) for i in range(5)]
        s += [("zt", 3 * o + i) for i in range(3)]
        s += [("zdft", 5 * o + i) for i in range(5)]
        s += path_steps(0) if o else convs
        s += [("inv", 4 * o + c) for c in range(4)]
    s += [("qk", c) for c in range(8)]
    for c in range(4):
        s += [("v", c)] + ([("kc", 0), ("sk", 0)] if c == 0 else [])
        if c:
            s += [("vt", c - 1)]
    s += [("vt", 3)]
    s += attention_steps("da", DAH, merge_steps(0), behind=lambda h: [("dasq", h), ("dams", h)])
    s += [("dasq", 3), ("dqkv", 0), ("dams", 3), ("dqkv", 1), ("dart", 0), ("dqkv", 2)]
    s += [("dab", h) for h in range(DAH)]
    s += [("dqkv", 3), ("mms", 0), ("dqkv", 4), ("kr", 0), ("mms", 1)]
    p = path_steps(1)
    s += p[:1] + [("mrt", 0)] + p[1:3] + [("mb", 0), ("mb", 1)] + p[3:] + [("cc", 0), ("sc", 0)]
    s += [("mv", i) for i in range(3)]
    head = lambda h, t: [("mq", h)] if t == 2 else [("mk", h // 2)] if t == NT - 1 and h % 2 == 0 else []
    gmods = [("gmod", g) for g in range(KD)]
    nmods = [("nmod", g) for g in range(2 * KD)] if l < DEPTH - 1 else []
    fillers = weave(merge_steps(1), gmods[:KD - 2] + nmods[:NMOD_EARLY - 2])
    s += head(0, 2) + head(0, NT - 1) + attention_steps("ml", MH, fillers, head)
    s += path_steps(2) + merge_steps(2) + gmods[KD - 2:] + nmods[NMOD_EARLY - 2:NMOD_EARLY]
    for d in range(KD):
        s += [("wo", d)]
        if d:
            s += [("xt", d - 1)]
        if l < DEPTH - 1:
            s += {3: [("nffn", 0)], 4: [("nsin", 0)], 5: [("nffn", 1)], 6: [("nsin", 1)]}.get(d, [])
    return s + [("xt", KD - 1), ("ln", 0)] + nmods[NMOD_EARLY:]


NMOD_EARLY = 12
STEPS = [layer_steps(l) for l in range(DEPTH)]




def owned(kind, i):
    first = {"conv": T_HY, "path": T_PATH, "mgate": T_MERGE, "qk": T_Q, "v": T_V, "dqkv": T_DQ, "kr": T_KR}
    if kind in ("nmod", "gmod"):
        return [("mod", i + (2 * KD if kind == "gmod" else 0))]
    if kind in first:
        return [("in", first[kind] + i)]
    if kind == "mbranch":
        return [("br", i)]
    return [("out", i)] if kind == "wo" else []


STREAM = [(l, kind, i, key) for l in range(DEPTH) for kind, i in STEPS[l] for key in owned(kind, i)]
TILE_AT = {}
for g_, (l_, kind_, i_, _) in enumerate(STREAM):
    TILE_AT.setdefault((l_, kind_, i_), g_)
NW = 3
NP = 5
SPLIT = [(kind, i) for kind, i in STEPS[0] if owned(kind, i) and kind not in ("nmod", "gmod")]
NSPLIT = len(SPLIT)
SPLIT_AT = {step: n for n, step in enumerate(SPLIT)}


JOBS = {
    "pmod": lambda i: [("ss_ready", 2 * i + 2)],
    "nmod": lambda i: [("ss_ready", PER["ss_ready"] + i + 1)],
    "gmod": lambda i: [("g_ready", i + 1)],
    "lam": lambda i: [],
    "dasq": lambda h: [],
    "dart": lambda i: [],
    "nsin": lambda i: [],
    "mrt": lambda i: [],
    "pmrow": lambda i: [("row_ready", i + 1)],
    "ht": lambda i: [("h_f32", i + 1)],
    "conv": lambda i: [("up_ready", i + 1)],
    "ffn": lambda i: [("farg_ready", i + 1)],
    "nffn": lambda i: [("farg_ready", PER["farg_ready"] + i + 1)],
    "filt": lambda i: [("fab_ready", i + 1)],
    "fdft": lambda i: [("spec_ready", i % 5 + 1 + 10 * (i // 5))],
    "zdft": lambda i: [("spec_ready", i % 5 + 6 + 10 * (i // 5))],
    "zt": lambda i: [("zt_ready", i + 1)],
    "inv": lambda i: [("z_ready", i + 1)],
    "path": lambda i: [("px_ready", i + 1) if i < CT else ("br_f32", i + 1)],
    "mgate": lambda i: [("th_ready", 12 * (i // 8) + i % 8 + 5)],
    "mbranch": lambda i: [("gate_used", 12 * (i // 8) + i % 8 + 5)],
    "qk": lambda i: [("raw_ready", i + 1)],
    "kc": lambda i: [("kc_ready", 1)],
    "sk": lambda i: [("sk_ready", 1)],
    "v": lambda i: [("raw_ready", 9 + i)],
    "vt": lambda i: [("v_ready", i + 1)],
    "da_score": lambda u: [("da_exp", 2 * u + 1), ("da_exp", 2 * u + 2)],
    "da_ptrans": lambda u: [("da_pt", u + 1)],
    "da_pv": lambda h: [("da_o", h + 1)],
    "dams": lambda h: [("da_ms", h + 1)],
    "dab": lambda h: [("da_n", h + 1)],
    "dqkv": lambda i: [("c_raw", i + 1)],
    "kr": lambda i: [("kr_raw", 1)],
    "cc": lambda i: [("cc_ready", 2)],
    "mms": lambda i: [("m_ms", i + 1)],
    "mb": lambda i: [("c_ready", i + 1)],
    "sc": lambda i: [("sc_ready", 1)],
    "mv": lambda i: [("mv_ready", i + 1)],
    "mq": lambda h: [("mq_raw", h + 1)],
    "mk": lambda p: [("mk_ready", 2 * p + 2)],
    "ml_score": lambda u: [("ml_exp", u + 1)],
    "ml_ptrans": lambda u: [("ml_pt", u + 1)],
    "ml_pv": lambda h: [("ml_o", h + 1)],
    "wo": lambda d: [("r_ready", d + 1)],
    "xt": lambda d: [("x_part", d + 1)],
    "ln": lambda d: [],
}
PER = dict(row_ready=KD, px_ready=4, ln_scaled=5, ss_ready=2 * KD, g_ready=KD, h_f32=8, h_hi=8, h_even=4,
           h_odd=4, br_f32=12, br_hi=12, mg_hi=8, mg_ready=8, w_hi=NSPLIT, w_lo=NSPLIT, up_ready=12,
           conv_ready=12, farg_ready=2, hid_ready=2, decay_ready=10, fab_ready=10, odd_ready=20, spec_ready=20,
           zt_ready=6, y_ready=2, z_ready=8, th_ready=36, gate_used=36, raw_ready=12, qk_ready=8, kc_ready=1,
           sk_ready=1, v_ready=4, da_max=40, da_exp=40, da_p=20, da_pt=20, da_o=4, da_sq=4, da_ms=4, da_rt=1,
           da_rc=1, da_n=4, c_raw=5, c_sq=5, kr_raw=1, cc_ready=2, kr_ready=1, m_ms=2, m_rt=1, m_rc=1,
           pad_ready=1, lam_sum=1, lam_exp=1, c_ready=2, sc_ready=1, mv_ready=3, mq_raw=8, mq_ready=8,
           mk_ready=8, ml_max=40, ml_exp=40, ml_p=40, ml_pt=40, ml_o=8, r_ready=8, x_part=8, ln_var=1, ln_rt=1,
           x_ready=5)


def slot_table():
    table, at, uses, last = {}, 0, [0] * SLOTS, [None] * SLOTS
    for l in range(DEPTH):
        for kind, i in STEPS[l]:
            for j, (name, count) in enumerate(JOBS[kind](i)):
                s = at % SLOTS
                table[l, kind, i, j] = (s, uses[s], last[s])
                last[s] = (name, l * PER[name] + count)
                uses[s] += 1
                at += 1
    return table


SLOT = slot_table()


def upto_table():
    table = {}
    for l in range(DEPTH):
        places = [n for n, step in enumerate(STEPS[l]) if step in SPLIT_AT]
        table[l, STEPS[l].index(("ht", 0))] = 1
        for n, (a, b) in enumerate(zip(places, places[1:])):
            table[l, a if b - a <= 2 else a + 1] = n + 2
    return table


UPTO = upto_table()


def constants():
    f = np.float32
    pos_row = np.repeat(np.arange(LAT // GRID_W), GRID_W).astype(f)
    pos_col = np.tile(np.arange(GRID_W), LAT // GRID_W).astype(f)

    def rope(dim, reps):
        q = dim // 4
        freqs = (1.0 / (np.float32(10000.0) ** (np.arange(q, dtype=f) / q))).astype(f)
        cos, sin = [], []
        for pos in (pos_row, pos_col):
            ang = (pos[None, :] * freqs[:, None]).astype(f)
            cos += [np.cos(ang), np.cos(ang)]
            sin += [-np.sin(ang), np.sin(ang)]
        one = np.stack([np.concatenate(cos), np.concatenate(sin)], 1).astype(f)
        return np.tile(one, (reps, 1, 1))

    def feats(n):
        t = np.arange(n, dtype=f)
        ang = (f(TWO_PI / n) * t[:, None] * np.arange(1, 17, dtype=f)).astype(f)
        lin = t / f(n - 1)
        return np.concatenate([lin[:, None], np.cos(ang), -np.sin(ang)], -1).T.astype(f), lin

    f_lat, lin_lat = feats(LAT)
    f_ctx, lin_ctx = feats(CTX)
    u = np.arange(128)
    tok = [2 * (128 * half + u) + par for par in range(2) for half in range(2)]
    negt = np.stack([-lin_lat[t] for t in tok] + [-lin_ctx], 1).astype(f)
    mask = np.ones((128, NT), f)
    mask[0, 0] = mask[0, 4] = 0.0
    k = np.arange(256)
    ang = lambda t: np.pi * np.outer(t, 2 * k + 1) / 1024
    fwd = np.stack([np.stack([np.cos(ang(t)), np.sin(ang(t))], 1) for t in tok], 1).astype(f)
    angc = np.pi * np.outer(u, 2 * u + 1) / 256
    fwdc = np.stack([np.cos(angc), np.sin(angc)], 1).astype(f)
    inv = np.zeros((128, 2, 2, 512), f)
    for m in range(2):
        for q, fn in enumerate((np.cos, np.sin)):
            for par in range(2):
                t = 2 * np.arange(256) + par
                inv[:, m, q, 256 * par:256 * par + 256] = fn(
                    np.pi * np.outer(2 * (128 * m + u) + 1, t) / 1024) / 512
    invc = np.stack([fn(np.pi * np.outer(2 * u + 1, u) / 256) / 128 for fn in (np.cos, np.sin)], 1).astype(f)
    lam = np.stack([[0.8 - 0.6 * math.exp(-0.3 * l), 0.2 + 0.6 * math.exp(-0.3 * l)] for l in range(DEPTH)])
    return {
        "ident": np.eye(128, dtype=f), "ones": np.ones((128, 128), f),
        "rope_da": rope(DHD, 2), "rope_m": rope(MR, 1),
        "feats": np.concatenate([f_lat, f_ctx], 1), "negt": negt, "hmask": mask,
        "fwd": fwd, "fwdc": fwdc, "inv": inv, "invc": invc, "lam_init": lam.astype(f),
    }


def build(nc, A, O):
    f32, f32r = mybir.dt.float32, mybir.dt.float32r
    ALU = mybir.AluOpType
    ACT = mybir.ActivationFunctionType
    AX = mybir.AxisListType.X
    o_prompt, o_sample, o_k, o_v, o_ckv, o_kr = O
    x_mid = nc.dram_tensor("x_mid", (128, NT * D), f32, kind="Internal").ap()

    ctx = ExitStack()
    with ctx:
        at = [(nc.sbuf_base + 31) // 32 * 32]

        def sb(name, shape, dtype=f32, over=None):
            if over is None:
                over = at[0]
                at[0] += -(-int(np.prod(shape[1:])) * 4 // 32) * 32
                assert at[0] <= nc.sbuf_usable_end, name
            return nc.alloc_sbuf_tensor_at(name, shape, dtype, offset=over)

        Hh_at = at[0]
        Hh = sb("Hh", [128, KD, NTOK], f32r)
        Hl = sb("Hl", [128, KD, NTOK], f32r)
        pmod_w = sb("pmod_w", [128, NP, 2, KD, 128], over=Hh_at)
        W = sb("W", [128, NW, KD, 128])
        Wh = sb("Wh", [128, 2, KD, 128], f32r)
        Wl = sb("Wl", [128, 2, KD, 128], f32r)
        MG = sb("MG", [128, KD * NTOK])
        br_at = at[0]
        BRh = sb("BRh", [128, CT, NTOK], f32r)
        BRl = sb("BRl", [128, CT, NTOK], f32r)
        BR = sb("BR", [128, 2 * CT * NTOK], over=br_at)
        raw = sb("raw", [128, 2, 644])
        th = sb("th", [128, 2, NTOK])
        ident = sb("ident", [128, 128])
        ones = sb("ones", [128, 128])
        rope_m = sb("rope_m", [96, 2, LAT])
        negt = sb("negt", [128, NT])
        hmask = sb("hmask", [128, NT])
        ccol = sb("ccol", [128, KD, 2])
        csig = sb("csig", [128, KD, 2])
        modcs = sb("modc", [128, 2, 3 * KD, 2])
        fold = sb("fold", [128, KD, 2])
        bmods = sb("b_mod", [128, DEPTH, 3 * KD])
        vecs = sb("vecs", [128, NVEC])
        convw = vec(vecs, "hy_conv_w").rearrange("p (a b) -> p a b", a=3)
        convb = vec(vecs, "hy_conv_b")
        skip = vec(vecs, "hy_skip").rearrange("p (a b) -> p a b", a=2)
        fvec = vec(vecs, "hy_ffn")[0:HY_FFN]
        subln = vec(vecs, "da_subln")
        qn = vec(vecs, "mla_q_norm")
        kvn = vec(vecs, "mla_kv_norm")
        fw1 = sb("fw1", [POS, HY_FFN])
        fw2 = sb("fw2", [HY_FFN, HY_FFN])
        lp = sb("lp", [128, 4, DHD])
        lpj = sb("lpj", [128, 2, DHD])
        lamc = sb("lamc", [128, 8])
        st = sb("st", [128, LAG + 1, 8])
        lnst = sb("lnst", [128, NT, 2, 6])
        lnmv = sb("lnmv", [128, NT, 2])
        lnr = sb("lnr", [128, NT])
        work_at = at[0]
        WORK = 20640
        work = sb("work", [128, WORK])

        def area(base, off, *dims):
            n = int(np.prod(dims))
            ap = base[:, off:off + n]
            if len(dims) == 1:
                return ap
            names = "abcd"[:len(dims)]
            return ap.rearrange(f"p ({' '.join(names)}) -> p {' '.join(names)}",
                                **{c: d for c, d in zip(names, dims)})

        pmrow = area(work, 12816, 4, 256)[0:2]
        ln_gc, ln_bc = vec(vecs, "ln_g"), vec(vecs, "ln_b")
        ZP = LAT + 2
        V4 = area(work, 0, CT, 642)
        G4 = area(work, 2568, CT, 642)
        feats = area(work, 5136, NTOK)[0:POS]
        rr = area(work, 5776, 2, NTOK)[0:HY_FFN]
        zT = area(work, 5136, NT, HY)
        tB, tC = area(work, 5136, 1024), area(work, 6160, 1024)
        PM = area(work, 7696, 2, 2, 1024)
        PMc = area(work, 11792, 2, HY)
        fab = area(work, 7696, 2, NT, HY)
        HS = area(work, 12816, 2, 2, 1024)
        HSc = area(work, 16912, 2, HY)
        decay = area(work, 17936, 2, HY)
        oddb = area(work, 18960, 2, HY)
        fwdc = area(work, 19984, 2, 128)
        invc = area(work, 20240, 2, 128)
        w3 = area(BR, 0, 2, 2, HY)[0:HY_FFN]
        expld = area(BR, 2048, 2, 2, HY)
        hid = area(BR, 4096, NTOK)[0:HY_FFN]
        fwd = area(MG, 0, 4, 2, 256)
        inv = area(MG, 2048, 2, 2, 512)
        tconv = area(MG, 4096, 642)
        path_th = area(BR, 0, CT, NTOK)
        path_x = area(BR, CT * NTOK, CT, NTOK)
        qT = area(work, 0, 4, NTOK)
        kT = area(work, 2560, 4, NKEY)
        V = area(work, 5632, 6, 512)
        E = [area(work, off, 2, NTOK) for off in (8704, 8704 + 2 * NTOK, 17664)]
        PT = area(work, 11264, NT, LAT)
        PTc = area(work, 13824, 2, 128)
        OT = area(work, 14080, 4, NTOK)
        ckc = area(work, 16640, 512)
        stk = area(work, 17152, 512)
        swp = area(work, 17664, LAT)
        rope_da = area(work, 18176, 2, LAT)
        sqd = area(work, 19200, 2, NTOK)
        msd = raw[:, 0, 0:NTOK]
        Y = area(work, 0, 4, NTOK)
        cq = area(work, 2560, 3, NTOK)
        ckv = area(work, 4480, 2, NKEY)
        Vm = area(work, 6016, 6, 512)
        mkT = area(work, 9088, 2, NKEY)
        wukv = area(work, 10624, 2, 1024)
        mqT = area(work, 12672, 2, NTOK)
        Em = [area(work, 13952, NTOK), area(work, 13952 + NTOK, NTOK), raw[:, 0, 0:NTOK]]
        PTm = area(work, 15232, NT, LAT)
        PTmc = area(work, 17792, 2, 128)
        wuq = area(work, 18176, 3, 768)
        sqm = area(work, 0, 3, NTOK)
        stc = area(work, 1920, KVL + MR)
        msm = area(work, 12672, NTOK)
        cc = area(work, 17216, KVL)
        ckr = area(work, 17472, MR)
        krs = raw[0:MR, 0, 0:NTOK]
        swm = raw[:, 1, 0:LAT]
        krt = Vm[0:MR, 0, 0:LAT]
        X = area(work, 0, NT, D)
        lng = area(work, 5120, D)
        lnb = area(work, 6144, D)
        MGh = sb("MGh", [128, KD, NTOK], f32r, over=work_at + 4 * 7168)
        MGl = sb("MGl", [128, KD, NTOK], f32r, over=work_at + 4 * 12288)
        rT = raw

        PS = [ctx.enter_context(nc.psum_tensor(f"PS{i}", [128, 1024], f32)) for i in range(SLOTS)]

        sems = {}

        def sem(name):
            sems[name] = ctx.enter_context(nc.semaphore(name))
            return sems[name]

        for name in PER:
            sem(name)
        full = [sem(f"psum_full{i}") for i in range(SLOTS)]
        w_here = [sem(f"weights_here{i}") for i in range(NW)]
        pmod_here = [sem(f"first_modulation_here{i}") for i in range(NP)]
        x_saved = sem("x_saved")
        consts_here = sem("consts_here")
        rope_here = sem("rope_here")
        x_here = sem("x_here")
        small_here = sem("small_here")
        hy_here = sem("hyena_tables_here")
        feats_here = sem("filter_positions_here")
        da_here = sem("da_cache_here")
        da_rope_here = sem("da_rope_here")
        ml_here = sem("mla_weights_here")
        ln_here = sem("ln_weights_here")
        c_sig = sem("c_sig")
        c_silu = sem("c_silu")
        store_k = sem("store_k")
        store_c = sem("store_c")
        store_y = sem("store_y")
        act_chain = sem("act_chain")
        dve_chain = sem("dve_chain")
        chain = {"act": 0, "dve": 0}

        def after(name, l, count):
            return sems[name], l * PER[name] + count

        def filled(l, kind, i, j=0):
            s, u, _ = SLOT[l, kind, i, j]
            return full[s], u + 1

        def full_of(l, kind, i, j=0):
            return full[SLOT[l, kind, i, j][0]]

        def freed(l, kind, i, j=0):
            before = SLOT[l, kind, i, j][2]
            return (sems[before[0]], before[1]) if before else (consts_here, 16 * N_CONSTS)

        def tile_done(l, n):
            l, n = (l, n) if n >= 0 else (l - 1, n + NSPLIT)
            return filled(l, *SPLIT[n])

        def slot(l, kind, i, j=0):
            return PS[SLOT[l, kind, i, j][0]]

        def halves(ap):
            return ap.rearrange("p (a b) -> p a b", a=2)

        def two(ps, n=HALF, p=128):
            return ps[0:p, :].rearrange("p (a b) -> p a b", a=2)[:, :, 0:n]

        block = ctx.enter_context(nc.Block())

        N_CONSTS, N_SMALL, N_HY, N_DA, N_ML = 6, 5, 6, 2, 4

        @block.sync
        def _(sp):
            def weight(g):
                l, step, i, (kind, n) = STREAM[g]
                if g >= NW:
                    lb, sb_, ib, (kb, _) = STREAM[g - NW]
                    if kb == "mod":
                        sp.wait_ge(*filled(lb, sb_, ib))
                    else:
                        sp.wait_ge(*after("w_lo", lb, SPLIT_AT[sb_, ib] + 1))
                src = A[{"mod": "w_mod", "in": "w_in", "br": "w_branch", "out": "w_out"}[kind]]
                src = src[l + (step == "nmod"), n]
                sp.dma_start(W[:, g % NW, 0:src.shape[1], :], src).then_inc(w_here[g % NW], 16)

            def first_modulation(g):
                if g >= NP:
                    sp.wait_ge(*filled(0, "pmrow", g - NP))
                sp.dma_start(pmod_w[:, g % NP], A["w_mod"][0, 2 * g:2 * g + 2].rearrange("m p k n -> p m k n"))\
                  .then_inc(pmod_here[g % NP], 16)

            for t, s in ((csig, "cvec"), (ident, "ident"), (ones, "ones"), (negt, "negt"), (hmask, "hmask"),
                         (bmods, "b_mod")):
                sp.dma_start(t[:], A[s]).then_inc(consts_here, 16)
            first_modulation(0)

            def load_x(l):
                if l == 0:
                    sp.dma_start(X[:, 0:4, :], A["x_sample"][0].rearrange("(t p) d -> p t d", p=128))\
                      .then_inc(x_here, 16)
                    sp.dma_start(X[:, 4, :], A["x_prompt"][0]).then_inc(x_here, 16)
                else:
                    sp.dma_start(X, x_mid.rearrange("p (t d) -> p t d", t=NT)).then_inc(x_here, 32)

            FIRST = (0, 2, 3)

            def layer_tables(l):
                small = [(vecs[:], A["vecs"][l]), (fw1[:], A["hy_ffn_w1"][l]), (fw2[:], A["hy_ffn_w2"][l]),
                         (lp[:].rearrange("p a b -> p (a b)"),
                          A["da_lambda"][l].rearrange("a b -> (a b)").partition_broadcast(128)),
                         (lamc[:, 0:2], A["lam_init"][l].partition_broadcast(128))]
                assert len(small) == N_SMALL
                for dst, src in small:
                    sp.dma_start(dst, src).then_inc(small_here, 16)
                for n, (dst, src) in enumerate(((feats, A["feats"]),
                                                (w3.rearrange("p a b c -> p (a b c)"), A["hy_ffn_w3"][l]),
                                 (expld.rearrange("p a b c -> p (a b c)"),
                                  A["hy_log_decay"][l].partition_broadcast(128)),
                                 (fwd, A["fwd"]), (fwdc, A["fwdc"]), (invc, A["invc"]), (inv, A["inv"]))):
                    if n:
                        sp.dma_start(dst, src).then_inc(hy_here, 16)
                    else:
                        sp.dma_start(dst, src).then_inc(feats_here, 16)
                    if l == 0 and n in FIRST:
                        first_modulation(1 + FIRST.index(n))

            def norm_rows(l):
                sp.dma_start(lng, A["ln_g"][l].partition_broadcast(128)).then_inc(ln_here, 16)
                sp.dma_start(lnb, A["ln_b"][l].partition_broadcast(128)).then_inc(ln_here, 16)

            layer_tables(0)
            for g in range(1 + len(FIRST), NP):
                first_modulation(g)
            load_x(0)
            for g in range(NP, KD):
                first_modulation(g)
            for t, s in ((rope_m[0:MR], "rope_m"), (rope_m[64:96], "rope_m")):
                sp.dma_start(t, A[s]).then_inc(rope_here, 16)

            for l in range(DEPTH):
                for kind, i in STEPS[l]:
                    if (kind, i) == ("conv", 1) and l:
                        sp.wait_ge(*after("x_ready", l - 1, 5))
                        sp.dma_start(x_mid.rearrange("p (t d) -> p t d", t=NT), X).then_inc(x_saved, 16)
                    if (kind, i) == ("wo", 2) and l < DEPTH - 1:
                        sp.wait_ge(*after("mg_ready", l, KD))
                        sp.wait_ge(*filled(l, "mbranch", 3 * KD - 1))
                        if l:
                            sp.wait_ge(*after("ln_scaled", l - 1, NT))
                        layer_tables(l + 1)
                    if (kind, i) == ("qk", 2):
                        sp.wait_ge(*after("y_ready", l, 2))
                        sp.dma_start(rope_da, A["rope_da"]).then_inc(da_rope_here, 16)
                    if (kind, i) == ("qk", 6):
                        sp.wait_ge(*after("gate_used", l, 4))
                        sp.dma_start(ckc, A["cache_diff_k"][0, l].rearrange("t a h d -> t (a h d)"))\
                          .then_inc(da_here, 16)
                        sp.dma_start(V[:, 0, :], A["cache_diff_v"][0, l].rearrange("t h d -> t (h d)"))\
                          .then_inc(da_here, 16)
                    if (kind, i) == ("mbranch", 2):
                        sp.wait_ge(*after("sk_ready", l, 1))
                        sp.wait_ge(*after("v_ready", l, 4))
                        sp.dma_start(o_k[0, l].rearrange("t a h d -> t (a h d)"), stk).then_inc(store_k, 16)
                        sp.dma_start(o_v[0, l].rearrange("t h d -> t (h d)"), V[:, 5, :]).then_inc(store_k, 16)
                    if (kind, i) == ("dqkv", 3):
                        sp.wait_ge(*filled(l, "dams", 3))
                        sp.wait_ge(store_k, 32 * (l + 1))
                        for dst, src in ((wuq, A["mla_w_uq"][l].rearrange("(k p) n -> p k n", p=128)),
                                         (wukv, A["mla_w_ukv"][l].rearrange("(k p) n -> p k n", p=128)),
                                         (cc, A["cache_mla_ckv"][0, l]), (ckr, A["cache_mla_krope"][0, l])):
                            sp.dma_start(dst, src).then_inc(ml_here, 16)
                    if (kind, i) == ("mbranch", KD + 2):
                        sp.wait_ge(*after("sc_ready", l, 1))
                        sp.dma_start(o_ckv[0, l], stc[:, 0:KVL]).then_inc(store_c, 16)
                        sp.dma_start(o_kr[0, l], stc[:, KVL:KVL + MR]).then_inc(store_c, 16)
                    if (kind, i) == ("mgate", 2 * KD + 3):
                        sp.wait_ge(*after("gate_used", l, 28))
                        sp.wait_ge(store_c, 32 * (l + 1))
                        if l:
                            norm_rows(l - 1)
                        load_x(l)
                    if (kind, i) == ("wo", 2) and l == DEPTH - 1:
                        sp.wait_ge(*after("ln_scaled", l - 1, NT))
                        norm_rows(l)
                    for n in range(len(owned(kind, i))):
                        weight(TILE_AT[l, kind, i] + n)
            for t in range(NT):
                sp.wait_ge(*after("x_ready", DEPTH - 1, t + 1))
                out = o_sample[0, 128 * t:128 * t + 128] if t < 4 else o_prompt[0]
                sp.dma_start(out, X[:, t, :]).then_inc(store_y, 16)
            sp.wait_ge(store_y, 16 * NT)

        @block.tensor
        def _(pe):
            def project(l, kind, i, xh, xl, k):
                n = SPLIT_AT[kind, i]
                b = n % 2
                ps = slot(l, kind, i)
                halves_of = [(ps[:, 512 * a:512 * a + HALF], slice(HALF * a, HALF * a + HALF)) for a in range(2)]
                pe.wait_ge(*after("w_hi", l, n + 1))
                pe.wait_ge(*freed(l, kind, i))
                for kk in range(k):
                    if (kind, i) == ("conv", 0):
                        pe.wait_ge(*after("h_odd" if kk % 2 else "h_even", l, kk // 2 + 1))
                    for out, t in halves_of:
                        pe.matmul(out, Wh[:, b, kk, :], xh[:, kk, t], start=kk == 0, stop=False)
                        pe.matmul(out, Wh[:, b, kk, :], xl[:, kk, t], start=False, stop=False)
                pe.wait_ge(*after("w_lo", l, n + 1))
                for kk in range(k):
                    for out, t in halves_of:
                        last = pe.matmul(out, Wl[:, b, kk, :], xh[:, kk, t], start=False, stop=kk == k - 1)
                last.then_inc(full_of(l, kind, i), 1)

            def sums(ps, i, squares):
                for a in range(2):
                    for k, sq in enumerate(squares):
                        last = pe.matmul(ps[32 * i:32 * i + 32, 512 * a:512 * a + HALF], ones[:, 0:32],
                                         sq[:, HALF * a:HALF * a + HALF], start=k == 0, stop=k == len(squares) - 1)
                return last

            def spread(ps, i, rows):
                for a in range(2):
                    last = pe.matmul(ps[:, 512 * a:512 * a + HALF], ones[32 * i:32 * i + 1, :],
                                     rows[32 * i:32 * i + 1, HALF * a:HALF * a + HALF], start=True, stop=True)
                return last

            def transpose(out, in_, p=128):
                return pe.transpose(out, in_, ident[0:p, 0:p])

            def dft(l, kind, i, srcs):
                pe.wait_ge(*freed(l, kind, i))
                ps = slot(l, kind, i)
                if i % 5 < 4:
                    q, m = divmod(i % 5, 2)
                    for par in range(2):
                        for half in range(2):
                            t = 2 * par + half
                            last = pe.matmul(ps[:, 512 * par:512 * par + HY], fwd[:, t, q, 128 * m:128 * m + 128],
                                             srcs[q][:, t, :], start=half == 0, stop=half == 1)
                else:
                    for q in range(2):
                        last = pe.matmul(ps[:, 512 * q:512 * q + HY], fwdc[:, q, :], srcs[q][:, 4, :],
                                         start=True, stop=True)
                last.then_inc(full_of(l, kind, i), 1)

            def keys(t):
                return (0, LKEY) if t < 4 else (LKEY, CTX)

            def scores(ps, q, k, t):
                k0, n = keys(t)
                if t == 4:
                    return pe.matmul(ps[:, 0:n], q[:, 128 * t:128 * t + 128], k[:, k0:k0 + n], start=True, stop=True)
                for a in range(2):
                    last = pe.matmul(ps[:, 512 * a:512 * a + HALF], q[:, 128 * t:128 * t + 128],
                                     k[:, HALF * a:HALF * a + HALF], start=True, stop=True)
                return last

            def ptrans(l, kind, u, P):
                pe.wait_ge(*freed(l, kind, u))
                ps = slot(l, kind, u)
                for kt in range(NT if u % NT < 4 else 1):
                    last = transpose(ps[:, 128 * kt:128 * kt + 128], P[:, 128 * kt:128 * kt + 128])
                last.then_inc(full_of(l, kind, u), 1)

            def values(l, kind, h, v, c0, m, pt, ptc):
                pe.wait_ge(*freed(l, kind, h))
                ps = slot(l, kind, h)
                for kt in range(NT):
                    pe.matmul(ps[0:m, 0:LAT], v[:, kt, c0:c0 + m], pt[:, kt, :], start=kt == 0, stop=kt == NT - 1)
                pe.matmul(ps[0:m, LAT:NTOK], v[:, 5, c0:c0 + m], ptc, start=True, stop=True)\
                    .then_inc(full_of(l, kind, h), 1)

            pe.wait_ge(consts_here, 16 * N_CONSTS)
            pe.wait_ge(c_silu, 1)
            for l in range(DEPTH):
                for kind, i in STEPS[l]:
                    if kind in ("nmod", "gmod"):
                        pe.wait_ge(*freed(l, kind, i))
                        ps = slot(l, kind, i)
                        g = TILE_AT[l, kind, i]
                        pe.wait_ge(w_here[g % NW], 16 * (g // NW + 1))
                        for k in range(KD):
                            last = pe.matmul(ps[:, 0:2], W[:, g % NW, k, :], ccol[:, k, :],
                                             start=k == 0, stop=k == KD - 1)
                        last.then_inc(full_of(l, kind, i), 1)
                    elif kind == "pmrow":
                        pe.wait_ge(*freed(l, kind, i))
                        ps = slot(l, kind, i)
                        pe.wait_ge(pmod_here[i % NP], 16 * (i // NP + 1))
                        for m in range(2):
                            for k in range(KD):
                                last = pe.matmul(ps[0:2, 128 * m:128 * m + 128], ccol[:, k, :],
                                                 pmod_w[:, i % NP, m, k, :], start=k == 0, stop=k == KD - 1)
                        last.then_inc(full_of(l, kind, i), 1)
                    elif kind == "pmod":
                        pe.wait_ge(*freed(l, kind, i))
                        ps = slot(l, kind, i)
                        pe.wait_ge(*after("row_ready", 0, i + 1))
                        for m in range(2):
                            last = transpose(ps[:, 2 * m:2 * m + 2], pmrow[:, i % 4, 128 * m:128 * m + 128], 2)
                        last.then_inc(full_of(l, kind, i), 1)
                    elif kind == "ht":
                        pe.wait_ge(*freed(l, kind, i))
                        ps = slot(l, kind, i)
                        if i == 0:
                            if l:
                                pe.wait_ge(*after("x_ready", l - 1, 5))
                            else:
                                pe.wait_ge(x_here, 32)
                        for t in range(NT):
                            last = transpose(ps[:, 128 * t:128 * t + 128], X[:, t, 128 * i:128 * i + 128])
                        last.then_inc(full_of(l, kind, i), 1)
                    elif kind == "conv":
                        project(l, kind, i, Hh, Hl, KD)
                    elif kind in ("ffn", "nffn"):
                        at_ = l + (kind == "nffn")
                        pe.wait_ge(*freed(l, kind, i))
                        ps = slot(l, kind, i)
                        if i == 0:
                            pe.wait_ge(small_here, 16 * N_SMALL * (at_ + 1))
                            pe.wait_ge(feats_here, 16 * (at_ + 1))
                        else:
                            pe.wait_ge(*after("hid_ready", at_, 1))
                        for a in range(2):
                            last = pe.matmul(ps[0:HY_FFN, 512 * a:512 * a + HALF], (fw2 if i else fw1)[:],
                                             (hid if i else feats)[:, HALF * a:HALF * a + HALF], start=True, stop=True)
                        last.then_inc(full_of(l, kind, i), 1)
                    elif kind == "filt":
                        o, t = divmod(i, NT)
                        pe.wait_ge(*freed(l, kind, i))
                        ps = slot(l, kind, i)
                        if i == 0:
                            pe.wait_ge(*after("hid_ready", l, 2))
                            pe.wait_ge(hy_here, 16 * N_HY * (l + 1))
                        par, half = divmod(t, 2)
                        hcol = (hid[:, 256 * half + par:256 * half + par + 255:2] if t < 4
                                else hid[:, LAT:NTOK])
                        for d in range(2):
                            last = pe.matmul(ps[:, 512 * d:512 * d + HY], hcol, w3[:, d, o, :], start=True, stop=True)
                        last.then_inc(full_of(l, kind, i), 1)
                    elif kind == "fdft":
                        if i % 5 == 0:
                            pe.wait_ge(*after("fab_ready", l, 5 * (i // 5) + 5))
                        dft(l, kind, i, (fab[:, 0], fab[:, 1]))
                    elif kind == "zt":
                        o, r = divmod(i, 3)
                        pe.wait_ge(*freed(l, kind, i))
                        ps = slot(l, kind, i)
                        if i == 0:
                            pe.wait_ge(*after("conv_ready", l, 4))
                        elif r == 0:
                            pe.wait_ge(*after("z_ready", l, 4 * o))
                        for b in range(2 if r < 2 else 1):
                            for c in range(CT):
                                src = (V4[:, c, 256 * b + r:256 * b + r + 255:2] if r < 2
                                       else V4[:, c, ZP:ZP + CTX])
                                last = transpose(ps[:, 512 * b + 128 * c:512 * b + 128 * c + 128], src)
                        last.then_inc(full_of(l, kind, i), 1)
                    elif kind == "zdft":
                        if i % 5 == 0:
                            pe.wait_ge(*after("zt_ready", l, 3 * (i // 5) + 3))
                        dft(l, kind, i, (zT, zT))
                    elif kind == "inv":
                        o, c = divmod(i, CT)
                        pe.wait_ge(*freed(l, kind, i))
                        ps = slot(l, kind, i)
                        if c == 0:
                            pe.wait_ge(*after("y_ready", l, o + 1))
                        for par in range(2):
                            for n_ in range(4):
                                q, m = divmod(n_, 2)
                                pe.matmul(ps[:, 256 * par:256 * par + 256],
                                          PM[:, par, q, 512 * m + 128 * c:512 * m + 128 * c + 128],
                                          inv[:, m, q, 256 * par:256 * par + 256], start=n_ == 0, stop=n_ == 3)
                        for q in range(2):
                            last = pe.matmul(ps[:, 512:640], PMc[:, q, 128 * c:128 * c + 128], invc[:, q, :],
                                             start=q == 0, stop=q == 1)
                        last.then_inc(full_of(l, kind, i), 1)
                    elif kind == "path":
                        project(l, kind, i, Hh, Hl, KD)
                    elif kind == "mgate":
                        project(l, kind, i, Hh, Hl, KD)
                    elif kind == "mbranch":
                        if i % KD == 0:
                            pe.wait_ge(*after("gate_used", l, 12 * (i // KD) + 4))
                        project(l, kind, i, BRh, BRl, CT)
                    elif kind == "qk":
                        project(l, kind, i, Hh, Hl, KD)
                    elif kind == "kc":
                        pe.wait_ge(*freed(l, kind, i))
                        ps = slot(l, kind, i)
                        pe.wait_ge(da_here, 16 * N_DA * (l + 1))
                        for c in range(4):
                            last = transpose(ps[:, 128 * c:128 * c + 128], ckc[:, 128 * c:128 * c + 128])
                        last.then_inc(full_of(l, kind, i), 1)
                    elif kind == "sk":
                        pe.wait_ge(*freed(l, kind, i))
                        ps = slot(l, kind, i)
                        pe.wait_ge(*after("qk_ready", l, 8))
                        for c in range(4):
                            last = transpose(ps[:, 128 * c:128 * c + 128], kT[:, c, LKEY:NKEY])
                        last.then_inc(full_of(l, kind, i), 1)
                    elif kind == "v":
                        project(l, kind, i, Hh, Hl, KD)
                    elif kind == "vt":
                        pe.wait_ge(*freed(l, kind, i))
                        ps = slot(l, kind, i)
                        pe.wait_ge(*after("raw_ready", l, 9 + i))
                        for t in range(NT):
                            last = transpose(ps[:, 128 * t:128 * t + 128], raw[:, i % 2, 128 * t:128 * t + 128])
                        last.then_inc(full_of(l, kind, i), 1)
                    elif kind == "da_score":
                        h, t = divmod(i, NT)
                        if i == 0:
                            pe.wait_ge(*after("kc_ready", l, 1))
                        p = 64 * (h % 2)
                        for j in range(2):
                            pe.wait_ge(*freed(l, kind, i, j))
                            ps = slot(l, kind, i, j)
                            last = scores(ps, qT[p:p + 64, 2 * j + h // 2], kT[p:p + 64, 2 * j + h // 2], t)
                            last.then_inc(full_of(l, kind, i, j), 1)
                    elif kind == "da_ptrans":
                        pe.wait_ge(*after("da_p", l, i + 1))
                        ptrans(l, kind, i, E[i % (LAG + 1)][:, 0])
                    elif kind == "da_pv":
                        if i == 0:
                            pe.wait_ge(*after("v_ready", l, 4))
                        pe.wait_ge(*after("da_pt", l, NT * (i + 1)))
                        values(l, kind, i, V, 128 * i, 128, PT, PTc[:, i % 2])
                    elif kind == "dams":
                        pe.wait_ge(*freed(l, kind, i))
                        ps = slot(l, kind, i)
                        pe.wait_ge(*after("da_sq", l, i + 1))
                        sums(ps, i, [sqd[:, i % 2]]).then_inc(full_of(l, kind, i), 1)
                    elif kind == "dab":
                        pe.wait_ge(*freed(l, kind, i))
                        pe.wait_ge(*after("da_rc", l, 1))
                        spread(slot(l, kind, i), i, msd).then_inc(full_of(l, kind, i), 1)
                    elif kind == "dqkv":
                        project(l, kind, i, Hh, Hl, KD)
                    elif kind == "kr":
                        project(l, kind, i, Hh, Hl, KD)
                    elif kind == "cc":
                        pe.wait_ge(*freed(l, kind, i))
                        ps = slot(l, kind, i)
                        pe.wait_ge(ml_here, 16 * N_ML * (l + 1))
                        for c in range(2):
                            transpose(ps[:, 128 * c:128 * c + 128], cc[:, 128 * c:128 * c + 128])
                        transpose(ps[0:MR, 512:640], ckr).then_inc(full_of(l, kind, i), 1)
                    elif kind == "mms":
                        pe.wait_ge(*freed(l, kind, i))
                        ps = slot(l, kind, i)
                        pe.wait_ge(*after("c_sq", l, 3 if i == 0 else 5))
                        sums(ps, i, [sqm[:, kk] for kk in range(3 - i)]).then_inc(full_of(l, kind, i), 1)
                    elif kind == "mb":
                        pe.wait_ge(*freed(l, kind, i))
                        pe.wait_ge(*after("m_rc", l, 1))
                        spread(slot(l, kind, i), i, msm).then_inc(full_of(l, kind, i), 1)
                    elif kind == "sc":
                        pe.wait_ge(*freed(l, kind, i))
                        ps = slot(l, kind, i)
                        pe.wait_ge(*after("c_ready", l, 2))
                        for c in range(2):
                            transpose(ps[:, 128 * c:128 * c + 128], ckv[:, c, LKEY:NKEY])
                        transpose(ps[:, 512:512 + MR], krs[:, LAT:NTOK], MR).then_inc(full_of(l, kind, i), 1)
                    elif kind == "mv":
                        if i == 0:
                            pe.wait_ge(*after("cc_ready", l, 2))
                        pe.wait_ge(*freed(l, kind, i))
                        ps = slot(l, kind, i)
                        for b in range(2):
                            t = 2 * i + b
                            for k in range(2):
                                last = pe.matmul(
                                    ps[:, 512 * b:512 * b + 512], ckv[:, k, 128 * t:128 * t + 128],
                                    wukv[:, k, MH * MN:MH * (MN + MV)],
                                    start=k == 0, stop=k == 1)
                        last.then_inc(full_of(l, kind, i), 1)
                    elif kind == "mq":
                        pe.wait_ge(*freed(l, kind, i))
                        ps = slot(l, kind, i)
                        for a in range(2):
                            for k in range(3):
                                last = pe.matmul(ps[0:96, 512 * a:512 * a + HALF], wuq[:, k, 96 * i:96 * i + 96],
                                                 cq[:, k, HALF * a:HALF * a + HALF], start=k == 0, stop=k == 2)
                        last.then_inc(full_of(l, kind, i), 1)
                    elif kind == "mk":
                        pe.wait_ge(*freed(l, kind, i))
                        ps = slot(l, kind, i)
                        n_ = NKEY // 2
                        for a in range(2):
                            for k in range(2):
                                last = pe.matmul(
                                    ps[:, 512 * a:512 * a + n_],
                                    wukv[:, k, 2 * MN * i:2 * MN * (i + 1)],
                                    ckv[:, k, n_ * a:n_ * a + n_], start=k == 0, stop=k == 1)
                        last.then_inc(full_of(l, kind, i), 1)
                    elif kind == "ml_score":
                        h, t = divmod(i, NT)
                        pe.wait_ge(*freed(l, kind, i))
                        ps = slot(l, kind, i)
                        if t == 0:
                            pe.wait_ge(*after("mq_ready", l, h + 1))
                            pe.wait_ge(*after("mk_ready", l, h + 1))
                            pe.wait_ge(*after("kr_ready", l, 1))
                        scores(ps, mqT[0:96, h % 2], mkT[0:96, h % 2], t).then_inc(full_of(l, kind, i), 1)
                    elif kind == "ml_ptrans":
                        pe.wait_ge(*after("ml_p", l, i + 1))
                        ptrans(l, kind, i, Em[i % (LAG + 1)])
                    elif kind == "ml_pv":
                        if i == 0:
                            pe.wait_ge(*after("mv_ready", l, 3))
                        pe.wait_ge(*after("ml_pt", l, NT * (i + 1)))
                        values(l, kind, i, Vm, MV * i, MV, PTm, PTmc[:, i % 2])
                    elif kind == "wo":
                        if i == 0:
                            pe.wait_ge(*after("mg_ready", l, KD))
                        project(l, kind, i, MGh, MGl, KD)
                    elif kind == "xt":
                        pe.wait_ge(*freed(l, kind, i))
                        ps = slot(l, kind, i)
                        pe.wait_ge(*after("r_ready", l, i + 1))
                        for t in range(NT):
                            last = transpose(ps[:, 128 * t:128 * t + 128], rT[:, i % 2, 128 * t:128 * t + 128])
                        last.then_inc(full_of(l, kind, i), 1)

        @block.scalar
        def _(act):
            def link(ins):
                chain["act"] += 1
                ins.then_inc(act_chain, 1)
                act.wait_ge(act_chain, chain["act"])

            def copy(out, in_, scale=1.0):
                return act.activation(out, in_, ACT.Copy, scale=scale)

            def odd_keys(l, pair):
                if pair:
                    act.wait_ge(*filled(l, "ml_score", 2 * NT * pair - 1))
                src = slot(l, "mk", pair)[MN:2 * MN, :].rearrange("p (a b) -> p a b", a=2)[:, :, 0:NKEY // 2]
                copy(halves(mkT[0:MN, 1]), src).then_inc(sems["mk_ready"], 1)

            act.wait_ge(consts_here, 16 * N_CONSTS)
            act.activation(ccol[:], csig[:], ACT.Sigmoid).then_inc(c_sig, 1)

            def high_part(l, n):
                g = TILE_AT[(l, *SPLIT[n])]
                act.wait_ge(w_here[g % NW], 16 * (g // NW + 1))
                if l or n >= 2:
                    act.wait_ge(*tile_done(l, n - 2))
                k = CT if SPLIT[n][0] == "mbranch" else KD
                copy(Wh[:, n % 2, 0:k, :], W[:, g % NW, 0:k, :]).then_inc(sems["w_hi"], 1)

            for l in range(DEPTH):
                split = 0
                for place, (kind, i) in enumerate(STEPS[l]):
                    while split < UPTO.get((l, place), 0):
                        high_part(l, split)
                        split += 1
                    if kind == "pmrow":
                        act.wait_ge(*filled(l, kind, i))
                        if i >= 4:
                            act.wait_ge(*filled(l, "pmod", i - 4))
                        copy(pmrow[:, i % 4], slot(l, kind, i)[0:2, 0:256]).then_inc(sems["row_ready"], 1)
                    elif kind == "lam":
                        act.wait_ge(*after("lam_sum", l, 1))
                        act.activation(lamc[:, 4:6], lamc[:, 4:6], ACT.Exp).then_inc(sems["lam_exp"], 1)
                    elif kind == "ht":
                        act.wait_ge(*after("h_f32", l, i + 1))
                        copy(Hh[:, i, :], th[:, i % 2]).then_inc(sems["h_hi"], 1)
                    elif kind == "conv":
                        act.wait_ge(*filled(l, kind, i))
                        ps = slot(l, kind, i)
                        if i >= 2:
                            act.wait_ge(*after("conv_ready", l, i - 1))
                        elif l:
                            act.wait_ge(*after("x_part", l - 1, 8))
                        if i < 2:
                            act.wait_ge(*after("pad_ready", l, 1))
                        r = raw[:, i % 2, :]
                        copy(r[:, 1:1 + HALF], ps[:, 0:HALF])
                        copy(r[:, 1 + HALF:1 + LAT], ps[:, 512:512 + LAT - HALF])
                        copy(r[:, ZP + 1:ZP + 1 + CTX], ps[:, 512 + LAT - HALF:512 + HALF])\
                            .then_inc(sems["up_ready"], 1)
                    elif kind in ("ffn", "nsin"):
                        act.wait_ge(*after("farg_ready", l + (kind == "nsin"), i + 1))
                        act.activation(hid, rr[:, 0], ACT.Sin).then_inc(sems["hid_ready"], 1)
                    elif kind == "filt":
                        o, t = divmod(i, NT)
                        if i:
                            act.wait_ge(*after("fab_ready", l, i))
                        else:
                            act.wait_ge(hy_here, 16 * N_HY * (l + 1))
                            link(act.activation(expld, expld, ACT.Exp))
                        act.activation(decay, expld[:, :, o, :], ACT.Exp, scale=negt[:, t:t + 1])\
                            .then_inc(sems["decay_ready"], 1)
                    elif kind in ("fdft", "zdft"):
                        n = 10 * (i // 5) + 5 * (kind == "zdft") + i % 5
                        act.wait_ge(*filled(l, kind, i))
                        ps = slot(l, kind, i)
                        if i % 5 < 4:
                            if n >= 2:
                                act.wait_ge(*after("spec_ready", l, n - 1))
                            copy(oddb[:, n % 2], ps[:, 512:1024]).then_inc(sems["odd_ready"], 1)
                        else:
                            dst = HSc if kind == "fdft" else PMc
                            if n >= 2:
                                act.wait_ge(*after("spec_ready", l, n))
                            copy(dst, halves(ps[:, :])).then_inc(sems["spec_ready"], 1)
                            act.nop().then_inc(sems["odd_ready"], 1)
                    elif kind == "zt":
                        o, r = divmod(i, 3)
                        act.wait_ge(*filled(l, kind, i))
                        ps = slot(l, kind, i)
                        if o == 1 and r == 0:
                            act.wait_ge(*after("y_ready", l, 1))
                        if r < 2:
                            copy(zT[:, 2 * r:2 * r + 2, :], halves(ps[:, :])).then_inc(sems["zt_ready"], 1)
                        else:
                            copy(zT[:, 4, :], ps[:, 0:HY]).then_inc(sems["zt_ready"], 1)
                    elif kind in ("path", "mgate"):
                        if kind == "path" and i < CT:
                            act.wait_ge(*filled(l, kind, i))
                            ps = slot(l, kind, i)
                            act.activation(halves(path_th[:, i]), two(ps), ACT.Tanh, scale=0.5)\
                               .then_inc(sems["th_ready"], 1)
                            copy(halves(path_x[:, i]), two(ps)).then_inc(sems["px_ready"], 1)
                            continue
                        n = 12 * (i // 4) + i % 4 if kind == "path" else 12 * (i // 8) + 4 + i % 8
                        act.wait_ge(*filled(l, kind, i))
                        ps = slot(l, kind, i)
                        if n >= 2:
                            act.wait_ge(*after("gate_used", l, n - 1))
                        act.activation(halves(th[:, n % 2]), two(ps), ACT.Tanh, scale=0.5)\
                           .then_inc(sems["th_ready"], 1)
                    elif kind in ("qk", "v"):
                        n = i + 8 * (kind == "v")
                        act.wait_ge(*filled(l, kind, i))
                        ps = slot(l, kind, i)
                        if n >= 10:
                            act.wait_ge(*after("v_ready", l, n - 9))
                        elif n >= 2:
                            act.wait_ge(*after("qk_ready", l, n - 1))
                        copy(halves(raw[:, n % 2, 0:NTOK]), two(ps), DA_SCALE if n < 4 else 1.0)\
                            .then_inc(sems["raw_ready"], 1)
                    elif kind == "kc":
                        act.wait_ge(*filled(l, kind, i))
                        ps = slot(l, kind, i)
                        copy(kT[:, :, 0:PAST], ps[:, 0:512].rearrange("p (a b) -> p a b", a=4))\
                            .then_inc(sems["kc_ready"], 1)
                    elif kind == "sk":
                        act.wait_ge(*filled(l, kind, i))
                        copy(stk, slot(l, kind, i)[:, 0:512]).then_inc(sems["sk_ready"], 1)
                    elif kind == "da_score":
                        n = keysn(i)
                        for j in range(2):
                            act.wait_ge(*filled(l, kind, i, j))
                            ps = slot(l, kind, i, j)
                            act.wait_ge(*after("da_max", l, 2 * i + j + 1))
                            e = E[i % (LAG + 1)][:, j, 0:n]
                            stat = st[:, i % (LAG + 1)]
                            act.activation(two_or_one(e, n), two(ps) if n > CTX else ps[:, 0:n], ACT.Exp,
                                           bias=stat[:, j:j + 1], accum_out=stat[:, 2 + j:3 + j])\
                                .then_inc(sems["da_exp"], 1)
                    elif kind in ("da_ptrans", "ml_ptrans"):
                        h, t = divmod(i, NT)
                        act.wait_ge(*filled(l, kind, i))
                        ps = slot(l, kind, i)
                        da = kind[0] == "d"
                        if t < 4:
                            dst = (PT if da else PTm)[:, :, 128 * t:128 * t + 128]
                            if t == 0 and h:
                                act.wait_ge(*after("da_o" if da else "ml_o", l, h))
                            ins = copy(dst, ps[:, 0:640].rearrange("p (a b) -> p a b", a=NT))
                        else:
                            ins = copy((PTc if da else PTmc)[:, h % 2], ps[:, 0:CTX])
                        ins.then_inc(sems[kind[:2] + "_pt"], 1)
                    elif kind == "da_pv":
                        act.wait_ge(*filled(l, kind, i))
                        copy(OT[:, i], slot(l, kind, i)[:, 0:NTOK]).then_inc(sems["da_o"], 1)
                    elif kind == "dart":
                        act.wait_ge(*after("da_ms", l, 4))
                        act.activation(msd, msd, ACT.Sqrt).then_inc(sems["da_rt"], 1)
                    elif kind == "dqkv":
                        act.wait_ge(*filled(l, kind, i))
                        ps = slot(l, kind, i)
                        dst = cq[:, i] if i < 3 else ckv[:, i - 3, PAST:NKEY]
                        copy(halves(dst), two(ps)).then_inc(sems["c_raw"], 1)
                    elif kind == "kr":
                        act.wait_ge(*filled(l, kind, i))
                        copy(halves(krs), two(slot(l, kind, i), p=MR)).then_inc(sems["kr_raw"], 1)
                    elif kind == "cc":
                        act.wait_ge(*filled(l, kind, i))
                        ps = slot(l, kind, i)
                        copy(ckv[:, :, 0:PAST], ps[:, 0:256].rearrange("p (a b) -> p a b", a=2))\
                            .then_inc(sems["cc_ready"], 1)
                        for b in range(2):
                            last = copy(mkT[64:96, b, 0:PAST], ps[0:MR, 512:640])
                        last.then_inc(sems["cc_ready"], 1)
                    elif kind == "mrt":
                        act.wait_ge(*after("m_ms", l, 2))
                        act.activation(msm[0:64], msm[0:64], ACT.Sqrt).then_inc(sems["m_rt"], 1)
                    elif kind == "sc":
                        act.wait_ge(*filled(l, kind, i))
                        ps = slot(l, kind, i)
                        copy(stc[:, 0:KVL], ps[:, 0:KVL])
                        copy(stc[:, KVL:KVL + MR], ps[:, 512:512 + MR]).then_inc(sems["sc_ready"], 1)
                    elif kind == "mv":
                        if i == 0:
                            act.wait_ge(store_k, 32 * (l + 1))
                            act.wait_ge(*after("br_f32", l, 8))
                        act.wait_ge(*filled(l, kind, i))
                        copy(Vm[:, 2 * i:2 * i + 2, :], halves(slot(l, kind, i)[:, :])).then_inc(sems["mv_ready"], 1)
                    elif kind == "mq":
                        act.wait_ge(*filled(l, kind, i))
                        copy(halves(mqT[0:96, i % 2]), two(slot(l, kind, i), p=96), MLA_SCALE)\
                            .then_inc(sems["mq_raw"], 1)
                    elif kind == "mk":
                        act.wait_ge(*filled(l, kind, i))
                        copy(halves(mkT[0:MN, 0]), two(slot(l, kind, i), NKEY // 2, MN)).then_inc(sems["mk_ready"], 1)
                        if i == 0:
                            odd_keys(l, i)
                    elif kind == "ml_score":
                        n = keysn(i)
                        act.wait_ge(*filled(l, kind, i))
                        ps = slot(l, kind, i)
                        act.wait_ge(*after("ml_max", l, i + 1))
                        stat = st[:, i % (LAG + 1)]
                        act.activation(two_or_one(Em[i % (LAG + 1)][:, 0:n], n), two(ps) if n > CTX else ps[:, 0:n],
                                       ACT.Exp, bias=stat[:, 0:1], accum_out=stat[:, 2:3])\
                           .then_inc(sems["ml_exp"], 1)
                        h, t = divmod(i, NT)
                        if t == NT - 1 and h % 2 and h + 1 < MH:
                            odd_keys(l, (h + 1) // 2)
                    elif kind == "ml_pv":
                        p = 64 * (i % 2)
                        if i == 6:
                            act.wait_ge(store_c, 32 * (l + 1))
                        act.wait_ge(*filled(l, kind, i))
                        copy(Y[p:p + 64, i // 2], slot(l, kind, i)[0:MV, 0:NTOK]).then_inc(sems["ml_o"], 1)
                    elif kind == "wo":
                        act.wait_ge(*filled(l, kind, i))
                        ps = slot(l, kind, i)
                        if i == 0:
                            act.wait_ge(*after("g_ready", l, KD))
                        if i >= 2:
                            act.wait_ge(*after("x_part", l, i - 1))
                        r, g = rT[:, i % 2, :], modcs[:, l % 2, 2 * KD + i, :]
                        copy(r[:, 0:HALF], ps[:, 0:HALF], g[:, 0:1])
                        copy(r[:, HALF:LAT], ps[:, 512:512 + LAT - HALF], g[:, 0:1])
                        copy(r[:, LAT:NTOK], ps[:, 512 + LAT - HALF:512 + HALF], g[:, 1:2])\
                            .then_inc(sems["r_ready"], 1)
                    elif kind == "ln":
                        act.wait_ge(*after("ln_var", l, 1))
                        act.activation(lnr[:], lnr[:], ACT.Sqrt).then_inc(sems["ln_rt"], 1)

        @block.vector
        def _(dve):
            def link(ins):
                chain["dve"] += 1
                ins.then_inc(dve_chain, 1)
                dve.wait_ge(dve_chain, chain["dve"])

            signalled = {}

            def own(name):
                signalled[name] = signalled.get(name, 0) + 1
                return sems[name], signalled[name]

            TT, TS, STT = dve.tensor_tensor, dve.tensor_scalar, dve.scalar_tensor_tensor

            def softmax_max(ps, n, out):
                return dve.tensor_reduce(out, two(ps) if n > CTX else ps[:, 0:n],
                                         mybir.AxisListType.XY if n > CTX else AX, ALU.max, negate=True)

            def da_weights(l, u):
                n, s, e = keysn(u), st[:, u % (LAG + 1)], E[u % (LAG + 1)]
                dve.wait_ge(*after("da_exp", l, 2 * u + 2))
                link(dve.reciprocal(s[:, 4:6], s[:, 2:4]))
                link(TT(s[:, 6:7], s[:, 5:6], lamc[:, 6:7], ALU.mult))
                link(TS(e[:, 0, 0:n], e[:, 0, 0:n], s[:, 4:5], None, ALU.mult))
                STT(e[:, 0, 0:n], e[:, 1, 0:n], s[:, 6:7], e[:, 0, 0:n], ALU.mult, ALU.add).then_inc(sems["da_p"], 1)
                dve.wait_ge(*own("da_p"))

            def ml_weights(l, u):
                n, s, e = keysn(u), st[:, u % (LAG + 1)], Em[u % (LAG + 1)]
                dve.wait_ge(*after("ml_exp", l, u + 1))
                link(dve.reciprocal(s[:, 4:5], s[:, 2:3]))
                TS(e[:, 0:n], e[:, 0:n], s[:, 4:5], None, ALU.mult).then_inc(sems["ml_p"], 1)
                dve.wait_ge(*own("ml_p"))

            dve.wait_ge(consts_here, 16 * N_CONSTS)
            dve.wait_ge(c_sig, 1)
            TT(ccol[:], ccol[:], csig[:], ALU.mult).then_inc(c_silu, 1)

            def clear_pads():
                dve.memset(raw[:, :, 0:1], 0.0)
                dve.memset(raw[:, :, LAT + 1:LAT + 3], 0.0)
                return dve.memset(raw[:, :, 643:644], 0.0)

            for l in range(DEPTH):
                for kind, i in STEPS[l]:
                    if kind in ("pmod", "nmod", "gmod"):
                        dve.wait_ge(*filled(l, kind, i))
                        ps = slot(l, kind, i)
                        at_ = l + (kind == "nmod")
                        for j in range(2 if kind == "pmod" else 1):
                            m = {"pmod": 2 * i + j, "nmod": i, "gmod": 2 * KD + i}[kind]
                            second = ((None, ALU.add), (1.0, ALU.add, ALU.add), (0.5, ALU.add, ALU.mult))[m // KD]
                            TS(modcs[:, at_ % 2, m, :], ps[:, 2 * j:2 * j + 2], bmods[:, at_, m:m + 1], *second)\
                                .then_inc(sems["g_ready" if kind == "gmod" else "ss_ready"], 1)
                    elif kind == "lam":
                        dve.wait_ge(small_here, 16 * N_SMALL * (l + 1))
                        clear_pads().then_inc(sems["pad_ready"], 1)
                        dve.wait_ge(*own("pad_ready"))
                        if l:
                            dve.wait_ge(*after("ss_ready", l, 2 * KD))
                            shift, scale = modcs[:, l % 2, 0:KD, :], modcs[:, l % 2, KD:2 * KD, :]
                            wide = lambda v: v.rearrange("p (m c) -> p m c", c=1).to_broadcast([128, KD, 2])
                            link(TT(fold[:], scale, wide(ln_bc), ALU.mult))
                            link(TT(shift, shift, fold[:], ALU.add))
                            link(TT(scale, scale, wide(ln_gc), ALU.mult))
                        link(TT(lpj[:], lp[:, 0:4:2, :], lp[:, 1:4:2, :], ALU.mult))
                        link(dve.tensor_reduce(lamc[:, 2:4], lpj[:], AX, ALU.add))
                        TS(lamc[:, 4:6], lamc[:, 2:4], 1.0, None, ALU.mult).then_inc(sems["lam_sum"], 1)
                        dve.wait_ge(*own("lam_sum"))
                    elif kind == "ht":
                        dve.wait_ge(*filled(l, kind, i))
                        ps = slot(l, kind, i)
                        s, b = modcs[:, l % 2, KD + i, :], modcs[:, l % 2, i, :]
                        if i == 0:
                            dve.wait_ge(*after("ss_ready", l, 2 * KD))
                        if i >= 2 and i % 2 == 0:
                            dve.wait_ge(*after("h_even", l, i // 2))
                        h = th[:, i % 2]
                        TS(h[:, 0:LAT], ps[:, 0:LAT], s[:, 0:1], b[:, 0:1], ALU.mult, ALU.add)
                        TS(h[:, LAT:NTOK], ps[:, LAT:NTOK], s[:, 1:2], b[:, 1:2], ALU.mult, ALU.add)\
                            .then_inc(sems["h_f32"], 1)
                        dve.wait_ge(*own("h_f32"))
                        odd = {2: 1, 4: 3, 6: 5, 7: 7}.get(i)
                        if odd:
                            dve.wait_ge(*after("h_hi", l, odd + 1))
                            TT(Hl[:, odd, :], th[:, 1], Hh[:, odd, :].bitcast(f32), ALU.subtract)\
                                .then_inc(sems["h_odd"], 1)
                            dve.wait_ge(*own("h_odd"))
                    elif kind == "conv":
                        dve.wait_ge(*after("up_ready", l, i + 1))
                        r = raw[:, i % 2, :]
                        dst = V4[:, i] if i < 4 else G4[:, i % 4]
                        w = lambda tap: convw[:, tap, i:i + 1]
                        if l and i == 0:
                            dve.wait_ge(x_saved, 16)
                        link(TS(tconv, r[:, 1:643], w(1), convb[:, i:i + 1], ALU.mult, ALU.add))
                        link(STT(tconv, r[:, 0:642], w(0), tconv, ALU.mult, ALU.add))
                        STT(dst, r[:, 2:644], w(2), tconv, ALU.mult, ALU.add).then_inc(sems["conv_ready"], 1)
                        dve.wait_ge(*own("conv_ready"))
                    elif kind in ("ffn", "nffn"):
                        dve.wait_ge(*filled(l, kind, i))
                        ps = slot(l, kind, i)
                        a, k = rr[:, 0], rr[:, 1]
                        if i:
                            dve.wait_ge(*after("hid_ready", l + (kind == "nffn"), 1))
                        link(TS(halves(a), two(ps, p=HY_FFN), fvec[:, i:i + 1], fvec[:, 2 + i:3 + i],
                                ALU.add, ALU.mult))
                        link(TS(k, a, 1 / TWO_PI, MAGIC, ALU.mult, ALU.add))
                        link(TS(k, k, MAGIC, None, ALU.subtract))
                        for part in (PI_HI, PI_MID, PI_LO):
                            link(STT(a, k, -part, a, ALU.mult, ALU.add))
                        TS(a, a, math.pi - 1e-6, -(math.pi - 1e-6), ALU.min, ALU.max).then_inc(sems["farg_ready"], 1)
                        dve.wait_ge(*own("farg_ready"))
                    elif kind == "filt":
                        o, t = divmod(i, NT)
                        dve.wait_ge(*filled(l, kind, i))
                        ps = slot(l, kind, i)
                        dve.wait_ge(*after("decay_ready", l, i + 1))
                        TT(oddb[:, 0], ps[:, 0:HY], decay[:, 0], ALU.mult)
                        link(STT(oddb[:, 1], ps[:, 512:1024], hmask[:, t:t + 1], decay[:, 1], ALU.mult, ALU.mult))
                        TT(fab[:, 0, t], oddb[:, 0], oddb[:, 1], ALU.add)
                        TT(fab[:, 1, t], oddb[:, 0], oddb[:, 1], ALU.subtract).then_inc(sems["fab_ready"], 1)
                        dve.wait_ge(*own("fab_ready"))
                    elif kind in ("fdft", "zdft"):
                        n = 10 * (i // 5) + 5 * (kind == "zdft") + i % 5
                        if i % 5 < 4:
                            q, m = divmod(i % 5, 2)
                            dve.wait_ge(*filled(l, kind, i))
                            ps = slot(l, kind, i)
                            dve.wait_ge(*after("odd_ready", l, n + 1))
                            dst = HS if kind == "fdft" else PM
                            TT(dst[:, 0, q, 512 * m:512 * m + 512], ps[:, 0:HY], oddb[:, n % 2], ALU.add)
                            TT(dst[:, 1, q, 512 * m:512 * m + 512], ps[:, 0:HY], oddb[:, n % 2], ALU.subtract)\
                                .then_inc(sems["spec_ready"], 1)
                            dve.wait_ge(*own("spec_ready"))
                        elif kind == "zdft":
                            dve.wait_ge(*after("spec_ready", l, n + 1))
                            for s in range(2):
                                product(dve, link, TT, ALU, PM[:, s], HS[:, s], tB, tC)
                            link(TT(PM[:, 1], PM[:, 0], PM[:, 1], ALU.subtract))
                            link(STT(PM[:, 0], PM[:, 0], 2.0, PM[:, 1], ALU.mult, ALU.subtract))
                            product(dve, link, TT, ALU, PMc, HSc, tB[:, 0:HY], tC[:, 0:HY])
                            dve.nop().then_inc(sems["y_ready"], 1)
                    elif kind == "inv":
                        o, c = divmod(i, CT)
                        dve.wait_ge(*filled(l, kind, i))
                        ps = slot(l, kind, i)
                        dve.wait_ge(*after("conv_ready", l, 8 + 4 * o))
                        sk = skip[:, o, c:c + 1]
                        t_lat, t_ctx = tconv[:, 0:LAT], tconv[:, ZP:ZP + CTX]
                        pairs = lambda ap: ap.rearrange("p (u a) -> p u a", a=2)
                        STT(pairs(t_lat), pairs(V4[:, c, 0:LAT]), sk,
                            ps[:, 0:LAT].rearrange("p (a u) -> p u a", a=2), ALU.mult, ALU.add)
                        link(STT(t_ctx, V4[:, c, ZP:ZP + CTX], sk, ps[:, 512:640], ALU.mult, ALU.add))
                        TT(V4[:, c, 0:LAT], t_lat, G4[:, c, 0:LAT], ALU.mult)
                        TT(V4[:, c, ZP:ZP + CTX], t_ctx, G4[:, c, ZP:ZP + CTX], ALU.mult).then_inc(sems["z_ready"], 1)
                        dve.wait_ge(*own("z_ready"))
                        if o == 1:
                            t_ = th[:, c % 2]
                            dve.wait_ge(*after("px_ready", l, c + 1))
                            if c >= 2:
                                dve.wait_ge(*after("gate_used", l, c - 1))
                            link(STT(t_, path_th[:, c], 1.0, path_x[:, c], ALU.add, ALU.mult))
                            STT(t_[:, 0:LAT], t_[:, 0:LAT], 0.5, V4[:, c, 0:LAT], ALU.mult, ALU.mult)
                            STT(t_[:, LAT:NTOK], t_[:, LAT:NTOK], 0.5, V4[:, c, ZP:ZP + CTX],
                                ALU.mult, ALU.mult).then_inc(sems["br_f32"], 1)
                            dve.wait_ge(*own("br_f32"))
                            dve.tensor_copy(BRh[:, c, :], t_).then_inc(sems["br_hi"], 1)
                            dve.wait_ge(*own("br_hi"))
                    elif kind == "path" and i >= CT:
                        n_, c = divmod(i, CT)
                        dve.wait_ge(*filled(l, kind, i))
                        ps = slot(l, kind, i)
                        dve.wait_ge(*after("th_ready", l, 12 * n_ + c + 1))
                        if n_ == 2 and c == 0:
                            dve.wait_ge(*after("ml_o", l, MH))
                        t_ = th[:, c % 2]
                        link(STT(halves(t_), halves(t_), 1.0, two(ps), ALU.add, ALU.mult))
                        y = OT[:, c] if n_ == 1 else Y[:, c]
                        STT(t_, t_, 0.5, y, ALU.mult, ALU.mult).then_inc(sems["br_f32"], 1)
                        dve.wait_ge(*own("br_f32"))
                        if c == 0:
                            dve.wait_ge(*filled(l, "mbranch", KD * n_ - 1))
                        dve.tensor_copy(BRh[:, c, :], t_).then_inc(sems["br_hi"], 1)
                        dve.wait_ge(*own("br_hi"))
                    elif kind == "mbranch":
                        n_, d = divmod(i, KD)
                        g = 12 * n_ + 4 + d
                        dve.wait_ge(*filled(l, kind, i))
                        ps = slot(l, kind, i)
                        dve.wait_ge(*after("th_ready", l, g + 1))
                        t_ = th[:, g % 2]
                        m = MG[:, NTOK * d:NTOK * d + NTOK]
                        if n_ == 0:
                            STT(halves(m), halves(t_), 1.0, two(ps), ALU.add, ALU.mult)\
                                .then_inc(sems["gate_used"], 1)
                        else:
                            link(STT(halves(t_), halves(t_), 1.0, two(ps), ALU.add, ALU.mult))
                            TT(m, m, t_, ALU.add).then_inc(sems["gate_used"], 1)
                        dve.wait_ge(*after("gate_used", l, g + 1))
                        if n_ == 2:
                            dve.tensor_copy(MGh[:, d, :], m).then_inc(sems["mg_hi"], 1)
                            dve.wait_ge(*own("mg_hi"))
                        t = i - 2 * KD - 3
                        if l and 0 <= t < NT:
                            x = X[:, t, :]
                            if t == 0:
                                dve.wait_ge(x_here, 32 * (l + 2))
                                dve.wait_ge(ln_here, 32 * l)
                            link(TT(x, x, lng, ALU.mult))
                            TT(x, x, lnb, ALU.add).then_inc(sems["ln_scaled"], 1)
                            dve.wait_ge(*own("ln_scaled"))
                    elif kind == "qk":
                        dve.wait_ge(*after("raw_ready", l, i + 1))
                        r = raw[:, i % 2, 0:LAT]
                        if i == 0:
                            dve.wait_ge(da_rope_here, 16 * (l + 1))
                        dst = qT[:, i, :] if i < 4 else kT[:, i - 4, PAST:NKEY]
                        mask = [(p + 16) % 32 for p in range(32)]
                        dve.stream_shuffle(swp, r, mask=mask).then_inc(dve_chain, 1)
                        chain["dve"] += 1
                        link(TT(dst[:, 0:LAT], r, rope_da[:, 0], ALU.mult))
                        link(TT(swp, swp, rope_da[:, 1], ALU.mult))
                        TT(dst[:, 0:LAT], dst[:, 0:LAT], swp, ALU.add)
                        dve.tensor_copy(dst[:, LAT:NTOK], raw[:, i % 2, LAT:NTOK]).then_inc(sems["qk_ready"], 1)
                        dve.wait_ge(*own("qk_ready"))
                    elif kind == "vt":
                        dve.wait_ge(*filled(l, kind, i))
                        ps = slot(l, kind, i)
                        dve.tensor_copy(V[:, 1:6, 128 * i:128 * i + 128],
                                            ps[:, 0:640].rearrange("p (a b) -> p a b", a=NT))\
                                                .then_inc(sems["v_ready"], 1)
                        dve.wait_ge(*own("v_ready"))
                    elif kind == "da_score":
                        if i == 0:
                            dve.wait_ge(*after("lam_exp", l, 1))
                            link(TT(lamc[:, 2:3], lamc[:, 4:5], lamc[:, 5:6], ALU.subtract))
                            link(TS(lamc[:, 6:7], lamc[:, 2:3], lamc[:, 0:1], -1.0, ALU.add, ALU.mult))
                            link(TT(lamc[:, 7:8], subln[:], lamc[:, 1:2], ALU.mult))
                        n = keysn(i)
                        for j in range(2):
                            dve.wait_ge(*filled(l, kind, i, j))
                            ps = slot(l, kind, i, j)
                            softmax_max(ps, n, st[:, i % (LAG + 1), j:j + 1]).then_inc(sems["da_max"], 1)
                            dve.wait_ge(*own("da_max"))
                        if i:
                            da_weights(l, i - 1)
                    elif kind == "da_ptrans" and i == DAH * NT - 1:
                        da_weights(l, i)
                    elif kind == "dasq":
                        dve.wait_ge(*after("da_o", l, i + 1))
                        TT(sqd[:, i % 2], OT[:, i], OT[:, i], ALU.mult).then_inc(sems["da_sq"], 1)
                        dve.wait_ge(*own("da_sq"))
                    elif kind == "dams":
                        dve.wait_ge(*filled(l, kind, i))
                        rows = slice(32 * i, 32 * i + 32)
                        TS(halves(msd[rows]), slot(l, kind, i)[rows].rearrange("p (a b) -> p a b", a=2)[:, :, 0:HALF],
                           1.0 / DAV, RMS_EPS, ALU.mult, ALU.add).then_inc(sems["da_ms"], 1)
                        dve.wait_ge(*own("da_ms"))
                    elif kind == "dart":
                        dve.wait_ge(*after("da_rt", l, 1))
                        dve.reciprocal(msd, msd).then_inc(sems["da_rc"], 1)
                        dve.wait_ge(*own("da_rc"))
                    elif kind == "dab":
                        dve.wait_ge(*filled(l, kind, i))
                        out = halves(OT[:, i])
                        STT(out, out, lamc[:, 7:8], two(slot(l, kind, i)), ALU.mult, ALU.mult)\
                            .then_inc(sems["da_n"], 1)
                        dve.wait_ge(*own("da_n"))
                    elif kind == "dqkv":
                        dve.wait_ge(*after("c_raw", l, i + 1))
                        c = cq[:, i] if i < 3 else ckv[:, i - 3, PAST:NKEY]
                        if i == 3:
                            dve.wait_ge(*filled(l, "mms", 0))
                        TT(sqm[:, i % 3], c, c, ALU.mult).then_inc(sems["c_sq"], 1)
                        dve.wait_ge(*own("c_sq"))
                    elif kind == "kr":
                        dve.wait_ge(*after("kr_raw", l, 1))
                        sw, r = swm[0:MR], krs[:, 0:LAT]
                        dve.stream_shuffle(sw, r, mask=[p ^ 8 for p in range(32)]).then_inc(dve_chain, 1)
                        chain["dve"] += 1
                        link(TT(krt, r, rope_m[0:MR, 0], ALU.mult))
                        link(TT(sw, sw, rope_m[0:MR, 1], ALU.mult))
                        for b in range(2):
                            TT(mkT[64:96, b, PAST:LKEY], krt, sw, ALU.add)
                            last = dve.tensor_copy(mkT[64:96, b, LKEY:NKEY], krs[:, LAT:NTOK])
                        last.then_inc(sems["kr_ready"], 1)
                        dve.wait_ge(*own("kr_ready"))
                    elif kind == "mms":
                        dve.wait_ge(*filled(l, kind, i))
                        rows = slice(32 * i, 32 * i + 32)
                        TS(halves(msm[rows]), slot(l, kind, i)[rows].rearrange("p (a b) -> p a b", a=2)[:, :, 0:HALF],
                           1.0 / (KVL if i else QL), RMS_EPS, ALU.mult, ALU.add).then_inc(sems["m_ms"], 1)
                        dve.wait_ge(*own("m_ms"))
                    elif kind == "mrt":
                        dve.wait_ge(*after("m_rt", l, 1))
                        dve.reciprocal(msm[0:64], msm[0:64]).then_inc(sems["m_rc"], 1)
                        dve.wait_ge(*own("m_rc"))
                    elif kind == "mb":
                        dve.wait_ge(*filled(l, kind, i))
                        for k in range(2 if i else 3):
                            c, gain = (ckv[:, k, PAST:NKEY], kvn) if i else (cq[:, k], qn)
                            last = STT(halves(c), halves(c), gain[:, k:k + 1], two(slot(l, kind, i)),
                                       ALU.mult, ALU.mult)
                        last.then_inc(sems["c_ready"], 1)
                        dve.wait_ge(*own("c_ready"))
                    elif kind == "mq":
                        dve.wait_ge(*after("mq_raw", l, i + 1))
                        sw, q = swm[64:96], mqT[64:96, i % 2, 0:LAT]
                        dve.stream_shuffle(sw, q, mask=[p ^ 8 for p in range(32)]).then_inc(dve_chain, 1)
                        chain["dve"] += 1
                        dve.wait_ge(dve_chain, chain["dve"])
                        TT(q, q, rope_m[64:96, 0], ALU.mult)
                        link(TT(sw, sw, rope_m[64:96, 1], ALU.mult))
                        TT(q, q, sw, ALU.add).then_inc(sems["mq_ready"], 1)
                        dve.wait_ge(*own("mq_ready"))
                    elif kind == "ml_score":
                        dve.wait_ge(*filled(l, kind, i))
                        softmax_max(slot(l, kind, i), keysn(i), st[:, i % (LAG + 1), 0:1]).then_inc(sems["ml_max"], 1)
                        dve.wait_ge(*own("ml_max"))
                        if i:
                            ml_weights(l, i - 1)
                    elif kind == "ml_ptrans" and i == MH * NT - 1:
                        ml_weights(l, i)
                    elif kind == "xt":
                        dve.wait_ge(*filled(l, kind, i))
                        ps = slot(l, kind, i)
                        x = X[:, :, 128 * i:128 * i + 128]
                        if i == 0:
                            dve.wait_ge(x_here, 32 * (l + 2))
                        STT(x, x, ALPHA, ps[:, 0:640].rearrange("p (a b) -> p a b", a=NT), ALU.mult, ALU.add)\
                            .then_inc(sems["x_part"], 1)
                        dve.wait_ge(*own("x_part"))
                        if i % 4 == 3:
                            b = i // 4
                            for t in range(NT):
                                last = dve.bn_stats(lnst[:, t, b, :], X[:, t, 512 * b:512 * b + 512])
                            link(last)
                    elif kind == "ln":
                        for t in range(NT):
                            last = dve.bn_aggr(lnmv[:, t, :], lnst[:, t, :, :].rearrange("p a b -> p (a b)"))
                        link(last)
                        TS(lnr[:], lnmv[:, :, 1], LN_EPS, None, ALU.add).then_inc(sems["ln_var"], 1)
                        dve.wait_ge(*own("ln_var"))
                        dve.wait_ge(*after("ln_rt", l, 1))
                        link(dve.reciprocal(lnr[:], lnr[:]))
                        if l == DEPTH - 1:
                            dve.wait_ge(ln_here, 32 * DEPTH)
                        for t in range(NT):
                            x = X[:, t, :]
                            scaled = TS(x, x, lnmv[:, t, 0:1], lnr[:, t:t + 1], ALU.subtract, ALU.mult)
                            if l == DEPTH - 1:
                                link(scaled)
                                link(TT(x, x, lng, ALU.mult))
                                TT(x, x, lnb, ALU.add).then_inc(sems["x_ready"], 1)
                            else:
                                scaled.then_inc(sems["x_ready"], 1)
                            dve.wait_ge(*own("x_ready"))

        @block.gpsimd
        def _(pool):
            def minus(out, in_, high):
                return pool.tensor_tensor(out, in_, high.bitcast(f32), ALU.subtract)

            def low_part(l, n):
                g = TILE_AT[(l, *SPLIT[n])]
                pool.wait_ge(*after("w_hi", l, n + 1))
                if l or n >= 2:
                    pool.wait_ge(*tile_done(l, n - 2))
                k = CT if SPLIT[n][0] == "mbranch" else KD
                minus(Wl[:, n % 2, 0:k, :], W[:, g % NW, 0:k, :], Wh[:, n % 2, 0:k, :])\
                    .then_inc(sems["w_lo"], 1)

            for l in range(DEPTH):
                split = 0
                for place, (kind, i) in enumerate(STEPS[l]):
                    while split < UPTO.get((l, place), 0):
                        low_part(l, split)
                        split += 1
                    if kind == "ht" and i % 2 == 0:
                        pool.wait_ge(*after("h_hi", l, i + 1))
                        minus(Hl[:, i, :], th[:, 0], Hh[:, i, :]).then_inc(sems["h_even"], 1)
                    elif (kind == "path" and i >= CT) or (kind == "inv" and i >= 4):
                        n_ = i if kind == "path" else i - 4
                        c = i % CT
                        pool.wait_ge(*after("br_hi", l, n_ + 1))
                        minus(BRl[:, c, :], th[:, c % 2], BRh[:, c, :]).then_inc(sems["gate_used"], 1)
                    elif kind == "mbranch" and i >= 2 * KD:
                        d = i - 2 * KD
                        m = MG[:, NTOK * d:NTOK * d + NTOK]
                        pool.wait_ge(*after("mg_hi", l, d + 1))
                        minus(MGl[:, d, :], m, MGh[:, d, :]).then_inc(sems["mg_ready"], 1)
    return nc


def keysn(u):
    return LKEY if u % NT < 4 else CTX


def two_or_one(e, n):
    return e.rearrange("p (a b) -> p a b", a=2) if n > CTX else e


def product(dve, link, TT, ALU, z, h, tb, tc):
    TT(tb, z[:, 0], h[:, 1], ALU.mult)
    link(TT(tc, z[:, 1], h[:, 1], ALU.mult))
    link(TT(z[:, 0], z[:, 0], h[:, 0], ALU.mult))
    TT(z[:, 0], z[:, 0], tc, ALU.subtract)
    link(TT(z[:, 1], z[:, 1], h[:, 0], ALU.mult))
    link(TT(z[:, 1], z[:, 1], tb, ALU.add))


def tiles(w, m=128):
    l, r, c = w.shape
    return w.reshape(l, r // 128, 128, c // m, m).transpose(0, 3, 2, 1, 4)


def columns(v):
    return v.reshape(DEPTH, -1, 128).transpose(0, 2, 1)


def before(v):
    return columns(np.roll(v, 1, 0))


def laid_out(x):
    w_in = x["w_in"]
    ffn = np.stack([x["hy_ffn_b1"], x["hy_ffn_b2"], x["hy_sin_freq"][:, 0], x["hy_sin_freq"][:, 1]], -1)
    ffn = np.concatenate([ffn, np.zeros((DEPTH, 128 - HY_FFN, 4), ffn.dtype)], 1)
    return {
        "cvec": np.stack([x["c"][0], x["c_ctx"]], -1).reshape(KD, 128, 2).transpose(1, 0, 2),
        "w_mod": tiles(x["w_mod"]),
        "mla_w_ukv": x["mla_w_ukv"].reshape(DEPTH, KVL, MH, 2, MN).transpose(0, 1, 3, 2, 4).reshape(DEPTH, KVL, -1),
        "b_mod": columns(x["b_mod"]).transpose(1, 0, 2),
        "w_in": tiles(np.concatenate([w_in[:, :, :C_KR + 128], w_in[:, :, C_PATH:]], -1)),
        "w_branch": np.stack([tiles(x["w_branch"][:, n]) for n in range(3)], 1).reshape(DEPTH, 3 * KD, 128, CT, 128),
        "w_out": tiles(x["w_out"]),
        "vecs": np.concatenate([before(x["ln_g"]), before(x["ln_b"]),
                                columns(x["hy_conv_w"]), columns(x["hy_conv_b"]),
                                columns(x["hy_skip"]), ffn, columns(x["da_subln"]), columns(x["mla_q_norm"]),
                                columns(x["mla_kv_norm"])], -1),
    }

INPUTS = ["x_prompt", "x_sample", "cache_diff_k", "cache_diff_v", "cache_mla_ckv", "cache_mla_krope", "hy_ffn_w1",
          "hy_ffn_w2", "hy_ffn_w3", "hy_log_decay", "da_lambda", "mla_w_uq", "ln_g", "ln_b"]
OUTPUTS = [(1, CTX, D), (1, LAT, D), (1, DEPTH, CTX, 2, DAH, DHD), (1, DEPTH, CTX, DAH, DAV), (1, DEPTH, CTX, KVL),
           (1, DEPTH, CTX, MR)]


def kernel(**inputs):
    import concourse.bacc as bacc
    from concourse.bass_utils import run_bass_kernel_spmd as run

    nc = bacc.Bacc("TRN2", target_bir_lowering=False, num_devices=1)
    f32 = mybir.dt.float32
    arrays, A = {}, {}
    for name, a in [(n, inputs[n]) for n in INPUTS] + list(laid_out(inputs).items()) + list(constants().items()):
        a = np.ascontiguousarray(a)
        arrays[f"in_{name}"] = a
        A[name] = nc.dram_tensor(f"in_{name}", a.shape, mybir.dt.from_np(a.dtype), kind="ExternalInput").ap()
    outs = [nc.dram_tensor(f"out_{i}", s, f32, kind="ExternalOutput").ap() for i, s in enumerate(OUTPUTS)]
    build(nc, A, outs)
    r = run(nc, [arrays], core_ids=[0])
    return tuple(r.results[0][f"out_{i}"] for i in range(len(OUTPUTS)))
```
